# Optimizing a Trainium2 kernel written in Bass

```python
import math
import jax
import jax.numpy as jnp
from jax import lax
import numpy as np

D_MODEL = 1024
BATCH = 1
SEQ = 256
DEPTH = 4

GRID_W = 64
CTX_LEN = 256
N_MIXERS = 3
N_RWKV = (DEPTH + 2) // 3
N_SSD = (DEPTH + 1) // 3
N_ATTN = DEPTH // 3
NORM_EPS = 1e-6

RW_HEAD = 64
RW_HEADS = D_MODEL // RW_HEAD
RW_DECAY_LORA = 64
RW_A_LORA = 64
RW_GATE_LORA = 128
RW_GN_EPS = 64e-5

SSD_INNER = 2 * D_MODEL
SSD_HEAD = 64
SSD_HEADS = SSD_INNER // SSD_HEAD
SSD_GROUPS = 8
SSD_STATE = 128
SSD_CONV = 3
SSD_CHUNK = 64
SSD_CONV_DIM = SSD_INNER + 2 * SSD_GROUPS * SSD_STATE
SSD_IN_DIM = SSD_INNER + SSD_CONV_DIM + 2 * SSD_HEADS

AT_HEADS = 16
AT_KV_HEADS = 4
AT_HEAD = 64
AT_WINDOW = 128
AT_BLOCK = 128
ROPE_BASE = 10000.0

FFN_DIM = 2816
FFN_CONV = 3

kernel_name = 'hybrid_rwkv_ssd_swa_flow_backbone'

def _ident(t):
    return t

def _flip(t):
    return jnp.flip(t, axis=1)

def rmsnorm(x, g, eps=NORM_EPS):
    xf = x.astype(jnp.float32)
    xf = xf * lax.rsqrt(jnp.mean(xf * xf, axis=-1, keepdims=True) + eps)
    return (xf * g.astype(jnp.float32)).astype(x.dtype)

def modulate(x, g, shift, scale):
    return rmsnorm(x, g) * (1 + scale) + shift

def dwconv_centred(x, w):
    K = w.shape[0]
    half = K // 2
    T = x.shape[1]
    xp = jnp.pad(x, ((0, 0), (half, half), (0, 0)))
    out = xp[:, 0:T] * w[0]
    for k in range(1, K):
        out = out + xp[:, k:k + T] * w[k]
    return out

def token_shift_centred(x):
    xp = jnp.pad(x, ((0, 0), (1, 1), (0, 0)))
    return 0.5 * (xp[:, :-2] + xp[:, 2:])

def _rotate(x, pos):
    d = x.shape[-1]
    inv = ROPE_BASE ** (-jnp.arange(0, d, 2, dtype=jnp.float32) / d)
    ang = pos.astype(jnp.float32)[:, None] * inv[None, :]
    cos = jnp.cos(ang)[None, :, None, :].astype(x.dtype)
    sin = jnp.sin(ang)[None, :, None, :].astype(x.dtype)
    x1, x2 = jnp.split(x, 2, axis=-1)
    return jnp.concatenate([x1 * cos - x2 * sin, x1 * sin + x2 * cos], axis=-1)

def rope_2d(x, row, col):
    xr, xc = jnp.split(x, 2, axis=-1)
    return jnp.concatenate([_rotate(xr, row), _rotate(xc, col)], axis=-1)

def rwkv7_scan(r, w, k, v, kk, a, s0):
    def step(s, inp):
        r_t, w_t, k_t, v_t, kk_t, a_t = inp
        s_kk = jnp.einsum('bhvk,bhk->bhv', s, kk_t)
        s = (s * w_t[:, :, None, :] - s_kk[..., None] * (kk_t * a_t)[:, :, None, :]
             + v_t[..., None] * k_t[:, :, None, :])
        return s, jnp.einsum('bhvk,bhk->bhv', s, r_t)
    xs = tuple(jnp.moveaxis(t, 1, 0) for t in (r, w, k, v, kk, a))
    s_fin, ys = lax.scan(step, s0, xs)
    return jnp.moveaxis(ys, 0, 1), s_fin

def rwkv7_stream(h, mu, wr, wk, wv, w0, w1, w2, a0, a1, a2, k_k, k_a):
    b, T, _ = h.shape
    heads = lambda t: t.reshape(b, T, RW_HEADS, RW_HEAD)
    dx = token_shift_centred(h) - h
    xr, xw, xk, xv, xa, xg = (h + dx * mu[i] for i in range(6))
    r = heads(xr @ wr)
    k = xk @ wk
    v = heads(xv @ wv)
    kkf = heads(k * k_k).astype(jnp.float32)
    kk = (kkf * lax.rsqrt(jnp.sum(kkf * kkf, axis=-1, keepdims=True) + 1e-12)).astype(h.dtype)
    dirs = []
    for d in range(2):
        w_log = -jax.nn.softplus(-(w0[d] + jnp.tanh(xw @ w1[d]) @ w2[d])) - 0.5
        decay = jnp.exp(-jnp.exp(w_log))
        a = jax.nn.sigmoid(a0[d] + (xa @ a1[d]) @ a2[d])
        dirs.append((heads(decay), heads(a), heads(k * (1 + (a - 1) * k_a))))
    return r, v, kk, xg, dirs

def head_groupnorm(y, g, bias):
    yf = y.astype(jnp.float32)
    mu = jnp.mean(yf, axis=-1, keepdims=True)
    var = jnp.mean(jnp.square(yf - mu), axis=-1, keepdims=True)
    yn = ((yf - mu) * lax.rsqrt(var + RW_GN_EPS)).astype(y.dtype)
    b, T = y.shape[:2]
    return yn.reshape(b, T, -1) * g + bias

def rwkv7_mixer(hc, hl, ctx_out, mu, wr, wk, wv, wo, w0, w1, w2, a0, a1, a2, g1, g2, k_k, k_a, r_k, ln_g, ln_b):
    proj = (mu, wr, wk, wv, w0, w1, w2, a0, a1, a2, k_k, k_a)
    sc = rwkv7_stream(hc, *proj)
    sl = rwkv7_stream(hl, *proj)
    b = hl.shape[0]
    s0 = jnp.zeros((b, RW_HEADS, RW_HEAD, RW_HEAD), hl.dtype)
    rc, vc, kkc, _, dc = sc
    rl, vl, kkl, _, dl = sl
    ys_c, ys_l = [], []
    for d, f in enumerate((_ident, _flip)):
        wc, ac, kc = dc[d]
        wl, al, kl = dl[d]
        yc_d, s_ctx = rwkv7_scan(f(rc), f(wc), f(kc), f(vc), f(kkc), f(ac), s0)
        yl_d, _ = rwkv7_scan(f(rl), f(wl), f(kl), f(vl), f(kkl), f(al), s_ctx)
        ys_c.append(f(yc_d))
        ys_l.append(f(yl_d))

    def finish(s, ys):
        r, v, _, xg, dirs = s
        bb, T = r.shape[:2]
        bonus = sum(jnp.sum(r * kd * r_k, axis=-1, keepdims=True) for _, _, kd in dirs) * v
        y = head_groupnorm(ys[0] + ys[1], ln_g, ln_b) + bonus.reshape(bb, T, -1)
        g = jax.nn.sigmoid(xg @ g1) @ g2
        return (y * g) @ wo

    yl = finish(sl, ys_l)
    yc = finish(sc, ys_c) if ctx_out else None
    return yc, yl

def ssd_scan(x, dt, A, B, C, h0):
    b, T, H, P = x.shape
    G, N = B.shape[2], B.shape[3]
    E = H // G
    Q = SSD_CHUNK
    nc = T // Q
    xdt = (x * dt[..., None]).reshape(b, nc, Q, G, E, P)
    Bq = B.reshape(b, nc, Q, G, N)
    Cq = C.reshape(b, nc, Q, G, N)
    a_cs = jnp.cumsum((dt * A).reshape(b, nc, Q, G, E), axis=2)
    a_t = jnp.moveaxis(a_cs, 2, -1)
    seg = a_t[..., :, None] - a_t[..., None, :]
    lower = jnp.tril(jnp.ones((Q, Q), dtype=bool))
    decay = jnp.exp(jnp.where(lower, seg, -jnp.inf))
    cb = jnp.einsum('bcign,bcjgn->bcgij', Cq, Bq)
    y_diag = jnp.einsum('bcgeij,bcjgep->bcigep', cb[:, :, :, None] * decay, xdt)
    from_start = jnp.exp(a_cs)
    to_end = jnp.exp(a_cs[:, :, -1:] - a_cs)
    chunk_decay = jnp.exp(a_cs[:, :, -1])

    def step(h, inp):
        c_q, b_q, x_q, fs, te, cd = inp
        y_off = jnp.einsum('bign,bgepn,bige->bigep', c_q, h, fs)
        h = cd[..., None, None] * h + jnp.einsum('bjgn,bjge,bjgep->bgepn', b_q, te, x_q)
        return h, y_off

    xs = tuple(jnp.moveaxis(t, 1, 0) for t in (Cq, Bq, xdt, from_start, to_end, chunk_decay))
    h_fin, y_off = lax.scan(step, h0.reshape(b, G, E, P, N), xs)
    y = y_diag + jnp.moveaxis(y_off, 0, 1)
    return y.reshape(b, T, H, P), h_fin.reshape(b, H, P, N)

def ssd_project(h, w_in, conv_w, conv_b):
    b, T, _ = h.shape
    z, xbc, dt = jnp.split(h @ w_in, [SSD_INNER, SSD_INNER + SSD_CONV_DIM], axis=-1)
    xbc = jax.nn.silu(dwconv_centred(xbc, conv_w) + conv_b)
    xs, B, C = jnp.split(xbc, [SSD_INNER, SSD_INNER + SSD_GROUPS * SSD_STATE], axis=-1)
    return (z, xs.reshape(b, T, SSD_HEADS, SSD_HEAD), B.reshape(b, T, SSD_GROUPS, SSD_STATE),
            C.reshape(b, T, SSD_GROUPS, SSD_STATE), dt)

def group_rmsnorm(y, g, groups):
    b, T, C = y.shape
    yf = y.astype(jnp.float32).reshape(b, T, groups, C // groups)
    yf = yf * lax.rsqrt(jnp.mean(yf * yf, axis=-1, keepdims=True) + NORM_EPS)
    return (yf.reshape(b, T, C) * g.astype(jnp.float32)).astype(y.dtype)

def ssd_mixer(hc, hl, ctx_out, w_in, conv_w, conv_b, dt_bias, a_log, d_skip, norm_g, w_out):
    pc = ssd_project(hc, w_in, conv_w, conv_b)
    pl = ssd_project(hl, w_in, conv_w, conv_b)
    b = hl.shape[0]
    h0 = jnp.zeros((b, SSD_HEADS, SSD_HEAD, SSD_STATE), hl.dtype)
    ys_c, ys_l = [], []
    for d, f in enumerate((_ident, _flip)):
        A = -jnp.exp(a_log[d])
        dtc = jax.nn.softplus(pc[4][..., d * SSD_HEADS:(d + 1) * SSD_HEADS] + dt_bias[d])
        dtl = jax.nn.softplus(pl[4][..., d * SSD_HEADS:(d + 1) * SSD_HEADS] + dt_bias[d])
        yc_d, h_ctx = ssd_scan(f(pc[1]), f(dtc), A, f(pc[2]), f(pc[3]), h0)
        yl_d, _ = ssd_scan(f(pl[1]), f(dtl), A, f(pl[2]), f(pl[3]), h_ctx)
        ys_c.append(f(yc_d))
        ys_l.append(f(yl_d))

    def finish(ys, z, xs):
        y = ys[0] + ys[1] + xs * d_skip[:, None]
        bb, T = y.shape[:2]
        y = y.reshape(bb, T, SSD_INNER) * jax.nn.silu(z)
        return group_rmsnorm(y, norm_g, SSD_GROUPS) @ w_out

    yl = finish(ys_l, pl[0], pl[1])
    yc = finish(ys_c, pc[0], pc[1]) if ctx_out else None
    return yc, yl

def sink_softmax(scores, sink_g):
    b, kh, g, q, _ = scores[0].shape
    sink_col = jnp.broadcast_to(sink_g.astype(scores[0].dtype)[None, :, :, None, None], (b, kh, g, q, 1))
    logits = jnp.concatenate(list(scores) + [sink_col], axis=-1).astype(jnp.float32)
    p = jax.nn.softmax(logits, axis=-1).astype(scores[0].dtype)[..., :-1]
    cuts, acc = [], 0
    for s in scores[:-1]:
        acc += s.shape[-1]
        cuts.append(acc)
    return jnp.split(p, cuts, axis=-1)

def window_attn_mixer(hc, hl, ctx_out, row, col, w_qkv, w_o, sink):
    b, T, _ = hl.shape
    grp = AT_HEADS // AT_KV_HEADS
    scale = AT_HEAD ** -0.5

    def qkv(h):
        n = h.shape[1]
        q, k, v = jnp.split(h @ w_qkv, [AT_HEADS * AT_HEAD, (AT_HEADS + AT_KV_HEADS) * AT_HEAD], axis=-1)
        return (q.reshape(b, n, AT_HEADS, AT_HEAD), k.reshape(b, n, AT_KV_HEADS, AT_HEAD),
                v.reshape(b, n, AT_KV_HEADS, AT_HEAD))

    qc, kc, vc = qkv(hc)
    ql, kl, vl = qkv(hl)
    ql = rope_2d(ql, row, col).reshape(b, T, AT_KV_HEADS, grp, AT_HEAD)
    kl = rope_2d(kl, row, col)
    sink_g = sink.reshape(AT_KV_HEADS, grp)
    pad = ((0, 0), (AT_WINDOW, AT_WINDOW), (0, 0), (0, 0))
    kl_p = jnp.pad(kl, pad)
    vl_p = jnp.pad(vl, pad)
    span = AT_BLOCK + 2 * AT_WINDOW
    q_off = jnp.arange(AT_BLOCK)
    k_off = jnp.arange(span) - AT_WINDOW

    def block(i):
        start = i * AT_BLOCK
        q = lax.dynamic_slice_in_dim(ql, start, AT_BLOCK, axis=1)
        k = lax.dynamic_slice_in_dim(kl_p, start, span, axis=1)
        v = lax.dynamic_slice_in_dim(vl_p, start, span, axis=1)
        qpos = start + q_off
        kpos = start + k_off
        allowed = ((jnp.abs(qpos[:, None] - kpos[None, :]) <= AT_WINDOW)
                   & (kpos[None, :] >= 0) & (kpos[None, :] < T))
        s_loc = jnp.where(allowed, jnp.einsum('bqkgd,bskd->bkgqs', q, k) * scale, -jnp.inf)
        s_ctx = jnp.einsum('bqkgd,bskd->bkgqs', q, kc) * scale
        p_loc, p_ctx = sink_softmax([s_loc, s_ctx], sink_g)
        o = jnp.einsum('bkgqs,bskd->bqkgd', p_loc, v) + jnp.einsum('bkgqs,bskd->bqkgd', p_ctx, vc)
        return o.reshape(b, AT_BLOCK, AT_HEADS * AT_HEAD)

    o_l = lax.map(block, jnp.arange(T // AT_BLOCK))
    yl = jnp.moveaxis(o_l, 0, 1).reshape(b, T, AT_HEADS * AT_HEAD) @ w_o
    yc = None
    if ctx_out:
        n = hc.shape[1]
        qg = qc.reshape(b, n, AT_KV_HEADS, grp, AT_HEAD)
        (p_c,) = sink_softmax([jnp.einsum('bqkgd,bskd->bkgqs', qg, kc) * scale], sink_g)
        yc = jnp.einsum('bkgqs,bskd->bqkgd', p_c, vc).reshape(b, n, AT_HEADS * AT_HEAD) @ w_o
    return yc, yl

def conv_ffn(h, w_in, conv_w, w_out):
    u = dwconv_centred(h @ w_in, conv_w)
    a, gate = jnp.split(u, 2, axis=-1)
    return (a * jax.nn.silu(gate)) @ w_out

def setup_inputs(seed: int = 0) -> dict:
    key = jax.random.key(seed)
    keys = iter(jax.random.split(key, 64))
    f32 = jnp.float32

    def nrm(shape, scale=1.0):
        return scale * jax.random.normal(next(keys), shape, f32)

    def uni(shape, lo, hi):
        return jax.random.uniform(next(keys), shape, f32, lo, hi)

    D = D_MODEL
    dt0 = jnp.exp(uni((N_SSD, 2, SSD_HEADS), math.log(1e-3), math.log(1e-1)))
    return {
        'x': nrm((BATCH, SEQ, D)),
        'c': nrm((BATCH, D)),
        'ctx': nrm((BATCH, CTX_LEN, D)),
        'c_ctx': nrm((D,)),
        'ada_w': nrm((DEPTH, D, 6 * D), 0.5 * D ** -0.5),
        'ada_b': nrm((DEPTH, 6 * D), 0.01),
        'norm1_g': 1.0 + nrm((DEPTH, D), 0.02),
        'norm2_g': 1.0 + nrm((DEPTH, D), 0.02),
        'ffn_w_in': nrm((DEPTH, D, 2 * FFN_DIM), D ** -0.5),
        'ffn_conv': nrm((DEPTH, FFN_CONV, 2 * FFN_DIM), FFN_CONV ** -0.5),
        'ffn_w_out': nrm((DEPTH, FFN_DIM, D), FFN_DIM ** -0.5),
        'final_g': 1.0 + nrm((D,), 0.02),
        'rw_mu': uni((N_RWKV, 6, D), 0.0, 1.0),
        'rw_wr': nrm((N_RWKV, D, D), D ** -0.5),
        'rw_wk': nrm((N_RWKV, D, D), D ** -0.5),
        'rw_wv': nrm((N_RWKV, D, D), D ** -0.5),
        'rw_wo': nrm((N_RWKV, D, D), D ** -0.5),
        'rw_w0': uni((N_RWKV, 2, D), -6.0, 0.0),
        'rw_w1': nrm((N_RWKV, 2, D, RW_DECAY_LORA), D ** -0.5),
        'rw_w2': nrm((N_RWKV, 2, RW_DECAY_LORA, D), 0.5 * RW_DECAY_LORA ** -0.5),
        'rw_a0': nrm((N_RWKV, 2, D), 0.3),
        'rw_a1': nrm((N_RWKV, 2, D, RW_A_LORA), D ** -0.5),
        'rw_a2': nrm((N_RWKV, 2, RW_A_LORA, D), 0.5 * RW_A_LORA ** -0.5),
        'rw_g1': nrm((N_RWKV, D, RW_GATE_LORA), D ** -0.5),
        'rw_g2': nrm((N_RWKV, RW_GATE_LORA, D), RW_GATE_LORA ** -0.5),
        'rw_kk': 0.85 + nrm((N_RWKV, D), 0.05),
        'rw_ka': 1.0 + nrm((N_RWKV, D), 0.05),
        'rw_rk': nrm((N_RWKV, RW_HEADS, RW_HEAD), 0.1),
        'rw_ln_g': 1.0 + nrm((N_RWKV, D), 0.02),
        'rw_ln_b': nrm((N_RWKV, D), 0.01),
        'ssd_w_in': nrm((N_SSD, D, SSD_IN_DIM), D ** -0.5),
        'ssd_conv_w': nrm((N_SSD, SSD_CONV, SSD_CONV_DIM), SSD_CONV ** -0.5),
        'ssd_conv_b': nrm((N_SSD, SSD_CONV_DIM), 0.01),
        'ssd_dt_bias': jnp.log(jnp.expm1(dt0)),
        'ssd_a_log': jnp.log(uni((N_SSD, 2, SSD_HEADS), 1.0, 16.0)),
        'ssd_d': 1.0 + nrm((N_SSD, SSD_HEADS), 0.02),
        'ssd_norm_g': 1.0 + nrm((N_SSD, SSD_INNER), 0.02),
        'ssd_w_out': nrm((N_SSD, SSD_INNER, D), SSD_INNER ** -0.5),
        'at_w_qkv': nrm((N_ATTN, D, (AT_HEADS + 2 * AT_KV_HEADS) * AT_HEAD), D ** -0.5),
        'at_w_o': nrm((N_ATTN, AT_HEADS * AT_HEAD, D), (AT_HEADS * AT_HEAD) ** -0.5),
        'at_sink': nrm((N_ATTN, AT_HEADS)),
    }

def reference(x, c, ctx, c_ctx, ada_w, ada_b, norm1_g, norm2_g, ffn_w_in, ffn_conv, ffn_w_out, final_g,
              rw_mu, rw_wr, rw_wk, rw_wv, rw_wo, rw_w0, rw_w1, rw_w2, rw_a0, rw_a1, rw_a2, rw_g1, rw_g2,
              rw_kk, rw_ka, rw_rk, rw_ln_g, rw_ln_b,
              ssd_w_in, ssd_conv_w, ssd_conv_b, ssd_dt_bias, ssd_a_log, ssd_d, ssd_norm_g, ssd_w_out,
              at_w_qkv, at_w_o, at_sink):
    T = x.shape[1]
    rows = T // GRID_W
    row = jnp.repeat(jnp.arange(rows), GRID_W, total_repeat_length=T)
    col = jnp.tile(jnp.arange(GRID_W), rows)
    silu_c = jax.nn.silu(c)
    silu_cc = jax.nn.silu(c_ctx)
    xl, xc = x, ctx
    for i in range(DEPTH):
        kind, j = i % N_MIXERS, i // N_MIXERS
        ctx_out = i < DEPTH - 1
        ml = jnp.split((silu_c @ ada_w[i] + ada_b[i])[:, None, :], 6, axis=-1)
        mc = jnp.split(silu_cc @ ada_w[i] + ada_b[i], 6, axis=-1)
        hl = modulate(xl, norm1_g[i], ml[0], ml[1])
        hc = modulate(xc, norm1_g[i], mc[0], mc[1])
        if kind == 0:
            yc, yl = rwkv7_mixer(hc, hl, ctx_out, rw_mu[j], rw_wr[j], rw_wk[j], rw_wv[j], rw_wo[j],
                                 rw_w0[j], rw_w1[j], rw_w2[j], rw_a0[j], rw_a1[j], rw_a2[j],
                                 rw_g1[j], rw_g2[j], rw_kk[j], rw_ka[j], rw_rk[j], rw_ln_g[j], rw_ln_b[j])
        elif kind == 1:
            yc, yl = ssd_mixer(hc, hl, ctx_out, ssd_w_in[j], ssd_conv_w[j], ssd_conv_b[j], ssd_dt_bias[j],
                               ssd_a_log[j], ssd_d[j], ssd_norm_g[j], ssd_w_out[j])
        else:
            yc, yl = window_attn_mixer(hc, hl, ctx_out, row, col, at_w_qkv[j], at_w_o[j], at_sink[j])
        xl = xl + ml[2] * yl
        xl = xl + ml[5] * conv_ffn(modulate(xl, norm2_g[i], ml[3], ml[4]), ffn_w_in[i], ffn_conv[i], ffn_w_out[i])
        if ctx_out:
            xc = xc + mc[2] * yc
            xc = xc + mc[5] * conv_ffn(modulate(xc, norm2_g[i], mc[3], mc[4]), ffn_w_in[i], ffn_conv[i], ffn_w_out[i])
    return rmsnorm(xl, final_g)


_drawn_inputs = setup_inputs


def setup_inputs(seed=0):
    import zlib

    import numpy as np

    out = dict(_drawn_inputs(seed))
    spreads = {}
    factors = {'norm1_g': 4.491,
     'norm2_g': 4.682,
     'final_g': 8.287,
     'rw_w1': 5.217,
     'rw_w2': 5.349,
     'rw_ln_g': 29.472,
     'rw_ln_b': 54.778,
     'ssd_conv_b': 32.693,
     'ssd_d': 64.0,
     'ssd_norm_g': 33.374,
     'at_sink': 8.0}
    for name, (base, spread) in spreads.items():
        noise = np.random.default_rng([zlib.crc32(name.encode()), seed]).standard_normal(out[name].shape)
        drawn = base * np.exp(spread * noise) if base else spread * noise
        out[name] = jnp.asarray(drawn.astype(out[name].dtype))
    for name, factor in factors.items():
        out[name] = (out[name] * factor).astype(out[name].dtype)
    return out
```

```python
from contextlib import ExitStack, contextmanager

import concourse.bass as bass
from concourse import mybir

P = 128
D = 1024
KD = D // P
CTX = 256
SEQ = 256
T = CTX + SEQ
SEG = 256
NCH = T // P
DEPTH = 4
F = 2816
NF = F // P
NMOD = 6 * D // P
EPS = 1e-6
GN_EPS = 64e-5
KK_EPS = 1e-12
LEAD = 256
LOG_W = 0.6065306597126334
MID = 38.8
HEADS = 16
SSD_IN = 6208
INNER = 2048
NEG = -1.0e30
ORDER = [[0, 1, 2, 3], [1, 0, 3, 2]]

F32 = mybir.dt.float32
ACT = mybir.ActivationFunctionType
ALU = mybir.AluOpType
AX_X = mybir.AxisListType.X

CONST = ["ident", "mean", "blk", "cent", "blkmean", "ones", "mask8", "lev8", "lev16", "lev32", "lev64",
         "gs0", "gi0", "gs1", "gi1", "gt0", "gt1", "mean256"]
ATTN_CONST = ["cos0", "cos1", "sin0", "sin1", "rot", "dup0", "dup1", "duprot0", "duprot1",
              "am00", "am01", "am10", "am11"]


class Counts:

    def __init__(self, draft=None):
        self.draft = draft
        self.now, self.marks, self.loops, self.ends, self.loop_name = {}, {}, {}, {}, None

    def mark(self, sem, label, n=1):
        name = getname(sem)
        self.now[name] = self.now.get(name, 0) + n
        assert label is None or label not in self.marks, label
        if label is not None:
            self.marks[label] = (name, self.now[name], self.loop_name)
        return n

    def at(self, label, i=None, back=0):
        if self.draft is None:
            return 1
        name, value, loop = self.draft.marks[label]
        if loop is None:
            return value
        step, trips = self.draft.loops[loop][name]
        if i is None:
            return value + (trips - 1) * step
        value -= back * step
        assert value >= 1, (label, value)
        return i * step + value

    def here(self, sem, i=None):
        name = getname(sem)
        value = self.now.get(name, 0)
        if self.draft is None:
            return 1
        if self.loop_name is None:
            return value
        step, _ = self.draft.loops[self.loop_name][name]
        return i * step + value

    def end(self, sem, stage):
        self.ends[(getname(sem), stage)] = self.now.get(getname(sem), 0)

    def ended(self, sem, stage):
        return 1 if self.draft is None else self.draft.ends.get((getname(sem), stage), 0)

    @contextmanager
    def loop(self, eng, name, trips):
        before = dict(self.now)
        self.loop_name = name
        with eng.Fori(0, trips) as i:
            yield i
        self.loop_name = None
        for sem, v in list(self.now.items()):
            step = v - before.get(sem, 0)
            if step:
                self.loops.setdefault(name, {})[sem] = (step, trips)
                self.now[sem] = before.get(sem, 0) + trips * step


def getname(sem):
    return sem if isinstance(sem, str) else sem.name


def program(nc, a, out, draft, scratch, layers=range(DEPTH), mixers=True, only=range(DEPTH)):
    C = Counts(draft)
    ctx = ExitStack()
    with ctx:
        def sb(name, *shape):
            return ctx.enter_context(nc.sbuf_tensor(name, [P, *shape], F32))

        def sem(name):
            return ctx.enter_context(nc.semaphore(name))

        PS = ctx.enter_context(nc.psum_tensor("PS", [P, 8, 512], F32))
        X = sb("X", KD, T)
        H = sb("H", KD * T)
        Hk = H[:, :].rearrange("p (k t) -> p k t", k=KD)
        WR = sb("WR", 2, 8, P)
        BIG = sb("BIG", 20480)
        WORK = sb("WORK", 14976)
        K = sb("K", len(CONST) * P)
        PV = sb("PV", 17, P)
        MOD = sb("MOD", DEPTH, NMOD, 2)
        MS = sb("MS", 2 * DEPTH + 1, KD, 2)
        MC = sb("MC", 5)
        SC = sb("SC", KD, 2)
        SEGS = (slice(0, SEG), slice(SEG, T))

        def const(name, n=1):
            c = CONST.index(name)
            return K[:, c * P:(c + n) * P]

        pe_done = sem("pe_done")
        w_used = sem("w_used")
        act_done = sem("act_done")
        vec_done = sem("vec_done")
        pool_done = sem("pool_done")
        w_loaded = [sem("w_loaded0"), sem("w_loaded1")]
        ada_loaded = [sem(f"ada_loaded{s}") for s in range(4)]
        in_loaded = sem("in_loaded")
        vec_loaded = sem("vec_loaded")
        side_loaded = [sem(f"side_loaded{s}") for s in range(4)]
        stored = sem("stored")
        scratch_stored = sem("scratch_stored")
        g2_loaded = sem("g2_loaded")
        loads_started = sem("loads_started")
        PROGRESS = (pe_done, w_used, act_done, vec_done, pool_done)

        pe, act, vec, pool, sp = nc.tensor, nc.scalar, nc.vector, nc.gpsimd, nc.sync

        def enter(eng, own, stage):
            for s in PROGRESS:
                if s not in own and C.ended(s, stage) > 0:
                    eng.wait_ge(s, C.ended(s, stage))

        def leave(own, stage):
            for s in own:
                C.end(s, stage)

        def v(ins, label=None, i=None):
            ins.then_inc(vec_done, C.mark(vec_done, label))
            vec.wait_ge(vec_done, C.here(vec_done, i))

        def s(ins, label=None, i=None):
            ins.then_inc(act_done, C.mark(act_done, label))
            act.wait_ge(act_done, C.here(act_done, i))

        def g(ins, label=None, i=None):
            ins.then_inc(pool_done, C.mark(pool_done, label))
            pool.wait_ge(pool_done, C.here(pool_done, i))

        def load_unit(i, label, *parts):
            slot = C.now.get("unit", 0) % 2
            sp.wait_ge(w_used, C.here("unit", i) + 1)
            sp.sem_inc(loads_started, 1)
            C.mark("unit", None)
            for n, (dst, src) in enumerate(parts):
                last = n == len(parts) - 1
                sp.dma_start(dst(WR[:, slot]), src).then_inc(
                    w_loaded[slot], C.mark(w_loaded[slot], label if last else None, 16))

        def rows(w):
            return w.rearrange("(k p) n -> p k n", p=P)

        def unit(w, k0, nk, c0, nc_=P):
            return (lambda slot: slot[:, 0:nk, 0:nc_], w[:, k0:k0 + nk, bass.ds(c0, nc_)])

        def use_unit(i, label, outs, rhs, nk, first, last, m=P):
            slot = C.now.get("w_unit_pe", 0) % 2
            C.mark("w_unit_pe", None)
            pe.wait_ge(w_loaded[slot], C.at(label, i))
            for k in range(nk):
                mm = pe.matmul(outs, WR[:, slot, k, 0:m], rhs(k), start=first and k == 0, stop=last and k == nk - 1)
            mm.then_inc(w_used, C.mark(w_used, label + ".used"))

        ST = BIG[:, 0:17 * P].rearrange("p (b c) -> p b c", c=P)
        XIN = BIG[:, 4096:8192].rearrange("p (c d) -> p c d", d=D)

        flat1 = lambda ap: ap.rearrange("(r c) -> r c", c=P)
        flat2 = lambda ap: ap.rearrange("a (r c) -> (a r) c", c=P)
        blocks = []
        for l in range(DEPTH):
            blocks.append([flat1(a["ada_b"][l]), flat1(a["norm1_g"][l]), flat1(a["norm2_g"][l])]
                          + ([flat1(a["final_g"])] if l == 0 else []))
            conv = flat2(a["ffn_conv"][l])
            blocks += [[conv[0:66]], [conv[66:132]]]
        for j in range(2):
            blocks.append([flat2(a["rw_mu"][j]), flat2(a["rw_w0"][j]), flat2(a["rw_a0"][j]), flat1(a["rw_kk"][j]),
                           flat1(a["rw_ka"][j]), flat1(a["rw_rk"][j].rearrange("h n -> (h n)")),
                           flat1(a["rw_ln_g"][j]), flat1(a["rw_ln_b"][j])])
        blocks.append([flat2(a["ssd_conv_w"][0]), flat1(a["ssd_conv_b"][0])])
        blocks.append([flat1(a["ssd_norm_g"][0])])
        blocks.append([flat1(a["c_ctx"]), flat1(a["c"][0])])
        B_RW, B_SSD, B_SSDN, B_C = 12, 14, 15, 16
        nrows = [sum(x.shape[0] for x in b) for b in blocks]

        def start_sp():
            sp.dma_start(K[:, :], a["consts"]).then_inc(vec_loaded, C.mark(vec_loaded, "consts", 16))
            for b, parts in enumerate(blocks):
                r = 0
                for n, part in enumerate(parts):
                    sp.dma_start(ST[r:r + part.shape[0], b, :], part).then_inc(
                        vec_loaded, C.mark(vec_loaded, "params" if (b, n) == (16, len(parts) - 1) else None, 16))
                    r += part.shape[0]
            sp.dma_start(XIN[:, 0:2, :], a["ctx"][0].rearrange("(c p) d -> p c d", p=P)).then_inc(
                in_loaded, C.mark(in_loaded, None, 16))
            sp.dma_start(XIN[:, 2:4, :], a["x"][0].rearrange("(c p) d -> p c d", p=P)).then_inc(
                in_loaded, C.mark(in_loaded, "inputs", 16))

        def start_pe():
            pe.wait_ge(vec_loaded, C.at("params"))
            for b in range(17):
                mm = pe.transpose(PS[:, b // 4, (b % 4) * P:(b % 4) * P + nrows[b]], ST[0:nrows[b], b, :],
                                  const("ident")[0:nrows[b], 0:nrows[b]])
                if b == 0:
                    mm.then_inc(w_used, C.mark(w_used, None, 2))
                else:
                    mm.then_inc(pe_done, C.mark(pe_done, f"par{b}", LEAD if b == 1 else 1))
            pe.wait_ge(in_loaded, C.at("inputs"))
            for k in range(KD):
                bank = 5 + k % 3
                if k >= 3:
                    pe.wait_ge(act_done, C.at(f"x{k - 3}"))
                for c in range(NCH):
                    mm = pe.transpose(PS[:, bank, c * P:(c + 1) * P], XIN[:, c, k * P:(k + 1) * P], const("ident"))
                mm.then_inc(pe_done, C.mark(pe_done, f"xt{k}"))
            leave((pe_done, w_used), "start")

        def start_act():
            act.wait_ge(pe_done, C.at("par16"))
            act.wait_ge(vec_done, C.at("columns"))
            act.activation(SC[:, :, 0], PV[:, B_C, 0:KD], ACT.Silu).then_inc(act_done, C.mark(act_done, None, LEAD))
            s(act.activation(SC[:, :, 1], PV[:, B_C, KD:2 * KD], ACT.Silu), "silu_c")
            for k in range(KD):
                act.wait_ge(pe_done, C.at(f"xt{k}"))
                s(act.activation(X[:, k, :], PS[:, 5 + k % 3, :], ACT.Copy), f"x{k}")
            leave((act_done,), "start")

        def start_vec():
            vec.memset(MC[:, :], 0.0).then_inc(vec_done, C.mark(vec_done, None, LEAD))
            vec.wait_ge(vec_done, LEAD)
            for n, value in enumerate((EPS, GN_EPS, MID, -MID, KK_EPS)):
                v(vec.memset(MC[:, n:n + 1], value))
            v(vec.memset(MS[:, :, :, :], 0.0))
            vec.wait_ge(w_used, 2)
            vec.wait_ge(pe_done, C.at("par16"))
            for b in range(17):
                v(vec.tensor_copy(PV[:, b, 0:nrows[b]], PS[:, b // 4, (b % 4) * P:(b % 4) * P + nrows[b]]),
                  "columns" if b == 16 else None)
            leave((vec_done,), "start")

        ADA = BIG[:, 0:16384].rearrange("p (s k c) -> p s k c", s=4, k=KD)

        def ada_sp():
            enter(sp, (), "start")
            for l in range(DEPTH):
                w = rows(a["ada_w"][l])
                with C.loop(sp, f"ada{l}", 3) as i:
                    for q in range(4):
                        sp.wait_ge(pe_done, C.at(f"ada{l}.{q}", i, 1))
                        sp.sem_inc(loads_started, 1)
                        sp.dma_start(ADA[:, q], w[:, :, bass.ds(i * 2048 + q * 512, 512)]).then_inc(
                            ada_loaded[q], C.mark(ada_loaded[q], f"ada{l}.load{q}", 16))

        def ada_pe():
            pe.wait_ge(act_done, C.at("silu_c"))
            for l in range(DEPTH):
                with C.loop(pe, f"ada{l}", 3) as i:
                    for q in range(4):
                        if q % 2 == 0:
                            pe.wait_ge(vec_done, C.at(f"ada{l}.sum{q // 2}", i, 1))
                        pe.wait_ge(ada_loaded[q], C.at(f"ada{l}.load{q}", i))
                        for m in range(4):
                            for k in range(KD):
                                c = ((q % 2) * 4 + m) * 2
                                mm = pe.matmul(PS[:, q // 2, c:c + 2], ADA[:, q, k, m * P:(m + 1) * P], SC[:, k, :],
                                               start=k == 0, stop=k == KD - 1)
                        mm.then_inc(pe_done, C.mark(pe_done, f"ada{l}.{q}"))
            leave((pe_done, w_used), "ada")

        def ada_vec():
            enter(vec, (vec_done,), "start")
            for l in range(DEPTH):
                with C.loop(vec, f"ada{l}", 3) as i:
                    for h in range(2):
                        vec.wait_ge(pe_done, C.at(f"ada{l}.{2 * h + 1}", i))
                        bias = PV[:, 3 * l, bass.ds(i * 16 + h * 8, 8)].unsqueeze(2).broadcast_to([P, 8, 2])
                        v(vec.tensor_tensor(MOD[:, l, bass.ds(i * 16 + h * 8, 8), :],
                                            PS[:, h, 0:16].rearrange("p (t s) -> p t s", s=2), bias, ALU.add),
                          f"ada{l}.sum{h}", i)
            for l in range(DEPTH):
                for n in range(2):
                    gain = PV[:, 3 * l, 48 + 8 * n:56 + 8 * n].unsqueeze(2).broadcast_to([P, KD, 2])
                    v(vec.scalar_tensor_tensor(MS[:, 2 * l + n, :, :], MOD[:, l, 24 * n + 8:24 * n + 16, :], 1.0, gain,
                                               ALU.add, ALU.mult))
            v(vec.tensor_copy(MS[:, 2 * DEPTH, :, 1], PV[:, 0, 64:72]))
            leave((vec_done,), "ada")

        SQ = WORK[:, 0:1024].rearrange("p (b t) -> p b t", b=2)
        RS = WORK[:, 1024:1536]
        TMP = WORK[:, 1536:3584].rearrange("p (b t) -> p b t", b=4)

        def norm_pe(tag, prev, lo):
            enter(pe, (pe_done, w_used), prev)
            for k in range(KD):
                pe.wait_ge(act_done, C.at(f"{tag}.sq{k}"))
                pe.matmul(PS[:, 0, lo:T], const("mean"), SQ[:, k % 2, lo:T], start=k == 0,
                          stop=k == KD - 1).then_inc(pe_done, C.mark(pe_done, f"{tag}.ms{k}"))
            leave((pe_done, w_used), tag)

        def norm_act(tag, prev, lo, gain, shift):
            enter(act, (act_done,), prev)
            for k in range(KD):
                if k >= 2:
                    act.wait_ge(pe_done, C.at(f"{tag}.ms{k - 2}"))
                s(act.activation(SQ[:, k % 2, lo:T], X[:, k, lo:T], ACT.Square), f"{tag}.sq{k}")
            act.wait_ge(pe_done, C.at(f"{tag}.ms7"))
            s(act.activation(RS[:, lo:T], PS[:, 0, lo:T], ACT.Ln, bias=MC[:, 0:1]))
            s(act.activation(RS[:, lo:T], RS[:, lo:T], ACT.Exp, scale=-0.5), f"{tag}.rs")
            for k in range(KD):
                act.wait_ge(vec_done, C.at(f"{tag}.t{k}"))
                for n in range(2):
                    if n == 0 and lo:
                        continue
                    s(act.activation(Hk[:, k, SEGS[n]], TMP[:, k % 4, SEGS[n]], ACT.Identity,
                                     scale=MS[:, gain, k, n:n + 1], bias=shift(k, n)), f"{tag}.h{k}" if n else None)
            leave((act_done,), tag)

        def norm_vec(tag, prev, lo):
            enter(vec, (vec_done,), prev)
            vec.wait_ge(act_done, C.at(f"{tag}.rs"))
            for k in range(KD):
                if k >= 4:
                    vec.wait_ge(act_done, C.at(f"{tag}.h{k - 4}"))
                v(vec.tensor_tensor(TMP[:, k % 4, lo:T], X[:, k, lo:T], RS[:, lo:T], ALU.mult), f"{tag}.t{k}")
            leave((vec_done,), tag)

        def mod_shift(l, n2):
            return lambda k, n: MOD[:, l, 24 * n2 + k, n:n + 1]

        G = BIG[:, 0:NF * T].rearrange("p (f t) -> p f t", f=NF)
        CV = WORK[:, 0:2048].rearrange("p (q h t) -> p q h t", q=2, h=2)
        SG = WORK[:, 2048:3072].rearrange("p (q t) -> p q t", q=2)
        CW = WORK[:, 3072:3204]
        CWj = WORK[:, 3204:3216].rearrange("p (q h t) -> p q h t", q=2, h=2)

        def ffn_sp(l):
            w = rows(a["ffn_w_in"][l])
            with C.loop(sp, f"f{l}", NF // 2) as i:
                for q in range(2):
                    for h in range(2):
                        load_unit(i, f"f{l}.w{q}{h}", unit(w, 0, 8, i * 256 + q * P + h * F))
            w = rows(a["ffn_w_out"][l])
            with C.loop(sp, f"fo{l}", KD // 2) as i:
                for q in range(2):
                    for r in range(3):
                        load_unit(i, f"fo{l}.w{q}{r}", unit(w, 8 * r, 8 if r < 2 else 6, i * 256 + q * P))

        def ffn_pe(l, lo):
            enter(pe, (pe_done, w_used), f"n2{l}")
            with C.loop(pe, f"f{l}", NF // 2) as i:
                for q in range(2):
                    for h in range(2):
                        pe.wait_ge(vec_done, C.at(f"f{l}.cv{q}{h}", i, 1))
                        use_unit(i, f"f{l}.w{q}{h}", PS[:, 2 * q + h, lo:T], lambda k: Hk[:, k, lo:T], 8, True, True)
            pe.wait_ge(vec_done, C.at(f"f{l}.g1"))
            with C.loop(pe, f"fo{l}", KD // 2) as i:
                for q in range(2):
                    pe.wait_ge(vec_done, C.at(f"fo{l}.x{q}", i, 1))
                    for r in range(3):
                        nk = 8 if r < 2 else 6
                        use_unit(i, f"fo{l}.w{q}{r}", PS[:, 4 + q, lo:T], lambda k: G[:, 8 * r + k, lo:T], nk,
                                 r == 0, r == 2)
            leave((pe_done, w_used), f"ffn{l}")

        def ffn_act(l, lo):
            enter(act, (act_done,), f"n2{l}")
            act.wait_ge(vec_done, C.at(f"f{l}.cw"))
            with C.loop(act, f"f{l}", NF // 2) as i:
                for q in range(2):
                    act.wait_ge(vec_done, C.at(f"f{l}.cwj", i))
                    for h in range(2):
                        act.wait_ge(w_used, C.at(f"f{l}.w{q}{h}.used", i))
                        if h == 0:
                            act.wait_ge(vec_done, C.at(f"f{l}.g{q}", i, 1))
                        s(act.activation(CV[:, q, h, lo:T], PS[:, 2 * q + h, lo:T], ACT.Copy,
                                         scale=CWj[:, q, h, 1:2]), f"f{l}.c{q}{h}", i)
                for q in range(2):
                    act.wait_ge(vec_done, C.at(f"f{l}.cv{q}1", i))
                    s(act.activation(SG[:, q, lo:T], CV[:, q, 1, lo:T], ACT.Silu), f"f{l}.sg{q}", i)
            leave((act_done,), f"ffn{l}")

        def seg2(ap, lo, x0, x1):
            return ap[:, lo:T].rearrange("p (s t) -> p s t", t=SEG)[:, :, x0:x1]

        def taps(dst, src, w0, w2, lo, label=None, i=None):
            v(vec.scalar_tensor_tensor(seg2(dst, lo, 1, SEG), seg2(src, lo, 0, SEG - 1), w0, seg2(dst, lo, 1, SEG),
                                       ALU.mult, ALU.add), None, i)
            v(vec.scalar_tensor_tensor(seg2(dst, lo, 0, SEG - 1), seg2(src, lo, 1, SEG), w2,
                                       seg2(dst, lo, 0, SEG - 1), ALU.mult, ALU.add), label, i)

        def ffn_vec(l, lo):
            enter(vec, (vec_done,), f"n2{l}")
            v(vec.tensor_copy(CW[:, 0:66], PV[:, 3 * l + 1, 0:66]))
            v(vec.tensor_copy(CW[:, 66:132], PV[:, 3 * l + 2, 0:66]), f"f{l}.cw")
            taps3 = CW[:, 0:132].rearrange("p (t h f) -> p h f t", t=3, h=2)
            with C.loop(vec, f"f{l}", NF // 2) as i:
                vec.wait_ge(act_done, C.at(f"f{l}.c11", i, 1))
                for h in range(2):
                    v(vec.tensor_copy(CWj[:, :, h, :], taps3[:, h, bass.ds(i * 2, 2), :]), f"f{l}.cwj" if h else None, i)
                for q in range(2):
                    for h in range(2):
                        vec.wait_ge(act_done, C.at(f"f{l}.c{q}{h}", i))
                        taps(CV[:, q, h, :], PS[:, 2 * q + h, :], CWj[:, q, h, 0:1], CWj[:, q, h, 2:3], lo,
                             f"f{l}.cv{q}{h}", i)
                for q in range(2):
                    vec.wait_ge(act_done, C.at(f"f{l}.sg{q}", i))
                    v(vec.tensor_tensor(G[:, i * 2 + q, lo:T], CV[:, q, 0, lo:T], SG[:, q, lo:T], ALU.mult),
                      f"f{l}.g{q}", i)
            with C.loop(vec, f"fo{l}", KD // 2) as i:
                for q in range(2):
                    vec.wait_ge(w_used, C.at(f"fo{l}.w{q}2.used", i))
                    residual(i, q, PS[:, 4 + q, :], l, 5, lo, f"fo{l}.x{q}")
            leave((vec_done,), f"ffn{l}")

        def residual(i, q, ps, l, which, lo, label):
            for n in range(2):
                if n == 0 and lo:
                    continue
                m = i * 2 + q
                v(vec.scalar_tensor_tensor(X[:, m, SEGS[n]], ps[:, SEGS[n]], MOD[:, l, which * 8 + m, n:n + 1],
                                           X[:, m, SEGS[n]], ALU.mult, ALU.add), label if n else None, i)

        def proj_sp(tag, w, units):
            w = rows(w)
            with C.loop(sp, tag, KD // 2) as i:
                for q in range(2):
                    for r in range(units):
                        load_unit(i, f"{tag}.w{q}{r}", unit(w, 8 * r, 8, i * 256 + q * P))

        def proj_pe(tag, rhs, units, lo):
            with C.loop(pe, tag, KD // 2) as i:
                for q in range(2):
                    pe.wait_ge(vec_done, C.at(f"{tag}.x{q}", i, 1))
                    for r in range(units):
                        use_unit(i, f"{tag}.w{q}{r}", PS[:, q, lo:T], lambda k: rhs(8 * r + k), 8, r == 0,
                                 r == units - 1)

        def proj_vec(tag, l, units, lo):
            with C.loop(vec, tag, KD // 2) as i:
                for q in range(2):
                    vec.wait_ge(w_used, C.at(f"{tag}.w{q}{units - 1}.used", i))
                    residual(i, q, PS[:, q, :], l, 2, lo, f"{tag}.x{q}")

        OUT = BIG[:, 0:2048].rearrange("p (c d) -> p c d", d=D)

        def end_pe(prev):
            enter(pe, (pe_done, w_used), prev)
            for c in range(2):
                for h in range(2):
                    for k in range(4):
                        mm = pe.transpose(PS[:, 2 * c + h, k * P:(k + 1) * P],
                                          Hk[:, 4 * h + k, (2 + c) * P:(3 + c) * P], const("ident"))
                    mm.then_inc(pe_done, C.mark(pe_done, f"out{c}{h}"))

        def end_act(prev):
            enter(act, (act_done,), prev)
            for c in range(2):
                for h in range(2):
                    act.wait_ge(pe_done, C.at(f"out{c}{h}"))
                    s(act.activation(OUT[:, c, h * 512:(h + 1) * 512], PS[:, 2 * c + h, :], ACT.Copy), f"o{c}{h}")

        def end_sp():
            for c in range(2):
                sp.wait_ge(act_done, C.at(f"o{c}1"))
                sp.dma_start(out[0, c * P:(c + 1) * P, :], OUT[:, c, :]).then_inc(stored, C.mark(stored, None, 16))
            sp.wait_ge(stored, C.here(stored))

        QKV = BIG[:, 0:6144].rearrange("p (m t) -> p m t", m=12)
        AO = BIG[:, 6144:10240].rearrange("p (m t) -> p m t", m=KD)
        VTOK = BIG[:, 10240:11264].rearrange("p (c d) -> p c d", c=NCH)
        KDUP = BIG[:, 11264:13312].rearrange("p (g t) -> p g t", g=4)
        AC = BIG[:, 13312:13312 + 13 * P]
        SINK = BIG[:, 15104:15120]
        COS, SIN, ROT = AC[:, 0:256], AC[:, 256:512], AC[:, 512:640]
        DUP = [AC[:, (5 + h) * P:(6 + h) * P] for h in range(2)]
        DUPROT = [AC[:, (7 + h) * P:(8 + h) * P] for h in range(2)]
        AMASK = [AC[:, (9 + 2 * b) * P:(11 + 2 * b) * P] for b in range(2)]
        RT = WORK[:, 0:1024].rearrange("p (b t) -> p b t", t=SEG)
        PX = WORK[:, 1024:3072].rearrange("p (e t) -> p e t", e=4)
        PT = WORK[:, 3072:5120].rearrange("p (e t) -> p e t", e=4)
        KG = WORK[:, 5120:5632]
        QG = WORK[:, 5632:6656].rearrange("p (m t) -> p m t", m=2)
        VG = WORK[:, 6656:6912].rearrange("p (c d) -> p c d", c=NCH)
        SM = WORK[:, 6912:6948]
        MX, NM, RSUM, ES, RD, SKG, MX8 = (SM[:, 4 * n:4 * n + 4] for n in range(7))

        def attn_pool(l):
            enter(pool, (), f"n1{l}")
            pool.dma_start(AC, a["attn_consts"]).then_inc(side_loaded[0], C.mark(side_loaded[0], None, 16))
            pool.dma_start(SINK, a["at_sink"][0].partition_broadcast(P)).then_inc(
                side_loaded[0], C.mark(side_loaded[0], "attn.consts", 16))

        def attn_sp(l):
            w = rows(a["at_w_qkv"][0])
            with C.loop(sp, "qkv", 6) as i:
                for q in range(2):
                    load_unit(i, f"qkv.w{q}", unit(w, 0, 8, i * 256 + q * P))
            proj_sp(f"mo{l}", a["at_w_o"][0], 1)

        def attn_pe(l, lo):
            enter(pe, (pe_done, w_used), f"n1{l}")
            with C.loop(pe, "qkv", 6) as i:
                for q in range(2):
                    pe.wait_ge(act_done, C.at(f"qkv.e{q}", i, 1))
                    use_unit(i, f"qkv.w{q}", PS[:, q, :], lambda k: Hk[:, k, :], 8, True, True)
            pe.wait_ge(act_done, C.at("qkv.e1"))
            pe.wait_ge(side_loaded[0], C.at("attn.consts"))
            with C.loop(pe, "rope", 4) as i:
                for q in range(2):
                    pe.wait_ge(vec_done, C.at(f"rope.t{q}", i, 1))
                    pe.matmul(PS[:, 2 + q, 0:SEG], ROT, QKV[:, i * 2 + q, SEG:T], start=True,
                              stop=True).then_inc(pe_done, C.mark(pe_done, f"rope.r{q}"))
            for kv in range(4):
                pe.matmul(PS[:, 4 + kv % 2, :], DUP[kv % 2], QKV[:, 8 + kv // 2, :], start=True, stop=True)
                if kv >= 2:
                    pe.wait_ge(vec_done, C.at(f"kd{kv - 2}"))
                pe.matmul(PS[:, 6 + kv % 2, 0:SEG], DUPROT[kv % 2], QKV[:, 8 + kv // 2, SEG:T], start=True,
                          stop=True).then_inc(pe_done, C.mark(pe_done, f"kr{kv}"))
                if kv == 1:
                    pe.wait_ge(vec_done, C.at("kd1"))
            for m in range(2):
                for c in range(NCH):
                    mm = pe.transpose(PS[:, m, c * P:(c + 1) * P], QKV[:, 10 + m, c * P:(c + 1) * P], const("ident"))
                mm.then_inc(pe_done, C.mark(pe_done, f"vt{m}"))
            with C.loop(pe, "heads", 4) as i:
                pe.wait_ge(vec_done, C.at("heads.in", i))
                pe.wait_ge(act_done, C.at("heads.in.a", i))
                for b in range(4):
                    nk = SEG if b < 2 else T
                    for e in range(4):
                        if e == 0:
                            pe.wait_ge(vec_done, C.at(f"heads.o{b - 1}", i) if b else C.at("heads.in", i))
                        h = slice(64 * (e % 2), 64 * (e % 2) + 64)
                        pe.matmul(PS[:, e, 0:nk], QG[h, e // 2, b * P:(b + 1) * P], KG[h, 0:nk], start=True,
                                  stop=True).then_inc(pe_done, C.mark(pe_done, f"heads.s{b}{e}"))
                    for e in range(4):
                        pe.wait_ge(vec_done, C.at(f"heads.p{b}{e}", i))
                        for kc in range(nk // P):
                            mm = pe.transpose(PS[:, 4 + e, kc * P:(kc + 1) * P], PX[:, e, kc * P:(kc + 1) * P],
                                              const("ident"))
                        mm.then_inc(pe_done, C.mark(pe_done, f"heads.pt{b}{e}"))
                    for e in range(4):
                        pe.wait_ge(act_done, C.at(f"heads.pc{b}{e}", i))
                        h = slice(64 * (e % 2), 64 * (e % 2) + 64)
                        for kc in range(nk // P):
                            mm = pe.matmul(PS[h, e // 2, 0:P], VG[:, kc, :], PT[:, e, kc * P:(kc + 1) * P],
                                           start=kc == 0, stop=kc == nk // P - 1)
                    mm.then_inc(pe_done, C.mark(pe_done, f"heads.ov{b}"))
            pe.wait_ge(vec_done, C.at("heads.o3"))
            proj_pe(f"mo{l}", lambda k: AO[:, k, lo:T], 1, lo)
            leave((pe_done, w_used), f"mix{l}")

        def attn_act(l, lo):
            enter(act, (act_done,), f"n1{l}")
            with C.loop(act, "qkv", 6) as i:
                for q in range(2):
                    act.wait_ge(w_used, C.at(f"qkv.w{q}.used", i))
                    s(act.activation(QKV[:, i * 2 + q, :], PS[:, q, :], ACT.Copy), f"qkv.e{q}", i)
            for m in range(2):
                act.wait_ge(pe_done, C.at(f"vt{m}"))
                s(act.activation(VTOK[:, :, m * P:(m + 1) * P], PS[:, m, :].rearrange("p (c d) -> p c d", c=NCH),
                                 ACT.Copy), f"vtok{m}")
            act.wait_ge(vec_done, C.at("kd3"))
            act.wait_ge(vec_done, C.at("rope.q1"))
            with C.loop(act, "heads", 4) as i:
                act.wait_ge(pe_done, C.at("heads.ov3", i, 1))
                s(act.activation(KG, KDUP[:, i, :], ACT.Copy), None, i)
                s(act.activation(VG[:, :, :], VTOK[:, :, bass.ds(i * 64, 64)], ACT.Copy), "heads.in.a", i)
                for b in range(4):
                    nk = SEG if b < 2 else T
                    act.wait_ge(vec_done, C.at(f"heads.nm{b}", i))
                    for e in range(4):
                        s(act.activation(PX[:, e, 0:nk], PS[:, e, 0:nk], ACT.Exp, bias=NM[:, e:e + 1], scale=0.125,
                                         accum_out=RSUM[:, e:e + 1]), f"heads.ex{b}{e}", i)
                    s(act.activation(ES, ES, ACT.Exp), f"heads.es{b}", i)
                    for e in range(4):
                        act.wait_ge(pe_done, C.at(f"heads.pt{b}{e}", i))
                        s(act.activation(PT[:, e, 0:nk], PS[:, 4 + e, 0:nk], ACT.Copy), f"heads.pc{b}{e}", i)
            leave((act_done,), f"mix{l}")

        def attn_vec(l, lo):
            enter(vec, (vec_done,), f"n1{l}")
            vec.wait_ge(side_loaded[0], C.at("attn.consts"))
            vec.wait_ge(act_done, C.at("qkv.e1"))
            with C.loop(vec, "rope", 4) as i:
                for q in range(2):
                    m = i * 2 + q
                    vec.wait_ge(pe_done, C.at(f"rope.r{q}", i))
                    v(vec.tensor_tensor(RT[:, q, :], PS[:, 2 + q, 0:SEG], SIN, ALU.mult), f"rope.t{q}", i)
                    v(vec.tensor_tensor(QKV[:, m, SEG:T], QKV[:, m, SEG:T], COS, ALU.mult), None, i)
                    v(vec.tensor_tensor(QKV[:, m, SEG:T], QKV[:, m, SEG:T], RT[:, q, :], ALU.add), f"rope.q{q}", i)
            for kv in range(4):
                vec.wait_ge(pe_done, C.at(f"kr{kv}"))
                v(vec.tensor_tensor(RT[:, 2, :], PS[:, 6 + kv % 2, 0:SEG], SIN, ALU.mult))
                v(vec.tensor_tensor(RT[:, 3, :], PS[:, 4 + kv % 2, SEG:T], COS, ALU.mult))
                v(vec.tensor_copy(KDUP[:, kv, 0:SEG], PS[:, 4 + kv % 2, 0:SEG]))
                v(vec.tensor_tensor(KDUP[:, kv, SEG:T], RT[:, 2, :], RT[:, 3, :], ALU.add), f"kd{kv}")
            with C.loop(vec, "heads", 4) as i:
                vec.wait_ge(pe_done, C.at("heads.ov3", i, 1))
                v(vec.tensor_copy(QG[:, :, :], QKV[:, bass.ds(i * 2, 2), :]), None, i)
                v(vec.tensor_copy(SKG, SINK[:, bass.ds(i * 4, 4)]), "heads.in", i)
                for b in range(4):
                    nk = SEG if b < 2 else T
                    for e in range(4):
                        vec.wait_ge(pe_done, C.at(f"heads.s{b}{e}", i))
                        if b >= 2:
                            v(vec.tensor_tensor(PS[:, e, SEG:T], PS[:, e, SEG:T], AMASK[b - 2], ALU.add), None, i)
                        v(vec.reduce_max(MX[:, e:e + 1], PS[:, e, 0:nk], AX_X), None, i)
                    v(vec.tensor_scalar(MX8, MX, 0.125, None, ALU.mult), None, i)
                    v(vec.tensor_tensor(MX8, MX8, SKG, ALU.max), None, i)
                    v(vec.tensor_tensor(ES, SKG, MX8, ALU.subtract), None, i)
                    v(vec.tensor_scalar(NM, MX8, -1.0, None, ALU.mult), f"heads.nm{b}", i)
                    vec.wait_ge(act_done, C.at(f"heads.es{b}", i))
                    v(vec.tensor_tensor(RD, RSUM, ES, ALU.add), None, i)
                    v(vec.reciprocal(RD, RD), None, i)
                    for e in range(4):
                        v(vec.tensor_scalar(PX[:, e, 0:nk], PX[:, e, 0:nk], RD[:, e:e + 1], None, ALU.mult),
                          f"heads.p{b}{e}", i)
                    vec.wait_ge(pe_done, C.at(f"heads.ov{b}", i))
                    v(vec.tensor_copy(AO[:, bass.ds(i * 2, 2), b * P:(b + 1) * P], PS[:, 0:2, 0:P]),
                      f"heads.o{b}", i)
            proj_vec(f"mo{l}", l, 1, lo)
            leave((vec_done,), f"mix{l}")

        YB = BIG[:, 0:8192].rearrange("p (m t) -> p m t", m=16)
        ACB = BIG[:, 8192:12288].rearrange("p (r t) -> p r t", r=8)
        FS = BIG[:, 12288:16384].rearrange("p (r t) -> p r t", r=8)
        XT = BIG[:, 16384:17408].rearrange("p (c f) -> p c f", c=NCH)
        BT = BIG[:, 17408:17920].rearrange("p (c f) -> p c f", c=NCH)
        XDT = BIG[:, 17920:19968].rearrange("p (d c f) -> p d c f", d=2, c=NCH)
        DCOL = BIG[:, 19968:19984]
        DTB, ALOG = BIG[0:64, 19984:19985], BIG[0:64, 19985:19986]
        DALL = BIG[:, 20000:20032]
        DTw = [BIG[0:64, 12288 + 512 * n:12800 + 512 * n] for n in range(8)]
        XTE = WORK[:, 0:2048].rearrange("p (d c f) -> p d c f", d=2, c=NCH)
        XS = WORK[:, 2048:4096].rearrange("p (m t) -> p m t", m=4)
        ZS = WORK[:, 4096:5120].rearrange("p (m t) -> p m t", m=2)
        CBM = WORK[:, 5120:6144].rearrange("p (d c t) -> p d c t", d=2, c=NCH)
        SEGM = WORK[:, 6144:7168].rearrange("p (b e t) -> p b e t", b=2, e=4)
        MM_ = WORK[:, 7168:8192].rearrange("p (b e t) -> p b e t", b=2, e=4)
        YT_ = WORK[:, 8192:9216].rearrange("p (m t) -> p m t", m=2)
        STT_ = WORK[:, 9216:9728].rearrange("p (d f) -> p d f", d=2)
        DTT = WORK[:, 9728:9984].rearrange("p (c h) -> p c h", c=NCH)
        ACST = WORK[:, 9984:10240].rearrange("p (c h) -> p c h", c=NCH)
        TE = WORK[:, 10240:10272].rearrange("p (d c e) -> p d c e", d=2, c=NCH)
        CD = WORK[:, 10272:10304].rearrange("p (d c e) -> p d c e", d=2, c=NCH)
        ACG = WORK[:, 10304:10336].rearrange("p (c d e) -> p c d e", d=2, c=NCH)
        DTG = WORK[:, 10336:10368].rearrange("p (c d e) -> p c d e", d=2, c=NCH)
        CP = WORK[:, 10368:10384].rearrange("p (k m) -> p k m", k=4)
        DG, NG = WORK[:, 10384:10386], WORK[:, 10386:10388]
        SQG = WORK[:, 10400:11424].rearrange("p (m t) -> p m t", m=2)
        RSG = WORK[:, 11424:11936]
        END = (P - 1, 0)

        def ssd_pool(l):
            enter(pool, (), f"n1{l}")
            pool.dma_start(DALL, a["ssd_d"][0].partition_broadcast(P)).then_inc(
                side_loaded[1], C.mark(side_loaded[1], None, 16))
            pool.dma_start(DTB, a["ssd_dt_bias"][0].rearrange("d h -> (d h)").unsqueeze(1)).then_inc(
                side_loaded[1], C.mark(side_loaded[1], None, 16))
            pool.dma_start(ALOG, a["ssd_a_log"][0].rearrange("d h -> (d h)").unsqueeze(1)).then_inc(
                side_loaded[1], C.mark(side_loaded[1], "ssd.params", 16))
            pool.wait_ge(vec_done, C.at("ssd.acs"))
            pool.dma_start(scratch, DTw[7]).then_inc(scratch_stored, C.mark(scratch_stored, "ssd.stored", 16))
            pool.wait_ge(scratch_stored, C.at("ssd.stored"))
            by_group = scratch.rearrange("(d g e) t -> g d e t", d=2, e=4)
            with C.loop(pool, "ssd", 8) as i:
                pool.wait_ge(vec_done, C.at("ssd.sg31", i, 1))
                pool.wait_ge(act_done, C.at("ssd.fs", i, 1))
                pool.dma_start(ACB[:, :, :].rearrange("p (d e) t -> p d e t", d=2),
                               by_group[i].partition_broadcast(P)).then_inc(
                    side_loaded[2], C.mark(side_loaded[2], "ssd.acbload", 16))

        def ssd_sp(l):
            w = rows(a["ssd_w_in"][0])
            load_unit(None, "ssd.wdt", unit(w, 0, 8, INNER + 4096, 64))
            with C.loop(sp, "ssd", 8) as i:
                for q, c0 in enumerate((i * 256 + INNER, i * 256 + (INNER + P), i * P + 2 * INNER,
                                        i * P + 2 * INNER + 1024, i * 256, i * 256 + P)):
                    load_unit(i, f"ssd.w{q}", unit(w, 0, 8, c0))
            proj_sp(f"mo{l}", a["ssd_w_out"][0], 2)

        def ssd_pe(l, lo):
            enter(pe, (pe_done, w_used), f"n1{l}")
            use_unit(None, "ssd.wdt", PS[0:64, 0, :], lambda k: Hk[:, k, :], 8, True, True, 64)
            pe.wait_ge(vec_done, C.at("ssd.acs"))
            for n, src in ((1, DTw[6]), (2, DTw[7])):
                for c in range(NCH):
                    mm = pe.transpose(PS[:, n, c * 64:(c + 1) * 64], src[:, c * P:(c + 1) * P],
                                      const("ident")[0:64, 0:64])
                mm.then_inc(pe_done, C.mark(pe_done, f"ssd.tr{n}"))
            pe.wait_ge(vec_done, C.at("ssd.acst"))
            with C.loop(pe, "ssd", 8) as i:
                pe.wait_ge(vec_done, C.at("ssd.y31", i, 1))
                for q in range(6):
                    use_unit(i, f"ssd.w{q}", PS[:, q, :], lambda k: Hk[:, k, :], 8, True, True)
                for q in range(3):
                    pe.wait_ge(act_done, C.at(f"ssd.silu{q}", i))
                    for c in range(NCH):
                        mm = pe.transpose(PS[:, (6, 7, 0)[q], c * P:(c + 1) * P], XS[:, q, c * P:(c + 1) * P],
                                          const("ident"))
                    mm.then_inc(pe_done, C.mark(pe_done, f"ssd.xt{q}"))
                pe.wait_ge(act_done, C.at("ssd.silu3", i))
                for c in range(NCH):
                    cs = slice(c * P, (c + 1) * P)
                    mm = pe.matmul(PS[:, 1, cs], XS[:, 2, cs], XS[:, 3, cs], start=True, stop=True)
                mm.then_inc(pe_done, C.mark(pe_done, "ssd.cb"))
                pe.wait_ge(vec_done, C.at("ssd.xte", i))
                pe.wait_ge(act_done, C.at("ssd.bt", i))
                pe.wait_ge(act_done, C.at("ssd.z1", i))
                for c in range(NCH):
                    for d in range(2):
                        ch = ORDER[d][c]
                        cs = slice(ch * P, (ch + 1) * P)
                        if c < NCH - 1:
                            if c:
                                pe.wait_ge(vec_done, C.at(f"ssd.st{c - 1}{d}", i))
                            pe.matmul(PS[:, 4 + d, 0:256], BT[:, ch, :], XTE[:, d, ch, :], start=True,
                                      stop=True).then_inc(pe_done, C.mark(pe_done, f"ssd.s{c}{d}"))
                        pe.wait_ge(vec_done, C.at(f"ssd.m{c}{d}", i))
                        for e in range(4):
                            h = slice(64 * (e % 2), 64 * (e % 2) + 64)
                            o = PS[h, 2 + d, (e // 2) * P:(e // 2 + 1) * P]
                            ef = slice(e * 64, (e + 1) * 64)
                            mm = pe.matmul(o, XDT[:, d, ch, ef], MM_[:, d, e, :], start=True, stop=c == 0)
                            if c:
                                mm = pe.matmul(o, STT_[:, d, ef], FS[:, 4 * d + e, cs], start=False, stop=True)
                        mm.then_inc(pe_done, C.mark(pe_done, f"ssd.yo{c}{d}"))
                pe.wait_ge(act_done, C.at("ssd.sq", i))
                for m in range(2):
                    mm = pe.matmul(PS[:, 6, :], const("mean256"), SQG[:, m, :], start=m == 0, stop=m == 1)
                mm.then_inc(pe_done, C.mark(pe_done, "ssd.ms"))
            pe.wait_ge(vec_done, C.at("ssd.yb"))
            proj_pe(f"mo{l}", lambda k: YB[:, k, lo:T], 2, lo)
            leave((pe_done, w_used), f"mix{l}")

        def ssd_act(l, lo):
            enter(act, (act_done,), f"n1{l}")
            act.wait_ge(vec_done, C.at("ssd.z"))
            s(act.activation(DTw[1], DTw[0], ACT.Abs))
            s(act.activation(DTw[1], DTw[1], ACT.Exp, scale=-1.0), "ssd.e")
            act.wait_ge(side_loaded[1], C.at("ssd.params"))
            s(act.activation(ALOG, ALOG, ACT.Exp), "ssd.a")
            act.wait_ge(vec_done, C.at("ssd.acst"))
            act.wait_ge(scratch_stored, C.at("ssd.stored"))
            with C.loop(act, "ssd", 8) as i:
                act.wait_ge(vec_done, C.at("ssd.cp", i))
                act.wait_ge(pe_done, C.at("ssd.ms", i, 1))
                for q in range(4):
                    act.wait_ge(w_used, C.at(f"ssd.w{q}.used", i))
                    s(act.activation(XS[:, q, :], PS[:, q, :], ACT.Identity, scale=CP[:, 1, q:q + 1],
                                     bias=CP[:, 3, q:q + 1]), f"ssd.c{q}", i)
                for q in range(4):
                    act.wait_ge(vec_done, C.at(f"ssd.cv{q}", i))
                    s(act.activation(XS[:, q, :], XS[:, q, :], ACT.Silu), f"ssd.silu{q}", i)
                for q in range(2):
                    act.wait_ge(w_used, C.at(f"ssd.w{4 + q}.used", i))
                    s(act.activation(ZS[:, q, :], PS[:, 4 + q, :], ACT.Silu), f"ssd.z{q}", i)
                for q in range(2):
                    act.wait_ge(pe_done, C.at(f"ssd.xt{q}", i))
                    s(act.activation(XT[:, :, q * P:(q + 1) * P], PS[:, 6 + q, :].rearrange("p (c f) -> p c f", c=NCH),
                                     ACT.Copy), f"ssd.xtok{q}", i)
                act.wait_ge(pe_done, C.at("ssd.xt2", i))
                s(act.activation(BT[:, :, :], PS[:, 0, :].rearrange("p (c f) -> p c f", c=NCH), ACT.Copy), "ssd.bt", i)
                act.wait_ge(vec_done, C.at("ssd.te0", i))
                s(act.activation(TE[:, :, :, :], TE[:, :, :, :], ACT.Exp), "ssd.te", i)
                act.wait_ge(side_loaded[2], C.at("ssd.acbload", i))
                for r in range(8):
                    s(act.activation(FS[:, r, :], ACB[:, r, :], ACT.Exp), "ssd.fs" if r == 7 else None, i)
                for c in range(NCH):
                    for d in range(2):
                        act.wait_ge(vec_done, C.at(f"ssd.sg{c}{d}", i))
                        s(act.activation(SEGM[:, d, :, :], SEGM[:, d, :, :], ACT.Exp), f"ssd.ex{c}{d}", i)
                act.wait_ge(vec_done, C.at("ssd.yz", i))
                s(act.activation(SQG[:, :, :], YT_[:, :, :], ACT.Square), "ssd.sq", i)
                act.wait_ge(pe_done, C.at("ssd.ms", i))
                s(act.activation(RSG, PS[:, 6, :], ACT.Ln, bias=MC[:, 0:1]), None, i)
                s(act.activation(RSG, RSG, ACT.Exp, scale=-0.5), "ssd.rs", i)
            leave((act_done,), f"mix{l}")

        def ssd_vec(l, lo):
            enter(vec, (vec_done,), f"n1{l}")
            Z, E, R, S, S2, Q, DT, AC_ = DTw
            vec.wait_ge(side_loaded[1], C.at("ssd.params"))
            for h in range(2):
                ph = slice(64 * h, 64 * h + 64)
                v(vec.tensor_copy(DCOL[ph, :], DALL[ph, :].rearrange("p (m h) -> p h m", h=2)[:, h, :]))
            vec.wait_ge(w_used, C.at("ssd.wdt.used"))
            v(vec.tensor_scalar(Z, PS[0:64, 0, :], DTB, None, ALU.add), "ssd.z")
            vec.wait_ge(act_done, C.at("ssd.e"))
            v(vec.tensor_scalar(R, E, 2.0, None, ALU.add))
            v(vec.reciprocal(R, R))
            v(vec.tensor_tensor(S, E, R, ALU.mult))
            v(vec.tensor_tensor(S2, S, S, ALU.mult))
            v(vec.tensor_scalar(Q, S2, 1.0 / 15, None, ALU.mult))
            for n in (13, 11, 9, 7, 5, 3):
                v(vec.scalar_tensor_tensor(Q, Q, 1.0 / n, S2, ALU.add, ALU.mult))
            v(vec.scalar_tensor_tensor(Q, Q, 1.0, S, ALU.add, ALU.mult))
            v(vec.tensor_scalar(Z, Z, 0.0, None, ALU.max))
            v(vec.scalar_tensor_tensor(DT, Q, 2.0, Z, ALU.mult, ALU.add))
            vec.wait_ge(act_done, C.at("ssd.a"))
            v(vec.tensor_scalar(ALOG, ALOG, -1.0, None, ALU.mult))
            v(vec.tensor_scalar(S, DT, ALOG, None, ALU.mult))
            for c in range(NCH):
                cs = slice(c * P, (c + 1) * P)
                v(vec.tensor_tensor_scan(AC_[:, cs], const("ones")[0:64, :], S[:, cs], 0.0, ALU.mult, ALU.add))
            b3 = lambda ap: ap[32:64, :].rearrange("p (c t) -> p c t", c=NCH)
            v(vec.tensor_tensor(b3(Q), b3(AC_)[:, :, P - 1:P].broadcast_to([32, NCH, P]), b3(AC_), ALU.subtract))
            v(vec.tensor_tensor(b3(AC_), b3(Q), b3(S), ALU.add), "ssd.acs")
            for n, dst in ((1, DTT), (2, ACST)):
                vec.wait_ge(pe_done, C.at(f"ssd.tr{n}"))
                v(vec.tensor_copy(dst[:, :, :], PS[:, n, 0:256].rearrange("p (c h) -> p c h", c=NCH)),
                  "ssd.acst" if n == 2 else None)
            cw = PV[:, B_SSD, :].rearrange("p (k m) -> p k m", k=4)
            with C.loop(vec, "ssd", 8) as i:
                v(vec.tensor_copy(CP[:, :, 0:2], cw[:, :, bass.ds(i * 2, 2)]), None, i)
                v(vec.tensor_copy(CP[:, :, 2], cw[:, :, i + 16]), None, i)
                v(vec.tensor_copy(CP[:, :, 3], cw[:, :, i + 24]), None, i)
                for d in range(2):
                    v(vec.tensor_copy(ACG[:, :, d, :], ACST[:, :, bass.ds(i * 4 + 32 * d, 4)]), None, i)
                    v(vec.tensor_copy(DTG[:, :, d, :], DTT[:, :, bass.ds(i * 4 + 32 * d, 4)]), None, i)
                v(vec.tensor_copy(DG, DCOL[:, bass.ds(i * 2, 2)]), None, i)
                v(vec.tensor_copy(NG, PV[:, B_SSDN, bass.ds(i * 2, 2)]), "ssd.cp", i)
                for q in range(4):
                    vec.wait_ge(act_done, C.at(f"ssd.c{q}", i))
                    taps(XS[:, q, :], PS[:, q, :], CP[:, 0, q:q + 1], CP[:, 2, q:q + 1], 0, f"ssd.cv{q}", i)
                vec.wait_ge(side_loaded[2], C.at("ssd.acbload", i))
                for d in range(2):
                    ends = ACB[:, 4 * d:4 * d + 4, :].rearrange("p e (c t) -> p c e t", c=NCH)[:, :, :, END[d]]
                    v(vec.tensor_tensor(TE[:, d, :, :], ends, ACG[:, :, d, :], ALU.subtract),
                      "ssd.te0" if d else None, i)
                for q in range(2):
                    vec.wait_ge(act_done, C.at(f"ssd.xtok{q}", i))
                xt4 = XT[:, :, :].rearrange("p c (e f) -> p c e f", e=4)
                for d in range(2):
                    v(vec.tensor_tensor(XDT[:, d, :, :].rearrange("p c (e f) -> p c e f", e=4), xt4,
                                        DTG[:, :, d, :].unsqueeze(3).broadcast_to([P, NCH, 4, 64]), ALU.mult), None, i)
                vec.wait_ge(act_done, C.at("ssd.te", i))
                for d in range(2):
                    v(vec.tensor_tensor(XTE[:, d, :, :].rearrange("p c (e f) -> p c e f", e=4),
                                        XDT[:, d, :, :].rearrange("p c (e f) -> p c e f", e=4),
                                        TE[:, d, :, :].unsqueeze(3).broadcast_to([P, NCH, 4, 64]), ALU.mult), None, i)
                vec.wait_ge(pe_done, C.at("ssd.cb", i))
                for d in range(2):
                    v(vec.tensor_tensor(CBM[:, d, :, :], PS[:, 1, :].rearrange("p (c t) -> p c t", c=NCH),
                                        const(f"gi{d}").unsqueeze(1).broadcast_to([P, NCH, P]), ALU.mult), None, i)
                vec.wait_ge(act_done, C.at("ssd.fs", i))
                for d in range(2):
                    ends = FS[:, 4 * d:4 * d + 4, :].rearrange("p e (c t) -> p c e t", c=NCH)[:, :, :, END[d]]
                    v(vec.tensor_copy(CD[:, d, :, :], ends), None, i)
                v(vec.tensor_tensor(FS[:, :, :], FS[:, :, :], XS[:, 3, :].unsqueeze(1).broadcast_to([P, 8, T]),
                                    ALU.mult), "ssd.xte", i)

                def segs(c, d):
                    ch = ORDER[d][c]
                    for e in range(4):
                        v(vec.tensor_scalar(SEGM[:, d, e, :], ACB[:, 4 * d + e, ch * P:(ch + 1) * P],
                                            ACG[:, ch, d, e:e + 1], 0.0, ALU.subtract, ALU.min),
                          f"ssd.sg{c}{d}" if e == 3 else None, i)

                def gather(c, d):
                    ch = ORDER[d][c]
                    cs = slice(ch * P, (ch + 1) * P)
                    if c < NCH - 1:
                        vec.wait_ge(pe_done, C.at(f"ssd.yo{c}{d}", i))
                        if c:
                            v(vec.tensor_tensor(STT_[:, d, :].rearrange("p (e f) -> p e f", e=4),
                                                STT_[:, d, :].rearrange("p (e f) -> p e f", e=4),
                                                CD[:, d, ch, :].unsqueeze(2).broadcast_to([P, 4, 64]), ALU.mult),
                              None, i)
                            v(vec.tensor_tensor(STT_[:, d, :], STT_[:, d, :], PS[:, 4 + d, 0:256], ALU.add),
                              f"ssd.st{c}{d}", i)
                        else:
                            v(vec.tensor_copy(STT_[:, d, :], PS[:, 4 + d, 0:256]), f"ssd.st{c}{d}", i)
                    else:
                        vec.wait_ge(pe_done, C.at(f"ssd.yo{c}{d}", i))
                    y = PS[:, 2 + d, 0:256].rearrange("p (m t) -> p m t", m=2)
                    if c % 2 == 0:
                        v(vec.tensor_copy(YT_[:, :, cs], y), f"ssd.y{c}{d}", i)
                    else:
                        v(vec.tensor_tensor(YT_[:, :, cs], YT_[:, :, cs], y, ALU.add), f"ssd.y{c}{d}", i)

                steps = [(c, d) for c in range(NCH) for d in range(2)]
                for d in range(2):
                    segs(0, d)
                for n, (c, d) in enumerate(steps):
                    ch = ORDER[d][c]
                    vec.wait_ge(act_done, C.at(f"ssd.ex{c}{d}", i))
                    if c:
                        vec.wait_ge(pe_done, C.at(f"ssd.yo{c - 1}{d}", i))
                    v(vec.tensor_tensor(MM_[:, d, :, :], SEGM[:, d, :, :],
                                        CBM[:, d, ch, :].unsqueeze(1).broadcast_to([P, 4, P]), ALU.mult),
                      f"ssd.m{c}{d}", i)
                    if c < NCH - 1:
                        segs(c + 1, d)
                    if n:
                        gather(*steps[n - 1])
                gather(*steps[-1])
                for m in range(2):
                    v(vec.scalar_tensor_tensor(YT_[:, m, :], XS[:, m, :], DG[:, m:m + 1], YT_[:, m, :], ALU.mult,
                                               ALU.add), None, i)
                v(vec.tensor_tensor(YT_[:, :, :], YT_[:, :, :], ZS[:, :, :], ALU.mult), "ssd.yz", i)
                vec.wait_ge(act_done, C.at("ssd.rs", i))
                for m in range(2):
                    v(vec.scalar_tensor_tensor(YB[:, i * 2 + m, :], YT_[:, m, :], NG[:, m:m + 1], RSG, ALU.mult,
                                               ALU.mult), "ssd.yb" if m else None, i)
            proj_vec(f"mo{l}", l, 2, lo)
            leave((vec_done,), f"mix{l}")

        RKV = BIG[:, 0:12288].rearrange("p (n k t) -> p n k t", n=3, k=KD)
        XM = BIG[:, 12288:16384].rearrange("p (k t) -> p k t", k=KD)
        DX = BIG[:, 16384:20480].rearrange("p (k t) -> p k t", k=KD)
        _w = [0]

        def work(n):
            _w[0] += n
            assert _w[0] <= 14976
            return WORK[:, _w[0] - n:_w[0]]

        TH, AL, GS = work(512), work(512), work(512)
        W2S, A2S, G2S = work(P), work(P), work(P)
        SD = work(1024).rearrange("p (d t) -> p d t", d=2)
        AD = work(1024).rearrange("p (d t) -> p d t", d=2)
        AR = work(2048).rearrange("p (d n t) -> p d n t", d=2, n=2)
        PN = work(1024).rearrange("p (d t) -> p d t", d=2)
        KK, KF, BV, YT, BS = (work(512) for _ in range(5))
        KBT = work(1024).rearrange("p (d c f) -> p d c f", d=2, c=NCH)
        BNT = work(1024).rearrange("p (d c f) -> p d c f", d=2, c=NCH)
        VTK = work(512).rearrange("p (c f) -> p c f", c=NCH)
        WS = work(256).rearrange("p (h d f) -> p h d f", h=2, d=2)
        US = work(256).rearrange("p (h d f) -> p h d f", h=2, d=2)
        STR = work(128).rearrange("p (d f) -> p d f", d=2)
        PCT = work(8).rearrange("p (d c) -> p d c", d=2)
        PC = work(10)
        home = [H[:, :], BIG[:, 16384:20480]]
        GM1 = [home[e][:, 0:1024].rearrange("p (q n t) -> p q n t", q=4, n=2) for e in range(2)]
        GM2 = [home[e][:, 1024:2048].rearrange("p (q n t) -> p q n t", q=4, n=2) for e in range(2)]
        NB = [[home[e][:, 2048 + 512 * n:2560 + 512 * n] for n in range(4)] + [work(512), work(512)] for e in range(2)]
        flat = lambda ap: ap.rearrange("p q t -> p (q t)")
        quad = lambda ap: ap.rearrange("p (q t) -> p q t", q=4)
        IB = ((6, 7), (4, 5))
        END_R = (P - 1, 0)
        MIXES = (("r", 0), ("k", 2), ("v", 3))
        LORA = (("w", 1), ("a", 4), ("g", 5))
        LEVELS = ("lev8", "lev16", "lev32", "lev64")

        def rwkv_sp(l):
            j, t = l // 3, f"r{l}"
            for name, w in (("r", "rw_wr"), ("k", "rw_wk"), ("v", "rw_wv")):
                w = rows(a[w][j])
                with C.loop(sp, t + name, 4) as i:
                    for q in range(2):
                        load_unit(i, f"{t}.{name}{q}", unit(w, 0, 8, i * 256 + q * P))
            for name, w in (("w", "rw_w1"), ("a", "rw_a1")):
                load_unit(None, f"{t}.{name}",
                          (lambda slot: slot[:, :, 0:64], rows(a[w][j][0])), (lambda slot: slot[:, :, 64:P], rows(a[w][j][1])))
            load_unit(None, f"{t}.g", unit(rows(a["rw_g1"][j]), 0, 8, 0))
            enter(sp, (), f"n1{l}")
            w2 = a["rw_w2"][j].rearrange("d r n -> (d r) n")
            a2 = a["rw_a2"][j].rearrange("d r n -> (d r) n")
            with C.loop(sp, t + "ct", KD) as i:
                sp.wait_ge(pe_done, C.at(f"{t}.wa", i, 1))
                sp.sem_inc(loads_started, 1)
                sp.dma_start(W2S, w2[:, bass.ds(i * P, P)]).then_inc(side_loaded[3], C.mark(side_loaded[3], None, 16))
                sp.dma_start(A2S, a2[:, bass.ds(i * P, P)]).then_inc(
                    side_loaded[3], C.mark(side_loaded[3], f"{t}.s2", 16))
                sp.wait_ge(pe_done, C.at(f"{t}.post", i, 1))
                sp.sem_inc(loads_started, 1)
                sp.dma_start(G2S, a["rw_g2"][j][:, bass.ds(i * P, P)]).then_inc(
                    g2_loaded, C.mark(g2_loaded, f"{t}.g2", 16))
            proj_sp(f"mo{l}", a["rw_wo"][j], 1)

        def rwkv_pe(l, lo):
            t = f"r{l}"
            enter(pe, (pe_done, w_used), f"n1{l}")
            for name, m in MIXES:
                pe.wait_ge(vec_done, C.at(f"{t}.mix{m}"))
                with C.loop(pe, t + name, 4) as i:
                    for q in range(2):
                        pe.wait_ge(act_done, C.at(f"{t}.{name}e{q}", i, 1))
                        use_unit(i, f"{t}.{name}{q}", PS[:, q, :], lambda k: XM[:, k, :], 8, True, True)
            for n, (name, m) in enumerate(LORA):
                pe.wait_ge(vec_done, C.at(f"{t}.mix{m}"))
                use_unit(None, f"{t}.{name}", PS[:, 2 + n, :], lambda k: XM[:, k, :], 8, True, True)
            pe.wait_ge(act_done, C.at(f"{t}.ge"))

            def gram(i, c):
                e = c % 2
                pe.wait_ge(act_done, C.at(f"{t}.vt", i))
                if e:
                    pe.wait_ge(vec_done, C.at(f"{t}.gm{c - 1}", i))
                elif c:
                    pe.wait_ge(vec_done, C.at(f"{t}.y{c - 1}", i))
                for h in range(2):
                    hs = slice(64 * h, 64 * h + 64)
                    for d in range(2):
                        ch = ORDER[d][c]
                        cs, ds = slice(ch * P, (ch + 1) * P), slice(256 * d, 256 * d + 256)
                        pe.matmul(PS[:, h, ds], AD[hs, d, cs], AR[hs, d, :, cs], start=True, stop=True)
                        pe.matmul(PS[:, 2 + h, ds], SD[hs, d, cs], AR[hs, d, :, cs], start=True, stop=True)
                        mm = pe.matmul(PS[:, 4 + h, d * P:(d + 1) * P], AR[hs, d, 0, cs], AD[hs, d, cs], start=True,
                                       stop=True)
                mm.then_inc(pe_done, C.mark(pe_done, f"{t}.gr{c}"))

            def four(bank, lhs, rhs):
                for q in range(4):
                    qs = slice(q * P, (q + 1) * P)
                    mm = pe.matmul(PS[:, bank, qs], lhs(q), rhs(q), start=True, stop=True)
                return mm

            def inverse(i, pair):
                two = [(e, 2 * pair + e) for e in range(2)]
                b = lambda e, n: (lambda q: NB[e][n][:, q * P:(q + 1) * P])
                for e, c in two:
                    gram(i, c)
                for e, c in two:
                    pe.wait_ge(vec_done, C.at(f"{t}.gm{c}", i))
                    pe.wait_ge(pool_done, C.at(f"{t}.dt{c}", i))
                    four(IB[e][0], b(e, 1), b(e, 0))
                    four(IB[e][1], b(e, 0), b(e, 1)).then_inc(pe_done, C.mark(pe_done, f"{t}.d2{c}"))
                for e, c in two:
                    pe.wait_ge(vec_done, C.at(f"{t}.u2{c}", i))
                    pe.wait_ge(act_done, C.at(f"{t}.d2t{c}", i))
                    four(IB[e][0], b(e, 1), b(e, 4))
                    four(IB[e][1], b(e, 2), b(e, 3)).then_inc(pe_done, C.mark(pe_done, f"{t}.x1{c}"))
                for e, c in two:
                    pe.wait_ge(vec_done, C.at(f"{t}.x1v{c}", i))
                    pe.wait_ge(act_done, C.at(f"{t}.d4{c}", i))
                    four(IB[e][0], b(e, 3), b(e, 0)).then_inc(pe_done, C.mark(pe_done, f"{t}.x2{c}"))
                for n in range(4):
                    for e, c in two:
                        pe.wait_ge(vec_done, C.at(f"{t}.xv{n}{c}", i))
                        for q in range(4):
                            qs = slice(q * P, (q + 1) * P)
                            mm = pe.transpose(PS[:, IB[e][1], qs], NB[e][2 + n % 2][:, qs], const("ident"))
                        mm.then_inc(pe_done, C.mark(pe_done, f"{t}.tr{n}{c}"))
                        pe.wait_ge(pool_done, C.at(f"{t}.o{n}{c}", i))
                        four(IB[e][0], b(e, 5 - n % 2), b(e, 2 + n % 2)).then_inc(
                            pe_done, C.mark(pe_done, f"{t}.yy{n}{c}"))
                    for e, c in two:
                        pe.wait_ge(act_done, C.at(f"{t}.yv{n}{c}", i))
                        if n < 3:
                            mm = four(IB[e][0], b(e, 1), b(e, 0))
                        else:
                            mm = four(IB[e][0], b(e, 0), b(e, 1))
                        mm.then_inc(pe_done, C.mark(pe_done, f"{t}.xx{n}{c}"))

            def chain(i, c):
                e = c % 2
                g2 = lambda h, d, n: GM2[e][:, 2 * h + d, n, :]
                g1 = lambda h, d, n: GM1[e][:, 2 * h + d, n, :]
                pe.wait_ge(vec_done, C.at(f"{t}.y{c - 1}" if e else f"{t}.xf{c}", i))
                for h in range(2):
                    hs = slice(64 * h, 64 * h + 64)
                    for d in range(2):
                        ch = ORDER[d][c]
                        cs, o = slice(ch * P, (ch + 1) * P), PS[:, h, 64 * d:64 * d + 64]
                        if c:
                            pe.matmul(o, AR[hs, d, 0, cs], STR[hs, d, :], start=True, stop=False)
                        mm = pe.matmul(o, g2(h, d, 0), VTK[:, ch, hs], start=c == 0, stop=True)
                mm.then_inc(pe_done, C.mark(pe_done, f"{t}.w{c}"))
                pe.wait_ge(act_done, C.at(f"{t}.ws{c}", i))
                for h in range(2):
                    for d in range(2):
                        q = 2 * h + d
                        mm = pe.matmul(PS[:, 2, 64 * q:64 * q + 64], NB[e][1][:, q * P:(q + 1) * P], WS[:, h, d, :],
                                       start=True, stop=True)
                mm.then_inc(pe_done, C.mark(pe_done, f"{t}.u{c}"))
                pe.wait_ge(vec_done, C.at(f"{t}.us{c}", i))
                for h in range(2):
                    hs = slice(64 * h, 64 * h + 64)
                    for d in range(2):
                        ch = ORDER[d][c]
                        cs = slice(ch * P, (ch + 1) * P)
                        if c < NCH - 1:
                            o = PS[hs, 7, 64 * d:64 * d + 64]
                            pe.matmul(o, KBT[:, d, ch, hs], VTK[:, ch, hs], start=True, stop=False)
                            pe.matmul(o, BNT[:, d, ch, hs], US[:, h, d, :], start=False, stop=True)
                        o = PS[hs, (3, 6)[h], d * P:(d + 1) * P]
                        pe.matmul(o, VTK[:, ch, hs], g2(h, d, 1), start=True, stop=False)
                        if c:
                            pe.matmul(o, STR[hs, d, :], AR[hs, d, 1, cs], start=False, stop=False)
                        mm = pe.matmul(o, US[:, h, d, :], g1(h, d, 1), start=False, stop=True)
                mm.then_inc(pe_done, C.mark(pe_done, f"{t}.yp{c}"))

            with C.loop(pe, t + "ct", KD) as i:
                pe.wait_ge(side_loaded[3], C.at(f"{t}.s2", i))
                pe.wait_ge(vec_done, C.at(f"{t}.out", i, 1))
                for d in range(2):
                    ds = slice(64 * d, 64 * d + 64)
                    pe.matmul(PS[:, d, :], W2S[ds, :], TH[ds, :], start=True, stop=True)
                    mm = pe.matmul(PS[:, 2 + d, :], A2S[ds, :], AL[ds, :], start=True, stop=True)
                mm.then_inc(pe_done, C.mark(pe_done, f"{t}.wa"))
                pe.wait_ge(act_done, C.at(f"{t}.kk2", i))
                pe.matmul(PS[:, 4, :], const("blk"), KK, start=True, stop=True).then_inc(
                    pe_done, C.mark(pe_done, f"{t}.kks"))
                pe.wait_ge(act_done, C.at(f"{t}.sg", i))
                pe.wait_ge(vec_done, C.at(f"{t}.prod", i))
                pe.matmul(PS[:, 5, :], const("blk"), BS, start=True, stop=True).then_inc(
                    pe_done, C.mark(pe_done, f"{t}.bs"))
                for n, src in enumerate((SD[:, 0], SD[:, 1], AD[:, 0], AD[:, 1], YT)):
                    for c in range(NCH):
                        mm = pe.transpose(PS[:, (0, 1, 2, 3, 6)[n], c * P:(c + 1) * P], src[:, c * P:(c + 1) * P],
                                          const("ident"))
                    mm.then_inc(pe_done, C.mark(pe_done, f"{t}.t{n}"))
                pe.wait_ge(vec_done, C.at(f"{t}.bv", i))
                for pair in range(2):
                    inverse(i, pair)
                    chain(i, 2 * pair)
                    chain(i, 2 * pair + 1)
                pe.wait_ge(vec_done, C.at(f"{t}.y3", i))
                pe.matmul(PS[:, 0, :], const("cent"), YT, start=True, stop=True).then_inc(
                    pe_done, C.mark(pe_done, f"{t}.ce"))
                pe.wait_ge(g2_loaded, C.at(f"{t}.g2", i))
                pe.matmul(PS[:, 2, :], G2S, GS, start=True, stop=True)
                pe.wait_ge(act_done, C.at(f"{t}.ysq", i))
                pe.matmul(PS[:, 1, :], const("blkmean"), PN[:, 0, :], start=True, stop=True).then_inc(
                    pe_done, C.mark(pe_done, f"{t}.post"))
            pe.wait_ge(vec_done, C.at(f"{t}.out"))
            proj_pe(f"mo{l}", lambda k: XM[:, k, lo:T], 1, lo)
            leave((pe_done, w_used), f"mix{l}")

        def rwkv_act(l, lo):
            t = f"r{l}"
            enter(act, (act_done,), f"n1{l}")
            for n, (name, m) in enumerate(MIXES):
                with C.loop(act, t + name, 4) as i:
                    for q in range(2):
                        act.wait_ge(w_used, C.at(f"{t}.{name}{q}.used", i))
                        s(act.activation(RKV[:, n, i * 2 + q, :], PS[:, q, :], ACT.Copy), f"{t}.{name}e{q}", i)
            for n, (dst, func) in enumerate(((TH, ACT.Tanh), (AL, ACT.Copy), (GS, ACT.Sigmoid))):
                name = LORA[n][0]
                act.wait_ge(w_used, C.at(f"{t}.{name}.used"))
                s(act.activation(dst, PS[:, 2 + n, :], func), f"{t}.{name}e")

            def inverse(i, pair):
                two = [(e, 2 * pair + e) for e in range(2)]
                cp = lambda e, n, k, label: s(act.activation(NB[e][n], PS[:, IB[e][k], :], ACT.Copy), label, i)
                for e, c in two:
                    act.wait_ge(pe_done, C.at(f"{t}.d2{c}", i))
                    cp(e, 3, 1, f"{t}.d2t{c}")
                for e, c in two:
                    act.wait_ge(pe_done, C.at(f"{t}.x1{c}", i))
                    cp(e, 3, 1, f"{t}.d4{c}")
                for n in range(4):
                    for e, c in two:
                        act.wait_ge(pe_done, C.at(f"{t}.tr{n}{c}", i))
                        cp(e, 1, 1, f"{t}.xt{n}{c}")
                        act.wait_ge(pe_done, C.at(f"{t}.yy{n}{c}", i))
                        cp(e, 0, 0, f"{t}.yv{n}{c}")

            def chain(i, c):
                act.wait_ge(pe_done, C.at(f"{t}.w{c}", i))
                s(act.activation(WS[:, :, :, :].rearrange("p h d f -> p h (d f)"), PS[:, 0:2, 0:P], ACT.Copy),
                  f"{t}.ws{c}", i)

            with C.loop(act, t + "ct", KD) as i:
                act.wait_ge(vec_done, C.at(f"{t}.kf", i))
                s(act.activation(YT, RKV[:, 2, i, :], ACT.Copy), None, i)
                s(act.activation(KK, KF, ACT.Square), f"{t}.kk2", i)
                act.wait_ge(pe_done, C.at(f"{t}.wa", i))
                for d in range(2):
                    s(act.activation(SD[:, d, :], PS[:, d, :], ACT.Sigmoid, bias=PC[:, d:d + 1]), f"{t}.s{d}", i)
                    s(act.activation(AD[:, d, :], PS[:, 2 + d, :], ACT.Sigmoid, bias=PC[:, 2 + d:3 + d]),
                      f"{t}.sg" if d else None, i)
                act.wait_ge(pe_done, C.at(f"{t}.kks", i))
                s(act.activation(KK, PS[:, 4, :], ACT.Ln, bias=MC[:, 4:5]), None, i)
                s(act.activation(KK, KK, ACT.Exp, scale=-0.5), f"{t}.rn", i)
                act.wait_ge(vec_done, C.at(f"{t}.sums", i))
                s(act.activation(PN[:, :, :], AR[:, :, 1, :], ACT.Exp, scale=LOG_W, bias=MC[:, 3:4]), None, i)
                for d in range(2):
                    ends = AR[:, d, 1, :].rearrange("p (c t) -> p c t", c=NCH)[:, :, END_R[d]]
                    s(act.activation(PCT[:, d, :], ends, ACT.Exp, scale=-LOG_W), None, i)
                s(act.activation(AR[:, :, 1, :], AR[:, :, 1, :], ACT.Exp, scale=-LOG_W, bias=MC[:, 2:3]), None, i)
                s(act.activation(AR[:, :, 0, :], AR[:, :, 0, :], ACT.Exp, scale=-LOG_W, bias=MC[:, 2:3]),
                  f"{t}.dec", i)
                for n, dst in enumerate((KBT[:, 0], KBT[:, 1], BNT[:, 0], BNT[:, 1], VTK)):
                    act.wait_ge(pe_done, C.at(f"{t}.t{n}", i))
                    s(act.activation(dst.rearrange("p c f -> p (c f)") if n < 4 else
                                     VTK[:, :, :].rearrange("p c f -> p (c f)"), PS[:, (0, 1, 2, 3, 6)[n], :],
                                     ACT.Copy), f"{t}.vt" if n == 4 else None, i)
                for pair in range(2):
                    inverse(i, pair)
                    chain(i, 2 * pair)
                    chain(i, 2 * pair + 1)
                act.wait_ge(pe_done, C.at(f"{t}.ce", i))
                s(act.activation(PN[:, 0, :], PS[:, 0, :], ACT.Square), f"{t}.ysq", i)
                act.wait_ge(pe_done, C.at(f"{t}.post", i))
                s(act.activation(PN[:, 1, :], PS[:, 1, :], ACT.Ln, bias=MC[:, 1:2]), None, i)
                s(act.activation(PN[:, 1, :], PN[:, 1, :], ACT.Exp, scale=-0.5), f"{t}.ry", i)
            leave((act_done,), f"mix{l}")

        def rwkv_pool(l):
            t = f"r{l}"
            with C.loop(pool, t + "ct", KD) as i:
                for pair in range(2):
                    two = [(e, 2 * pair + e) for e in range(2)]

                    def mt(e, dst, mask, label):
                        g(pool.tensor_tensor(quad(dst), GM1[e][:, :, 0, :],
                                             const(mask).unsqueeze(1).broadcast_to([P, 4, P]), ALU.mult), label, i)
                    for e, c in two:
                        pool.wait_ge(vec_done, C.at(f"{t}.gm{c}", i))
                        mt(e, NB[e][1], "mask8", f"{t}.dt{c}")
                    for e, c in two:
                        mt(e, NB[e][5], LEVELS[0], f"{t}.o0{c}")
                    for n in range(1, 4):
                        for e, c in two:
                            pool.wait_ge(pe_done, C.at(f"{t}.x1{c}" if n == 1 else f"{t}.yy{n - 2}{c}", i))
                            if n == 1:
                                pool.wait_ge(vec_done, C.at(f"{t}.x1v{c}", i))
                            mt(e, NB[e][5 - n % 2], LEVELS[n], f"{t}.o{n}{c}")
            leave((pool_done,), f"mix{l}")

        def rwkv_vec(l, lo):
            j, t = l // 3, f"r{l}"
            B = B_RW + j
            enter(vec, (vec_done,), f"n1{l}")
            h2 = H[:, :].rearrange("p (n t) -> p n t", t=SEG)
            d2 = BIG[:, 16384:20480].rearrange("p (n t) -> p n t", t=SEG)
            v(vec.tensor_tensor(d2[:, :, 1:SEG - 1], h2[:, :, 0:SEG - 2], h2[:, :, 2:SEG], ALU.add))
            v(vec.tensor_copy(d2[:, :, 0:1], h2[:, :, 1:2]))
            v(vec.tensor_copy(d2[:, :, SEG - 1:SEG], h2[:, :, SEG - 2:SEG - 1]))
            v(vec.scalar_tensor_tensor(d2[:, :, :], d2[:, :, :], 0.5, h2[:, :, :], ALU.mult, ALU.subtract))
            last = None
            for name, m in MIXES + LORA:
                if last:
                    vec.wait_ge(w_used, C.at(last))
                for k in range(KD):
                    v(vec.scalar_tensor_tensor(XM[:, k, :], DX[:, k, :], PV[:, B, 8 * m + k:8 * m + k + 1], Hk[:, k, :],
                                               ALU.mult, ALU.add), f"{t}.mix{m}" if k == KD - 1 else None)
                last = f"{t}.{name}1.used" if (name, m) in MIXES else f"{t}.{name}.used"
            vec.wait_ge(act_done, C.at(f"{t}.ge"))
            vec.wait_ge(w_used, C.at(last))
            both = lambda ap: ap.unsqueeze(1).broadcast_to([P, 2, T])

            def inverse(i, pair):
                two = [(e, 2 * pair + e) for e in range(2)]
                bank = lambda e, k: PS[:, IB[e][k], :]
                for e, c in two:
                    vec.wait_ge(pe_done, C.at(f"{t}.gr{c}", i))
                    for h in range(2):
                        hq = slice(2 * h, 2 * h + 2)
                        v(vec.tensor_tensor(GM1[e][:, hq].rearrange("p q n t -> p (q n t)"), PS[:, h, :],
                                            const("gs0", 4), ALU.mult), None, i)
                        v(vec.tensor_tensor(NB[e][0][:, 256 * h:256 * h + 256], PS[:, 4 + h, 0:256], const("gt0", 2),
                                            ALU.mult), None, i)
                    for h in range(2):
                        hq = slice(2 * h, 2 * h + 2)
                        v(vec.tensor_tensor(GM2[e][:, hq].rearrange("p q n t -> p (q n t)"), PS[:, 2 + h, :],
                                            const("gs0", 4), ALU.mult), f"{t}.gm{c}" if h else None, i)
                for e, c in two:
                    vec.wait_ge(pe_done, C.at(f"{t}.d2{c}", i))
                    v(vec.tensor_copy(NB[e][2], bank(e, 0)), None, i)
                    v(vec.tensor_tensor(quad(NB[e][4]), quad(NB[e][2]),
                                        const("ident").unsqueeze(1).broadcast_to([P, 4, P]), ALU.add),
                      f"{t}.u2{c}", i)
                for e, c in two:
                    vec.wait_ge(pe_done, C.at(f"{t}.x1{c}", i))
                    v(vec.tensor_tensor(NB[e][0], bank(e, 0), NB[e][4], ALU.add), f"{t}.x1v{c}", i)
                for e, c in two:
                    vec.wait_ge(pe_done, C.at(f"{t}.x2{c}", i))
                    v(vec.tensor_tensor(NB[e][2], bank(e, 0), NB[e][0], ALU.add), f"{t}.xv0{c}", i)
                for n in range(3):
                    for e, c in two:
                        vec.wait_ge(pe_done, C.at(f"{t}.xx{n}{c}", i))
                        v(vec.tensor_tensor(NB[e][2 + (n + 1) % 2], bank(e, 0), NB[e][2 + n % 2], ALU.add),
                          f"{t}.xv{n + 1}{c}", i)
                for e, c in two:
                    vec.wait_ge(pe_done, C.at(f"{t}.xx3{c}", i))
                    v(vec.tensor_tensor(NB[e][1], bank(e, 0), NB[e][1], ALU.add), f"{t}.xf{c}", i)

            def chain(i, c):
                vec.wait_ge(pe_done, C.at(f"{t}.u{c}", i))
                v(vec.tensor_copy(US[:, :, :, :].rearrange("p h d f -> p (h d f)"), PS[:, 2, 0:256]), f"{t}.us{c}", i)
                vec.wait_ge(pe_done, C.at(f"{t}.yp{c}", i))
                if c < NCH - 1:
                    s7 = PS[:, 7, 0:P].rearrange("p (d f) -> p d f", d=2)
                    if c:
                        v(vec.tensor_tensor(STR[:, :, :], STR[:, :, :], s7, ALU.add), None, i)
                    for d in range(2):
                        ch = ORDER[d][c]
                        v(vec.tensor_scalar(STR[:, d, :], STR[:, d, :] if c else s7[:, d, :], PCT[:, d, ch:ch + 1],
                                            None, ALU.mult), None, i)
                for h in range(2):
                    hs = slice(64 * h, 64 * h + 64)
                    for d in range(2):
                        ch = ORDER[d][c]
                        y, ps = YT[hs, ch * P:(ch + 1) * P], PS[hs, (3, 6)[h], d * P:(d + 1) * P]
                        label = f"{t}.y{c}" if (h, d) == (1, 1) else None
                        if c % 2 == 0:
                            v(vec.tensor_copy(y, ps), label, i)
                        else:
                            v(vec.tensor_tensor(y, y, ps, ALU.add), label, i)

            with C.loop(vec, t + "ct", KD) as i:
                v(vec.tensor_copy(PC[:, 0:9], PV[:, B, 48:120].rearrange("p (n c) -> p n c", c=8)[:, :, i]), None, i)
                v(vec.tensor_scalar(PC[:, 9:10], PC[:, 5:6], -1.0, 1.0, ALU.mult, ALU.add), None, i)
                v(vec.tensor_scalar(KF, RKV[:, 1, i, :], PC[:, 4:5], None, ALU.mult), f"{t}.kf", i)
                for d in range(2):
                    vec.wait_ge(act_done, C.at(f"{t}.s{d}", i))
                    for c in range(NCH):
                        cs = slice(c * P, (c + 1) * P)
                        v(vec.tensor_tensor_scan(AR[:, d, 1, cs], const("ones"), SD[:, d, cs], 0.0, ALU.mult, ALU.add),
                          None, i)
                v(vec.tensor_tensor(AR[:, 0, 0, :], AR[:, 0, 1, :], SD[:, 0, :], ALU.subtract), None, i)
                c4 = lambda ap: ap.rearrange("p (c t) -> p c t", c=NCH)
                v(vec.tensor_tensor(c4(AR[:, 1, 0, :]), c4(AR[:, 1, 1, :])[:, :, P - 1:P].broadcast_to([P, NCH, P]),
                                    c4(AR[:, 1, 1, :]), ALU.subtract), None, i)
                v(vec.tensor_tensor(AR[:, 1, 1, :], AR[:, 1, 0, :], SD[:, 1, :], ALU.add), f"{t}.sums", i)
                vec.wait_ge(act_done, C.at(f"{t}.rn", i))
                v(vec.tensor_tensor(KK, KK, KF, ALU.mult), None, i)
                v(vec.tensor_scalar(SD[:, :, :], AD[:, :, :], PC[:, 5:6], PC[:, 9:10], ALU.mult, ALU.add), None, i)
                v(vec.tensor_tensor(SD[:, :, :], SD[:, :, :], both(RKV[:, 1, i, :]), ALU.mult), None, i)
                v(vec.tensor_tensor(BS, SD[:, 0, :], SD[:, 1, :], ALU.add), None, i)
                v(vec.scalar_tensor_tensor(BS, BS, PC[:, 6:7], RKV[:, 0, i, :], ALU.mult, ALU.mult), None, i)
                v(vec.tensor_tensor(AD[:, :, :], AD[:, :, :], both(KK), ALU.mult), None, i)
                vec.wait_ge(act_done, C.at(f"{t}.dec", i))
                v(vec.scalar_tensor_tensor(AD[:, :, :], AD[:, :, :], -1.0, PN[:, :, :], ALU.mult, ALU.mult), None, i)
                v(vec.tensor_tensor(SD[:, :, :], SD[:, :, :], PN[:, :, :], ALU.mult), None, i)
                v(vec.tensor_tensor(AR[:, :, 0, :], AR[:, :, 0, :], both(KK), ALU.mult), None, i)
                v(vec.tensor_tensor(AR[:, :, 1, :], AR[:, :, 1, :], both(RKV[:, 0, i, :]), ALU.mult), f"{t}.prod", i)
                vec.wait_ge(pe_done, C.at(f"{t}.bs", i))
                v(vec.tensor_tensor(BV, RKV[:, 2, i, :], PS[:, 5, :], ALU.mult), f"{t}.bv", i)
                for pair in range(2):
                    inverse(i, pair)
                    chain(i, 2 * pair)
                    chain(i, 2 * pair + 1)
                vec.wait_ge(act_done, C.at(f"{t}.ry", i))
                v(vec.tensor_tensor(YT, PN[:, 1, :], PS[:, 0, :], ALU.mult), None, i)
                v(vec.tensor_scalar(YT, YT, PC[:, 7:8], PC[:, 8:9], ALU.mult, ALU.add), None, i)
                v(vec.tensor_tensor(YT, YT, BV, ALU.add), None, i)
                v(vec.tensor_tensor(XM[:, i, :], YT, PS[:, 2, :], ALU.mult), f"{t}.out", i)
            proj_vec(f"mo{l}", l, 1, lo)
            leave((vec_done,), f"mix{l}")

        MIX = {}
        MIX[2] = {'sp': attn_sp, 'pe': attn_pe, 'act': attn_act, 'vec': attn_vec, 'pool': attn_pool}
        MIX[1] = {'sp': ssd_sp, 'pe': ssd_pe, 'act': ssd_act, 'vec': ssd_vec, 'pool': ssd_pool}
        MIX[0] = MIX[3] = {'sp': rwkv_sp, 'pe': rwkv_pe, 'act': rwkv_act, 'vec': rwkv_vec, 'pool': rwkv_pool}
        MIX = {n: m for n, m in MIX.items() if n in only}


        block = ctx.enter_context(nc.Block())
        kinds = ["rwkv", "ssd", "attn", "rwkv"]

        def los(l):
            return SEG if l == DEPTH - 1 else 0

        def before(l):
            return "ada" if l == list(layers)[0] else f"ffn{l - 1}"

        @block.sync
        def _(sp):
            start_sp()
            ada_sp()
            for l in layers:
                if mixers and l in MIX:
                    MIX[l]["sp"](l)
                ffn_sp(l)
            end_sp()

        @block.gpsimd
        def _(pool):
            for l in layers:
                if mixers and l in MIX and "pool" in MIX[l]:
                    MIX[l]["pool"](l)

        @block.tensor
        def _(pe):
            start_pe()
            ada_pe()
            for l in layers:
                if mixers and l in MIX:
                    norm_pe(f"n1{l}", before(l), 0)
                    MIX[l]["pe"](l, los(l))
                norm_pe(f"n2{l}", f"mix{l}" if mixers and l in MIX else before(l), los(l))
                ffn_pe(l, los(l))
            norm_pe("nf", f"ffn{list(layers)[-1]}", SEG)
            end_pe("nf")

        @block.scalar
        def _(act):
            start_act()
            for l in layers:
                if mixers and l in MIX:
                    norm_act(f"n1{l}", before(l), 0, 2 * l, mod_shift(l, 0))
                    MIX[l]["act"](l, los(l))
                norm_act(f"n2{l}", f"mix{l}" if mixers and l in MIX else before(l), los(l), 2 * l + 1, mod_shift(l, 1))
                ffn_act(l, los(l))
            norm_act("nf", f"ffn{list(layers)[-1]}", SEG, 2 * DEPTH, lambda k, n: MS[:, 2 * DEPTH, k, 0:1])
            end_act("nf")

        @block.vector
        def _(vec):
            start_vec()
            ada_vec()
            for l in layers:
                if mixers and l in MIX:
                    norm_vec(f"n1{l}", before(l), 0)
                    MIX[l]["vec"](l, los(l))
                norm_vec(f"n2{l}", f"mix{l}" if mixers and l in MIX else before(l), los(l))
                ffn_vec(l, los(l))
            norm_vec("nf", f"ffn{list(layers)[-1]}", SEG)
    return C


_INS = ['x', 'c', 'ctx', 'c_ctx', 'ada_w', 'ada_b', 'norm1_g', 'norm2_g', 'ffn_w_in', 'ffn_conv', 'ffn_w_out',
        'final_g', 'rw_mu', 'rw_wr', 'rw_wk', 'rw_wv', 'rw_wo', 'rw_w0', 'rw_w1', 'rw_w2', 'rw_a0', 'rw_a1', 'rw_a2',
        'rw_g1', 'rw_g2', 'rw_kk', 'rw_ka', 'rw_rk', 'rw_ln_g', 'rw_ln_b', 'ssd_w_in', 'ssd_conv_w', 'ssd_conv_b',
        'ssd_dt_bias', 'ssd_a_log', 'ssd_d', 'ssd_norm_g', 'ssd_w_out', 'at_w_qkv', 'at_w_o', 'at_sink']


def shape_constants():
    import numpy as np
    f = np.float32
    r, c = np.arange(P)[:, None], np.arange(P)[None, :]
    same = lambda n: (r // n == c // n).astype(f)
    level = lambda n: ((r // (2 * n) == c // (2 * n)) & (r // n != c // n)).astype(f)
    m = {"ident": np.eye(P, dtype=f), "mean": np.full((P, P), 1.0 / D, f), "blk": same(64),
         "cent": np.eye(P, dtype=f) - same(64) / 64, "blkmean": same(64) / 64, "ones": np.ones((P, P), f),
         "mean256": np.full((P, P), 1.0 / 256, f),
         "mask8": same(8), "lev8": level(8), "lev16": level(16), "lev32": level(32), "lev64": level(64),
         "gs0": (r < c).astype(f), "gi0": (r <= c).astype(f), "gs1": (r > c).astype(f), "gi1": (r >= c).astype(f),
         "gt0": (r > c) * same(8), "gt1": (r < c) * same(8)}
    consts = np.concatenate([m[n] for n in CONST], 1)

    inv = (f(10000.0) ** (-np.arange(0, 32, 2, dtype=f) / f(32))).astype(f)
    tok = np.arange(SEQ)
    p = np.arange(P)
    pos = np.where((p % 64)[:, None] < 32, (tok // 64)[None, :], (tok % 64)[None, :]).astype(f)
    ang = (pos * inv[p % 16][:, None]).astype(f)
    cos, sin = np.cos(ang).astype(f), np.sin(ang).astype(f)
    rot = np.zeros((P, P), f)
    for q in range(P):
        if q % 32 < 16:
            rot[q + 16, q] = -1.0
        else:
            rot[q - 16, q] = 1.0
    dup = [np.zeros((P, P), f) for _ in range(2)]
    for h in range(2):
        for q in range(P):
            dup[h][64 * h + q % 64, q] = 1.0
    am = []
    for b in range(2):
        q = b * P + np.arange(P)[:, None]
        k = np.arange(SEQ)[None, :]
        am.append(np.where(np.abs(q - k) <= 128, f(0), f(NEG)))
    attn = np.concatenate([cos, sin, rot, dup[0], dup[1], rot @ dup[0], rot @ dup[1], am[0], am[1]], 1).astype(f)
    return consts, attn, dup, rot


def kernel(**inputs):
    import numpy as _np
    import concourse.bacc as _bacc
    from concourse import mybir as _mybir
    from concourse.bass_utils import run_bass_kernel_spmd as _run

    consts, attn, _, _ = shape_constants()
    extra = {"consts": consts, "attn_consts": attn}

    def build(draft):
        nc = _bacc.Bacc("TRN2", target_bir_lowering=False, num_devices=1)
        arrays, args = {}, {}
        for name in _INS + list(extra):
            arr = _np.ascontiguousarray(extra[name] if name in extra else inputs[name])
            arrays[f"in_{name}_dram"] = arr
            args[name] = nc.dram_tensor(f"in_{name}_dram", arr.shape, _mybir.dt.from_np(arr.dtype),
                                        kind="ExternalInput").ap()
        out = nc.dram_tensor("out_0_dram", (1, SEQ, D), F32, kind="ExternalOutput").ap()
        scratch = nc.dram_tensor("scratch_dram", (64, T), F32, kind="Internal").ap()
        counts = program(nc, args, out, draft, scratch, **OPTIONS)
        return nc, arrays, counts

    _, _, draft = build(None)
    nc, arrays, _ = build(draft)
    r = _run(nc, [arrays], core_ids=[0])
    return r.results[0]["out_0_dram"]


OPTIONS = {}
```

```python
from contextlib import ExitStack, contextmanager

import concourse.bass as bass
from concourse import mybir

P = 128
D = 1024
KD = D // P
CTX = 256
SEQ = 256
T = CTX + SEQ
SEG = 256
NCH = T // P
DEPTH = 4
F = 2816
NF = F // P
NMOD = 6 * D // P
EPS = 1e-6
WORK_N = 18272
GN_EPS = 64e-5
KK_EPS = 1e-12
LEAD = 256
LOG_W = 0.6065306597126334
MID = 38.8
HEADS = 16
SSD_IN = 6208
INNER = 2048
NEG = -1.0e30
ORDER = [[0, 1, 2, 3], [1, 0, 3, 2]]

F32 = mybir.dt.float32
ACT = mybir.ActivationFunctionType
ALU = mybir.AluOpType
AX_X = mybir.AxisListType.X

CONST = ["ident", "mean", "blk", "cent", "blkmean", "ones", "mask8", "lev8", "lev16", "lev32", "lev64",
         "gs0", "gi0", "gs1", "gi1", "gt0", "gt1", "mean256"]
ATTN_CONST = ["cos0", "cos1", "sin0", "sin1", "rot", "dup0", "dup1", "duprot0", "duprot1",
              "am00", "am01", "am10", "am11"]


class Counts:

    def __init__(self, draft=None):
        self.draft = draft
        self.now, self.marks, self.loops, self.ends, self.loop_name = {}, {}, {}, {}, None

    def mark(self, sem, label, n=1):
        name = getname(sem)
        self.now[name] = self.now.get(name, 0) + n
        assert label is None or label not in self.marks, label
        if label is not None:
            self.marks[label] = (name, self.now[name], self.loop_name)
        return n

    def at(self, label, i=None, back=0):
        if self.draft is None:
            return 1
        name, value, loop = self.draft.marks[label]
        if loop is None:
            return value
        step, trips = self.draft.loops[loop][name]
        if i is None:
            return value + (trips - 1) * step
        value -= back * step
        assert value >= 1, (label, value)
        return i * step + value

    def here(self, sem, i=None):
        name = getname(sem)
        value = self.now.get(name, 0)
        if self.draft is None:
            return 1
        if self.loop_name is None:
            return value
        step, _ = self.draft.loops[self.loop_name][name]
        return i * step + value

    def end(self, sem, stage):
        self.ends[(getname(sem), stage)] = self.now.get(getname(sem), 0)

    def ended(self, sem, stage):
        return 1 if self.draft is None else self.draft.ends.get((getname(sem), stage), 0)

    @contextmanager
    def loop(self, eng, name, trips):
        before = dict(self.now)
        self.loop_name = name
        with eng.Fori(0, trips) as i:
            yield i
        self.loop_name = None
        for sem, v in list(self.now.items()):
            step = v - before.get(sem, 0)
            if step:
                self.loops.setdefault(name, {})[sem] = (step, trips)
                self.now[sem] = before.get(sem, 0) + trips * step


def getname(sem):
    return sem if isinstance(sem, str) else sem.name


def program(nc, a, out, draft, scratch, layers=range(DEPTH), mixers=True, only=range(DEPTH)):
    C = Counts(draft)
    ctx = ExitStack()
    with ctx:
        def sb(name, *shape):
            return ctx.enter_context(nc.sbuf_tensor(name, [P, *shape], F32))

        def sem(name):
            return ctx.enter_context(nc.semaphore(name))

        PS = ctx.enter_context(nc.psum_tensor("PS", [P, 8, 512], F32))
        X = sb("X", KD, T)
        H = sb("H", KD * T)
        Hk = H[:, :].rearrange("p (k t) -> p k t", k=KD)
        WR = sb("WR", 2, 8, P)
        BIG = sb("BIG", 20480)
        WORK = sb("WORK", WORK_N)
        K = sb("K", len(CONST) * P)
        PV = sb("PV", 1200)
        MOD = sb("MOD", DEPTH, NMOD, 2)
        MS = sb("MS", 2 * DEPTH + 1, KD, 2)
        MC = sb("MC", 5)
        SC = sb("SC", KD, 2)
        SEGS = (slice(0, SEG), slice(SEG, T))

        def const(name, n=1):
            c = CONST.index(name)
            return K[:, c * P:(c + n) * P]

        pe_done = sem("pe_done")
        w_used = sem("w_used")
        act_done = sem("act_done")
        vec_done = sem("vec_done")
        pool_done = sem("pool_done")
        w_loaded = [sem("w_loaded0"), sem("w_loaded1")]
        ada_loaded = [sem(f"ada_loaded{s}") for s in range(3)]
        ride_loaded = [sem(f"ride_loaded{s}") for s in range(4)]
        in_loaded = sem("in_loaded")
        vec_loaded = sem("vec_loaded")
        side_loaded = [sem(f"side_loaded{s}") for s in range(4)]
        stored = sem("stored")
        scratch_stored = sem("scratch_stored")
        g2_loaded = sem("g2_loaded")
        loads_started = sem("loads_started")
        staged = sem("staged")
        w2_used = sem("w2_used")
        PROGRESS = (pe_done, w_used, act_done, vec_done, pool_done)

        pe, act, vec, pool, sp = nc.tensor, nc.scalar, nc.vector, nc.gpsimd, nc.sync

        def enter(eng, own, stage):
            for s in PROGRESS:
                if s not in own and C.ended(s, stage) > 0:
                    eng.wait_ge(s, C.ended(s, stage))

        def leave(own, stage):
            for s in own:
                C.end(s, stage)

        def v(ins, label=None, i=None):
            ins.then_inc(vec_done, C.mark(vec_done, label))
            vec.wait_ge(vec_done, C.here(vec_done, i))

        def s(ins, label=None, i=None):
            ins.then_inc(act_done, C.mark(act_done, label))
            act.wait_ge(act_done, C.here(act_done, i))

        def g(ins, label=None, i=None):
            ins.then_inc(pool_done, C.mark(pool_done, label))
            pool.wait_ge(pool_done, C.here(pool_done, i))

        def load_unit(i, label, *parts):
            slot = C.now.get("unit", 0) % 2
            sp.wait_ge(w_used, C.here("unit", i) + 1)
            sp.sem_inc(loads_started, 1)
            C.mark("unit", None)
            for n, (dst, src) in enumerate(parts):
                last = n == len(parts) - 1
                sp.dma_start(dst(WR[:, slot]), src).then_inc(
                    w_loaded[slot], C.mark(w_loaded[slot], label if last else None, 16))

        def rows(w):
            return w.rearrange("(k p) n -> p k n", p=P)

        def unit(w, k0, nk, c0, nc_=P):
            return (lambda slot: slot[:, 0:nk, 0:nc_], w[:, k0:k0 + nk, bass.ds(c0, nc_)])

        def use_unit(i, label, outs, rhs, nk, first, last, m=P):
            slot = C.now.get("w_unit_pe", 0) % 2
            C.mark("w_unit_pe", None)
            pe.wait_ge(w_loaded[slot], C.at(label, i))
            for k in range(nk):
                mm = pe.matmul(outs, WR[:, slot, k, 0:m], rhs(k), start=first and k == 0, stop=last and k == nk - 1)
            mm.then_inc(w_used, C.mark(w_used, label + ".used"))

        ST = BIG[:, 0:17 * P].rearrange("p (b c) -> p b c", c=P)
        XIN = BIG[:, 4096:8192].rearrange("p (c d) -> p c d", d=D)

        flat1 = lambda ap: ap.rearrange("(r c) -> r c", c=P)
        flat2 = lambda ap: ap.rearrange("a (r c) -> (a r) c", c=P)
        blocks = []
        for l in range(DEPTH):
            blocks.append([flat1(a["ada_b"][l]), flat1(a["norm1_g"][l]), flat1(a["norm2_g"][l])]
                          + ([flat1(a["final_g"])] if l == 0 else []))
            conv = flat2(a["ffn_conv"][l])
            blocks += [[conv[0:66]], [conv[66:132]]]
        for j in range(2):
            blocks.append([flat2(a["rw_mu"][j]), flat2(a["rw_w0"][j]), flat2(a["rw_a0"][j]), flat1(a["rw_kk"][j]),
                           flat1(a["rw_ka"][j]), flat1(a["rw_rk"][j].rearrange("h n -> (h n)")),
                           flat1(a["rw_ln_g"][j]), flat1(a["rw_ln_b"][j])])
        blocks.append([flat2(a["ssd_conv_w"][0]), flat1(a["ssd_conv_b"][0])])
        blocks.append([flat1(a["ssd_norm_g"][0])])
        blocks.append([flat1(a["c_ctx"]), flat1(a["c"][0])])
        B_RW, B_SSD, B_SSDN, B_C = 12, 14, 15, 16
        nrows = [sum(x.shape[0] for x in b) for b in blocks]
        first_column = [sum(nrows[:b]) for b in range(len(blocks) + 1)]
        assert first_column[-1] <= 1200

        def columns(b, c0, n):
            return PV[:, bass.ds(c0 + first_column[b], n)]

        def start_sp():
            sp.dma_start(K[:, :], a["consts"]).then_inc(vec_loaded, C.mark(vec_loaded, "consts", 16))
            for b, parts in enumerate(blocks):
                r = 0
                for n, part in enumerate(parts):
                    sp.dma_start(ST[r:r + part.shape[0], b, :], part).then_inc(
                        vec_loaded, C.mark(vec_loaded, "params" if (b, n) == (16, len(parts) - 1) else None, 16))
                    r += part.shape[0]
            sp.dma_start(XIN[:, 0:2, :], a["ctx"][0].rearrange("(c p) d -> p c d", p=P)).then_inc(
                in_loaded, C.mark(in_loaded, None, 16))
            sp.dma_start(XIN[:, 2:4, :], a["x"][0].rearrange("(c p) d -> p c d", p=P)).then_inc(
                in_loaded, C.mark(in_loaded, "inputs", 16))

        def start_pe():
            pe.wait_ge(vec_loaded, C.at("params"))
            for b in range(17):
                mm = pe.transpose(PS[:, b // 4, (b % 4) * P:(b % 4) * P + nrows[b]], ST[0:nrows[b], b, :],
                                  const("ident")[0:nrows[b], 0:nrows[b]])
                if b == 0:
                    mm.then_inc(w_used, C.mark(w_used, None, 2))
                else:
                    mm.then_inc(pe_done, C.mark(pe_done, f"par{b}", LEAD if b == 1 else 1))
            pe.wait_ge(in_loaded, C.at("inputs"))
            for k in range(KD):
                bank = 5 + k % 3
                if k >= 3:
                    pe.wait_ge(act_done, C.at(f"x{k - 3}"))
                for c in range(NCH):
                    mm = pe.transpose(PS[:, bank, c * P:(c + 1) * P], XIN[:, c, k * P:(k + 1) * P], const("ident"))
                mm.then_inc(pe_done, C.mark(pe_done, f"xt{k}"))
            leave((pe_done, w_used), "start")

        def start_act():
            act.wait_ge(pe_done, C.at("par16"))
            act.wait_ge(vec_done, C.at("columns"))
            act.activation(SC[:, :, 0], columns(B_C, 0, KD), ACT.Silu).then_inc(act_done, C.mark(act_done, None, LEAD))
            s(act.activation(SC[:, :, 1], columns(B_C, KD, KD), ACT.Silu), "silu_c")
            for k in range(KD):
                act.wait_ge(pe_done, C.at(f"xt{k}"))
                s(act.activation(X[:, k, :], PS[:, 5 + k % 3, :], ACT.Copy), f"x{k}")
            leave((act_done,), "start")

        def start_vec():
            vec.memset(MC[:, :], 0.0).then_inc(vec_done, C.mark(vec_done, None, LEAD))
            vec.wait_ge(vec_done, LEAD)
            for n, value in enumerate((EPS, GN_EPS, MID, -MID, KK_EPS)):
                v(vec.memset(MC[:, n:n + 1], value))
            v(vec.memset(MS[:, :, :, :], 0.0))
            vec.wait_ge(w_used, 2)
            vec.wait_ge(pe_done, C.at("par16"))
            for b in range(17):
                v(vec.tensor_copy(columns(b, 0, nrows[b]), PS[:, b // 4, (b % 4) * P:(b % 4) * P + nrows[b]]),
                  "columns" if b == 16 else None)
            leave((vec_done,), "start")

        ADA = BIG[:, 0:12288].rearrange("p (s k c) -> p s k c", s=3, k=KD)
        AW = WORK[:, 4096:8192].rearrange("p (s k c) -> p s k c", s=4, k=KD)
        ABANK = 7

        def ada_sp():
            enter(sp, (), "start")
            w = rows(a["ada_w"][0])
            with C.loop(sp, "ada", 2) as i:
                for q in range(3):
                    sp.wait_ge(pe_done, C.at(f"ada.{q}", i, 1))
                    sp.sem_inc(loads_started, 1)
                    sp.dma_start(ADA[:, q], w[:, :, bass.ds(i * 1536 + q * 512, 512)]).then_inc(
                        ada_loaded[q], C.mark(ada_loaded[q], f"ada.load{q}", 16))

        def ada_pe():
            pe.wait_ge(act_done, C.at("silu_c"))
            with C.loop(pe, "ada", 2) as i:
                for q in range(3):
                    pe.wait_ge(vec_done, C.at(f"ada.sum{q}", i, 1))
                    pe.wait_ge(ada_loaded[q], C.at(f"ada.load{q}", i))
                    for m in range(4):
                        for k in range(KD):
                            mm = pe.matmul(PS[:, q, 2 * m:2 * m + 2], ADA[:, q, k, m * P:(m + 1) * P], SC[:, k, :],
                                           start=k == 0, stop=k == KD - 1)
                    mm.then_inc(pe_done, C.mark(pe_done, f"ada.{q}"))
            leave((pe_done, w_used), "ada")

        def mod_rows(l, tile, n, ps, label, i):
            bias = columns(3 * l, tile, n).unsqueeze(2).broadcast_to([P, n, 2])
            v(vec.tensor_tensor(MOD[:, l, bass.ds(tile, n), :], ps.rearrange("p (t s) -> p t s", s=2), bias, ALU.add),
              label, i)

        def norm_gain(l, n):
            gain = columns(3 * l, 48 + 8 * n, 8).unsqueeze(2).broadcast_to([P, KD, 2])
            v(vec.scalar_tensor_tensor(MS[:, 2 * l + n, :, :], MOD[:, l, 24 * n + 8:24 * n + 16, :], 1.0, gain,
                                       ALU.add, ALU.mult))

        def ada_vec():
            enter(vec, (vec_done,), "start")
            with C.loop(vec, "ada", 2) as i:
                for q in range(3):
                    vec.wait_ge(pe_done, C.at(f"ada.{q}", i))
                    mod_rows(0, i * 12 + 4 * q, 4, PS[:, q, 0:8], f"ada.sum{q}", i)
            norm_gain(0, 0)
            v(vec.tensor_copy(MS[:, 2 * DEPTH, :, 1], columns(0, 64, 8)))
            leave((vec_done,), "ada")

        def ride_pool(tag, l, i, slot, tile):
            pool.wait_ge(pe_done, C.at(f"{tag}.a{slot}", i, 1))
            pool.sem_inc(loads_started, 1)
            pool.dma_start(AW[:, slot], rows(a["ada_w"][l])[:, :, bass.ds(tile * P, P)]).then_inc(
                ride_loaded[slot], C.mark(ride_loaded[slot], f"{tag}.al{slot}", 16))

        def ride_pe(tag, i, slot, first):
            if first:
                pe.wait_ge(vec_done, C.at(f"{tag}.am", i, 1))
            pe.wait_ge(ride_loaded[slot], C.at(f"{tag}.al{slot}", i))
            for k in range(KD):
                mm = pe.matmul(PS[:, ABANK, 2 * slot:2 * slot + 2], AW[:, slot, k, :], SC[:, k, :], start=k == 0,
                               stop=k == KD - 1)
            mm.then_inc(pe_done, C.mark(pe_done, f"{tag}.a{slot}"))

        def ride_vec(tag, l, i, tile, n):
            vec.wait_ge(pe_done, C.at(f"{tag}.a{n - 1}", i))
            mod_rows(l, tile, n, PS[:, ABANK, 0:2 * n], f"{tag}.am", i)

        SQ = WORK[:, 0:1024].rearrange("p (b t) -> p b t", b=2)
        RS = WORK[:, 1024:1536]
        TMP = WORK[:, 1536:3584].rearrange("p (b t) -> p b t", b=4)

        def norm_pe(tag, prev, lo):
            enter(pe, (pe_done, w_used), prev)
            for k in range(KD):
                pe.wait_ge(act_done, C.at(f"{tag}.sq{k}"))
                pe.matmul(PS[:, 0, lo:T], const("mean"), SQ[:, k % 2, lo:T], start=k == 0,
                          stop=k == KD - 1).then_inc(pe_done, C.mark(pe_done, f"{tag}.ms{k}"))
            leave((pe_done, w_used), tag)

        def norm_act(tag, prev, lo, gain, shift):
            enter(act, (act_done,), prev)
            for k in range(KD):
                if k >= 2:
                    act.wait_ge(pe_done, C.at(f"{tag}.ms{k - 2}"))
                s(act.activation(SQ[:, k % 2, lo:T], X[:, k, lo:T], ACT.Square), f"{tag}.sq{k}")
            act.wait_ge(pe_done, C.at(f"{tag}.ms7"))
            s(act.activation(RS[:, lo:T], PS[:, 0, lo:T], ACT.Ln, bias=MC[:, 0:1]))
            s(act.activation(RS[:, lo:T], RS[:, lo:T], ACT.Exp, scale=-0.5), f"{tag}.rs")
            for k in range(KD):
                act.wait_ge(vec_done, C.at(f"{tag}.t{k}"))
                for n in range(2):
                    if n == 0 and lo:
                        continue
                    s(act.activation(Hk[:, k, SEGS[n]], TMP[:, k % 4, SEGS[n]], ACT.Identity,
                                     scale=MS[:, gain, k, n:n + 1], bias=shift(k, n)), f"{tag}.h{k}" if n else None)
            leave((act_done,), tag)

        def norm_vec(tag, prev, lo):
            enter(vec, (vec_done,), prev)
            vec.wait_ge(act_done, C.at(f"{tag}.rs"))
            for k in range(KD):
                if k >= 4:
                    vec.wait_ge(act_done, C.at(f"{tag}.h{k - 4}"))
                v(vec.tensor_tensor(TMP[:, k % 4, lo:T], X[:, k, lo:T], RS[:, lo:T], ALU.mult), f"{tag}.t{k}")
            leave((vec_done,), tag)

        def mod_shift(l, n2):
            return lambda k, n: MOD[:, l, 24 * n2 + k, n:n + 1]

        G = BIG[:, 0:NF * T].rearrange("p (f t) -> p f t", f=NF)
        CV = WORK[:, 0:2048].rearrange("p (q h t) -> p q h t", q=2, h=2)
        SG = WORK[:, 2048:3072].rearrange("p (q t) -> p q t", q=2)
        CW = WORK[:, 3072:3204]
        CWj = WORK[:, 3204:3216].rearrange("p (q h t) -> p q h t", q=2, h=2)

        def ffn_sp(l):
            w = rows(a["ffn_w_in"][l])
            with C.loop(sp, f"f{l}", NF // 2) as i:
                for q in range(2):
                    for h in range(2):
                        load_unit(i, f"f{l}.w{q}{h}", unit(w, 0, 8, i * 256 + q * P + h * F))
            w = rows(a["ffn_w_out"][l])
            with C.loop(sp, f"fo{l}", KD // 2) as i:
                for q in range(2):
                    for r in range(3):
                        load_unit(i, f"fo{l}.w{q}{r}", unit(w, 8 * r, 8 if r < 2 else 6, i * 256 + q * P))

        def ffn_pe(l, lo):
            enter(pe, (pe_done, w_used), f"n2{l}")
            with C.loop(pe, f"f{l}", NF // 2) as i:
                for q in range(2):
                    for h in range(2):
                        pe.wait_ge(vec_done, C.at(f"f{l}.cv{q}{h}", i, 1))
                        use_unit(i, f"f{l}.w{q}{h}", PS[:, 2 * q + h, lo:T], lambda k: Hk[:, k, lo:T], 8, True, True)
                        if l + 1 < DEPTH:
                            ride_pe(f"f{l}", i, 2 * q + h, (q, h) == (0, 0))
            pe.wait_ge(vec_done, C.at(f"f{l}.g1"))
            with C.loop(pe, f"fo{l}", KD // 2) as i:
                for q in range(2):
                    pe.wait_ge(vec_done, C.at(f"fo{l}.x{q}", i, 1))
                    for r in range(3):
                        nk = 8 if r < 2 else 6
                        use_unit(i, f"fo{l}.w{q}{r}", PS[:, 4 + q, lo:T], lambda k: G[:, 8 * r + k, lo:T], nk,
                                 r == 0, r == 2)
                if l + 1 < DEPTH:
                    ride_pe(f"fo{l}", i, 0, True)
            leave((pe_done, w_used), f"ffn{l}")

        def ffn_pool(l, prev):
            if l + 1 == DEPTH:
                return
            enter(pool, (pool_done,), prev)
            with C.loop(pool, f"f{l}", NF // 2) as i:
                for slot in range(4):
                    ride_pool(f"f{l}", l + 1, i, slot, i * 4 + slot)
            with C.loop(pool, f"fo{l}", KD // 2) as i:
                ride_pool(f"fo{l}", l + 1, i, 0, i + 44)

        def ffn_act(l, lo):
            enter(act, (act_done,), f"n2{l}")
            act.wait_ge(vec_done, C.at(f"f{l}.cw"))
            with C.loop(act, f"f{l}", NF // 2) as i:
                for q in range(2):
                    act.wait_ge(vec_done, C.at(f"f{l}.cwj", i))
                    for h in range(2):
                        act.wait_ge(w_used, C.at(f"f{l}.w{q}{h}.used", i))
                        if h == 0:
                            act.wait_ge(vec_done, C.at(f"f{l}.g{q}", i, 1))
                        s(act.activation(CV[:, q, h, lo:T], PS[:, 2 * q + h, lo:T], ACT.Copy,
                                         scale=CWj[:, q, h, 1:2]), f"f{l}.c{q}{h}", i)
                for q in range(2):
                    act.wait_ge(vec_done, C.at(f"f{l}.cv{q}1", i))
                    s(act.activation(SG[:, q, lo:T], CV[:, q, 1, lo:T], ACT.Silu), f"f{l}.sg{q}", i)
            leave((act_done,), f"ffn{l}")

        def seg2(ap, lo, x0, x1):
            return ap[:, lo:T].rearrange("p (s t) -> p s t", t=SEG)[:, :, x0:x1]

        def taps(dst, src, w0, w2, lo, label=None, i=None):
            v(vec.scalar_tensor_tensor(seg2(dst, lo, 1, SEG), seg2(src, lo, 0, SEG - 1), w0, seg2(dst, lo, 1, SEG),
                                       ALU.mult, ALU.add), None, i)
            v(vec.scalar_tensor_tensor(seg2(dst, lo, 0, SEG - 1), seg2(src, lo, 1, SEG), w2,
                                       seg2(dst, lo, 0, SEG - 1), ALU.mult, ALU.add), label, i)

        def ffn_vec(l, lo):
            enter(vec, (vec_done,), f"n2{l}")
            v(vec.tensor_copy(CW[:, 0:66], columns(3 * l + 1, 0, 66)))
            v(vec.tensor_copy(CW[:, 66:132], columns(3 * l + 2, 0, 66)), f"f{l}.cw")
            taps3 = CW[:, 0:132].rearrange("p (t h f) -> p h f t", t=3, h=2)
            with C.loop(vec, f"f{l}", NF // 2) as i:
                vec.wait_ge(act_done, C.at(f"f{l}.c11", i, 1))
                for h in range(2):
                    v(vec.tensor_copy(CWj[:, :, h, :], taps3[:, h, bass.ds(i * 2, 2), :]), f"f{l}.cwj" if h else None, i)
                for q in range(2):
                    for h in range(2):
                        vec.wait_ge(act_done, C.at(f"f{l}.c{q}{h}", i))
                        taps(CV[:, q, h, :], PS[:, 2 * q + h, :], CWj[:, q, h, 0:1], CWj[:, q, h, 2:3], lo,
                             f"f{l}.cv{q}{h}", i)
                for q in range(2):
                    vec.wait_ge(act_done, C.at(f"f{l}.sg{q}", i))
                    v(vec.tensor_tensor(G[:, i * 2 + q, lo:T], CV[:, q, 0, lo:T], SG[:, q, lo:T], ALU.mult),
                      f"f{l}.g{q}", i)
                if l + 1 < DEPTH:
                    ride_vec(f"f{l}", l + 1, i, i * 4, 4)
            with C.loop(vec, f"fo{l}", KD // 2) as i:
                for q in range(2):
                    vec.wait_ge(w_used, C.at(f"fo{l}.w{q}2.used", i))
                    residual(i, q, PS[:, 4 + q, :], l, 5, lo, f"fo{l}.x{q}")
                if l + 1 < DEPTH:
                    ride_vec(f"fo{l}", l + 1, i, i + 44, 1)
            if l + 1 < DEPTH:
                norm_gain(l + 1, 0)
                norm_gain(l + 1, 1)
            leave((vec_done,), f"ffn{l}")

        def residual(i, q, ps, l, which, lo, label):
            for n in range(2):
                if n == 0 and lo:
                    continue
                m = i * 2 + q
                v(vec.scalar_tensor_tensor(X[:, m, SEGS[n]], ps[:, SEGS[n]], MOD[:, l, which * 8 + m, n:n + 1],
                                           X[:, m, SEGS[n]], ALU.mult, ALU.add), label if n else None, i)

        def proj_sp(tag, w, units):
            w = rows(w)
            with C.loop(sp, tag, KD // 2) as i:
                for q in range(2):
                    for r in range(units):
                        load_unit(i, f"{tag}.w{q}{r}", unit(w, 8 * r, 8, i * 256 + q * P))

        def proj_pe(tag, rhs, units, lo):
            with C.loop(pe, tag, KD // 2) as i:
                for q in range(2):
                    pe.wait_ge(vec_done, C.at(f"{tag}.x{q}", i, 1))
                    for r in range(units):
                        use_unit(i, f"{tag}.w{q}{r}", PS[:, q, lo:T], lambda k: rhs(8 * r + k), 8, r == 0,
                                 r == units - 1)

        def proj_vec(tag, l, units, lo):
            with C.loop(vec, tag, KD // 2) as i:
                for q in range(2):
                    vec.wait_ge(w_used, C.at(f"{tag}.w{q}{units - 1}.used", i))
                    residual(i, q, PS[:, q, :], l, 2, lo, f"{tag}.x{q}")

        OUT = BIG[:, 0:2048].rearrange("p (c d) -> p c d", d=D)

        def end_pe(prev):
            enter(pe, (pe_done, w_used), prev)
            for c in range(2):
                for h in range(2):
                    for k in range(4):
                        mm = pe.transpose(PS[:, 2 * c + h, k * P:(k + 1) * P],
                                          Hk[:, 4 * h + k, (2 + c) * P:(3 + c) * P], const("ident"))
                    mm.then_inc(pe_done, C.mark(pe_done, f"out{c}{h}"))

        def end_act(prev):
            enter(act, (act_done,), prev)
            for c in range(2):
                for h in range(2):
                    act.wait_ge(pe_done, C.at(f"out{c}{h}"))
                    s(act.activation(OUT[:, c, h * 512:(h + 1) * 512], PS[:, 2 * c + h, :], ACT.Copy), f"o{c}{h}")

        def end_sp():
            for c in range(2):
                sp.wait_ge(act_done, C.at(f"o{c}1"))
                sp.dma_start(out[0, c * P:(c + 1) * P, :], OUT[:, c, :]).then_inc(stored, C.mark(stored, None, 16))
            sp.wait_ge(stored, C.here(stored))

        QKV = BIG[:, 0:6144].rearrange("p (m t) -> p m t", m=12)
        AO = BIG[:, 6144:10240].rearrange("p (m t) -> p m t", m=KD)
        VTOK = BIG[:, 10240:11264].rearrange("p (c d) -> p c d", c=NCH)
        KDUP = BIG[:, 11264:13312].rearrange("p (g t) -> p g t", g=4)
        AC = BIG[:, 13312:13312 + 13 * P]
        SINK = BIG[:, 15104:15120]
        COS, SIN, ROT = AC[:, 0:256], AC[:, 256:512], AC[:, 512:640]
        DUP = [AC[:, (5 + h) * P:(6 + h) * P] for h in range(2)]
        DUPROT = [AC[:, (7 + h) * P:(8 + h) * P] for h in range(2)]
        AMASK = [AC[:, (9 + 2 * b) * P:(11 + 2 * b) * P] for b in range(2)]
        RT = WORK[:, 0:1024].rearrange("p (b t) -> p b t", t=SEG)
        PX = WORK[:, 1024:3072].rearrange("p (e t) -> p e t", e=4)
        PT = WORK[:, 3072:5120].rearrange("p (e t) -> p e t", e=4)
        KG = WORK[:, 5120:5632]
        QG = WORK[:, 5632:6656].rearrange("p (m t) -> p m t", m=2)
        VG = WORK[:, 6656:6912].rearrange("p (c d) -> p c d", c=NCH)
        SM = WORK[:, 6912:6948]
        MX, NM, RSUM, ES, RD, SKG, MX8 = (SM[:, 4 * n:4 * n + 4] for n in range(7))

        def attn_pool(l):
            enter(pool, (), f"n1{l}")
            pool.dma_start(AC, a["attn_consts"]).then_inc(side_loaded[0], C.mark(side_loaded[0], None, 16))
            pool.dma_start(SINK, a["at_sink"][0].partition_broadcast(P)).then_inc(
                side_loaded[0], C.mark(side_loaded[0], "attn.consts", 16))

        def attn_sp(l):
            w = rows(a["at_w_qkv"][0])
            with C.loop(sp, "qkv", 6) as i:
                for q in range(2):
                    load_unit(i, f"qkv.w{q}", unit(w, 0, 8, i * 256 + q * P))
            proj_sp(f"mo{l}", a["at_w_o"][0], 1)

        def attn_pe(l, lo):
            enter(pe, (pe_done, w_used), f"n1{l}")
            with C.loop(pe, "qkv", 6) as i:
                for q in range(2):
                    pe.wait_ge(act_done, C.at(f"qkv.e{q}", i, 1))
                    use_unit(i, f"qkv.w{q}", PS[:, q, :], lambda k: Hk[:, k, :], 8, True, True)
            pe.wait_ge(act_done, C.at("qkv.e1"))
            pe.wait_ge(side_loaded[0], C.at("attn.consts"))
            with C.loop(pe, "rope", 4) as i:
                for q in range(2):
                    pe.wait_ge(vec_done, C.at(f"rope.t{q}", i, 1))
                    pe.matmul(PS[:, 2 + q, 0:SEG], ROT, QKV[:, i * 2 + q, SEG:T], start=True,
                              stop=True).then_inc(pe_done, C.mark(pe_done, f"rope.r{q}"))
            for kv in range(4):
                pe.matmul(PS[:, 4 + kv % 2, :], DUP[kv % 2], QKV[:, 8 + kv // 2, :], start=True, stop=True)
                if kv >= 2:
                    pe.wait_ge(vec_done, C.at(f"kd{kv - 2}"))
                pe.matmul(PS[:, 6 + kv % 2, 0:SEG], DUPROT[kv % 2], QKV[:, 8 + kv // 2, SEG:T], start=True,
                          stop=True).then_inc(pe_done, C.mark(pe_done, f"kr{kv}"))
                if kv == 1:
                    pe.wait_ge(vec_done, C.at("kd1"))
            for m in range(2):
                for c in range(NCH):
                    mm = pe.transpose(PS[:, m, c * P:(c + 1) * P], QKV[:, 10 + m, c * P:(c + 1) * P], const("ident"))
                mm.then_inc(pe_done, C.mark(pe_done, f"vt{m}"))
            with C.loop(pe, "heads", 4) as i:
                pe.wait_ge(vec_done, C.at("heads.in", i))
                pe.wait_ge(act_done, C.at("heads.in.a", i))
                for b in range(4):
                    nk = SEG if b < 2 else T
                    for e in range(4):
                        if e == 0:
                            pe.wait_ge(vec_done, C.at(f"heads.o{b - 1}", i) if b else C.at("heads.in", i))
                        h = slice(64 * (e % 2), 64 * (e % 2) + 64)
                        pe.matmul(PS[:, e, 0:nk], QG[h, e // 2, b * P:(b + 1) * P], KG[h, 0:nk], start=True,
                                  stop=True).then_inc(pe_done, C.mark(pe_done, f"heads.s{b}{e}"))
                    for e in range(4):
                        pe.wait_ge(vec_done, C.at(f"heads.p{b}{e}", i))
                        for kc in range(nk // P):
                            mm = pe.transpose(PS[:, 4 + e, kc * P:(kc + 1) * P], PX[:, e, kc * P:(kc + 1) * P],
                                              const("ident"))
                        mm.then_inc(pe_done, C.mark(pe_done, f"heads.pt{b}{e}"))
                    for e in range(4):
                        pe.wait_ge(act_done, C.at(f"heads.pc{b}{e}", i))
                        h = slice(64 * (e % 2), 64 * (e % 2) + 64)
                        for kc in range(nk // P):
                            mm = pe.matmul(PS[h, e // 2, 0:P], VG[:, kc, :], PT[:, e, kc * P:(kc + 1) * P],
                                           start=kc == 0, stop=kc == nk // P - 1)
                    mm.then_inc(pe_done, C.mark(pe_done, f"heads.ov{b}"))
            pe.wait_ge(vec_done, C.at("heads.o3"))
            proj_pe(f"mo{l}", lambda k: AO[:, k, lo:T], 1, lo)
            leave((pe_done, w_used), f"mix{l}")

        def attn_act(l, lo):
            enter(act, (act_done,), f"n1{l}")
            with C.loop(act, "qkv", 6) as i:
                for q in range(2):
                    act.wait_ge(w_used, C.at(f"qkv.w{q}.used", i))
                    s(act.activation(QKV[:, i * 2 + q, :], PS[:, q, :], ACT.Copy), f"qkv.e{q}", i)
            for m in range(2):
                act.wait_ge(pe_done, C.at(f"vt{m}"))
                s(act.activation(VTOK[:, :, m * P:(m + 1) * P], PS[:, m, :].rearrange("p (c d) -> p c d", c=NCH),
                                 ACT.Copy), f"vtok{m}")
            act.wait_ge(vec_done, C.at("kd3"))
            act.wait_ge(vec_done, C.at("rope.q1"))
            with C.loop(act, "heads", 4) as i:
                act.wait_ge(pe_done, C.at("heads.ov3", i, 1))
                s(act.activation(KG, KDUP[:, i, :], ACT.Copy), None, i)
                s(act.activation(VG[:, :, :], VTOK[:, :, bass.ds(i * 64, 64)], ACT.Copy), "heads.in.a", i)
                for b in range(4):
                    nk = SEG if b < 2 else T
                    act.wait_ge(vec_done, C.at(f"heads.nm{b}", i))
                    for e in range(4):
                        s(act.activation(PX[:, e, 0:nk], PS[:, e, 0:nk], ACT.Exp, bias=NM[:, e:e + 1], scale=0.125,
                                         accum_out=RSUM[:, e:e + 1]), f"heads.ex{b}{e}", i)
                    s(act.activation(ES, ES, ACT.Exp), f"heads.es{b}", i)
                    for e in range(4):
                        act.wait_ge(pe_done, C.at(f"heads.pt{b}{e}", i))
                        s(act.activation(PT[:, e, 0:nk], PS[:, 4 + e, 0:nk], ACT.Copy), f"heads.pc{b}{e}", i)
            leave((act_done,), f"mix{l}")

        def attn_vec(l, lo):
            enter(vec, (vec_done,), f"n1{l}")
            vec.wait_ge(side_loaded[0], C.at("attn.consts"))
            vec.wait_ge(act_done, C.at("qkv.e1"))
            with C.loop(vec, "rope", 4) as i:
                for q in range(2):
                    m = i * 2 + q
                    vec.wait_ge(pe_done, C.at(f"rope.r{q}", i))
                    v(vec.tensor_tensor(RT[:, q, :], PS[:, 2 + q, 0:SEG], SIN, ALU.mult), f"rope.t{q}", i)
                    v(vec.tensor_tensor(QKV[:, m, SEG:T], QKV[:, m, SEG:T], COS, ALU.mult), None, i)
                    v(vec.tensor_tensor(QKV[:, m, SEG:T], QKV[:, m, SEG:T], RT[:, q, :], ALU.add), f"rope.q{q}", i)
            for kv in range(4):
                vec.wait_ge(pe_done, C.at(f"kr{kv}"))
                v(vec.tensor_tensor(RT[:, 2, :], PS[:, 6 + kv % 2, 0:SEG], SIN, ALU.mult))
                v(vec.tensor_tensor(RT[:, 3, :], PS[:, 4 + kv % 2, SEG:T], COS, ALU.mult))
                v(vec.tensor_copy(KDUP[:, kv, 0:SEG], PS[:, 4 + kv % 2, 0:SEG]))
                v(vec.tensor_tensor(KDUP[:, kv, SEG:T], RT[:, 2, :], RT[:, 3, :], ALU.add), f"kd{kv}")
            with C.loop(vec, "heads", 4) as i:
                vec.wait_ge(pe_done, C.at("heads.ov3", i, 1))
                v(vec.tensor_copy(QG[:, :, :], QKV[:, bass.ds(i * 2, 2), :]), None, i)
                v(vec.tensor_copy(SKG, SINK[:, bass.ds(i * 4, 4)]), "heads.in", i)
                for b in range(4):
                    nk = SEG if b < 2 else T
                    for e in range(4):
                        vec.wait_ge(pe_done, C.at(f"heads.s{b}{e}", i))
                        if b >= 2:
                            v(vec.tensor_tensor(PS[:, e, SEG:T], PS[:, e, SEG:T], AMASK[b - 2], ALU.add), None, i)
                        v(vec.reduce_max(MX[:, e:e + 1], PS[:, e, 0:nk], AX_X), None, i)
                    v(vec.tensor_scalar(MX8, MX, 0.125, None, ALU.mult), None, i)
                    v(vec.tensor_tensor(MX8, MX8, SKG, ALU.max), None, i)
                    v(vec.tensor_tensor(ES, SKG, MX8, ALU.subtract), None, i)
                    v(vec.tensor_scalar(NM, MX8, -1.0, None, ALU.mult), f"heads.nm{b}", i)
                    vec.wait_ge(act_done, C.at(f"heads.es{b}", i))
                    v(vec.tensor_tensor(RD, RSUM, ES, ALU.add), None, i)
                    v(vec.reciprocal(RD, RD), None, i)
                    for e in range(4):
                        v(vec.tensor_scalar(PX[:, e, 0:nk], PX[:, e, 0:nk], RD[:, e:e + 1], None, ALU.mult),
                          f"heads.p{b}{e}", i)
                    vec.wait_ge(pe_done, C.at(f"heads.ov{b}", i))
                    v(vec.tensor_copy(AO[:, bass.ds(i * 2, 2), b * P:(b + 1) * P], PS[:, 0:2, 0:P]),
                      f"heads.o{b}", i)
            proj_vec(f"mo{l}", l, 1, lo)
            leave((vec_done,), f"mix{l}")

        YB = BIG[:, 0:8192].rearrange("p (m t) -> p m t", m=16)
        ACB = BIG[:, 8192:12288].rearrange("p (r t) -> p r t", r=8)
        FS = BIG[:, 12288:16384].rearrange("p (r t) -> p r t", r=8)
        XT = BIG[:, 16384:17408].rearrange("p (c f) -> p c f", c=NCH)
        BT = BIG[:, 17408:17920].rearrange("p (c f) -> p c f", c=NCH)
        XDT = BIG[:, 17920:19968].rearrange("p (d c f) -> p d c f", d=2, c=NCH)
        DCOL = BIG[:, 19968:19984]
        DTB, ALOG = BIG[0:64, 19984:19985], BIG[0:64, 19985:19986]
        DALL = BIG[:, 20000:20032]
        DTw = [BIG[0:64, 12288 + 512 * n:12800 + 512 * n] for n in range(8)]
        XTE = WORK[:, 0:2048].rearrange("p (d c f) -> p d c f", d=2, c=NCH)
        XS = WORK[:, 2048:4096].rearrange("p (m t) -> p m t", m=4)
        ZS = WORK[:, 4096:5120].rearrange("p (m t) -> p m t", m=2)
        CBM = WORK[:, 5120:6144].rearrange("p (d c t) -> p d c t", d=2, c=NCH)
        SEGM = WORK[:, 6144:7168].rearrange("p (b e t) -> p b e t", b=2, e=4)
        MM_ = WORK[:, 7168:8192].rearrange("p (b e t) -> p b e t", b=2, e=4)
        YT_ = WORK[:, 8192:9216].rearrange("p (m t) -> p m t", m=2)
        STT_ = WORK[:, 9216:9728].rearrange("p (d f) -> p d f", d=2)
        DTT = WORK[:, 9728:9984].rearrange("p (c h) -> p c h", c=NCH)
        ACST = WORK[:, 9984:10240].rearrange("p (c h) -> p c h", c=NCH)
        TE = WORK[:, 10240:10272].rearrange("p (d c e) -> p d c e", d=2, c=NCH)
        CD = WORK[:, 10272:10304].rearrange("p (d c e) -> p d c e", d=2, c=NCH)
        ACG = WORK[:, 10304:10336].rearrange("p (c d e) -> p c d e", d=2, c=NCH)
        DTG = WORK[:, 10336:10368].rearrange("p (c d e) -> p c d e", d=2, c=NCH)
        CP = WORK[:, 10368:10384].rearrange("p (k m) -> p k m", k=4)
        DG, NG = WORK[:, 10384:10386], WORK[:, 10386:10388]
        SQG = WORK[:, 10400:11424].rearrange("p (m t) -> p m t", m=2)
        RSG = WORK[:, 11424:11936]
        END = (P - 1, 0)

        def ssd_pool(l):
            enter(pool, (), f"n1{l}")
            pool.dma_start(DALL, a["ssd_d"][0].partition_broadcast(P)).then_inc(
                side_loaded[1], C.mark(side_loaded[1], None, 16))
            pool.dma_start(DTB, a["ssd_dt_bias"][0].rearrange("d h -> (d h)").unsqueeze(1)).then_inc(
                side_loaded[1], C.mark(side_loaded[1], None, 16))
            pool.dma_start(ALOG, a["ssd_a_log"][0].rearrange("d h -> (d h)").unsqueeze(1)).then_inc(
                side_loaded[1], C.mark(side_loaded[1], "ssd.params", 16))
            pool.wait_ge(vec_done, C.at("ssd.acs"))
            pool.dma_start(scratch, DTw[7]).then_inc(scratch_stored, C.mark(scratch_stored, "ssd.stored", 16))
            pool.wait_ge(scratch_stored, C.at("ssd.stored"))
            by_group = scratch.rearrange("(d g e) t -> g d e t", d=2, e=4)
            with C.loop(pool, "ssd", 8) as i:
                pool.wait_ge(vec_done, C.at("ssd.sg31", i, 1))
                pool.wait_ge(act_done, C.at("ssd.fs", i, 1))
                pool.dma_start(ACB[:, :, :].rearrange("p (d e) t -> p d e t", d=2),
                               by_group[i].partition_broadcast(P)).then_inc(
                    side_loaded[2], C.mark(side_loaded[2], "ssd.acbload", 16))

        def ssd_sp(l):
            w = rows(a["ssd_w_in"][0])
            load_unit(None, "ssd.wdt", unit(w, 0, 8, INNER + 4096, 64))
            with C.loop(sp, "ssd", 8) as i:
                for q, c0 in enumerate((i * 256 + INNER, i * 256 + (INNER + P), i * P + 2 * INNER,
                                        i * P + 2 * INNER + 1024, i * 256, i * 256 + P)):
                    load_unit(i, f"ssd.w{q}", unit(w, 0, 8, c0))
            proj_sp(f"mo{l}", a["ssd_w_out"][0], 2)

        def ssd_pe(l, lo):
            enter(pe, (pe_done, w_used), f"n1{l}")
            use_unit(None, "ssd.wdt", PS[0:64, 0, :], lambda k: Hk[:, k, :], 8, True, True, 64)
            pe.wait_ge(vec_done, C.at("ssd.acs"))
            for n, src in ((1, DTw[6]), (2, DTw[7])):
                for c in range(NCH):
                    mm = pe.transpose(PS[:, n, c * 64:(c + 1) * 64], src[:, c * P:(c + 1) * P],
                                      const("ident")[0:64, 0:64])
                mm.then_inc(pe_done, C.mark(pe_done, f"ssd.tr{n}"))
            pe.wait_ge(vec_done, C.at("ssd.acst"))
            with C.loop(pe, "ssd", 8) as i:
                pe.wait_ge(vec_done, C.at("ssd.y31", i, 1))
                for q in range(6):
                    use_unit(i, f"ssd.w{q}", PS[:, q, :], lambda k: Hk[:, k, :], 8, True, True)
                for q in range(3):
                    pe.wait_ge(act_done, C.at(f"ssd.silu{q}", i))
                    for c in range(NCH):
                        mm = pe.transpose(PS[:, (6, 7, 0)[q], c * P:(c + 1) * P], XS[:, q, c * P:(c + 1) * P],
                                          const("ident"))
                    mm.then_inc(pe_done, C.mark(pe_done, f"ssd.xt{q}"))
                pe.wait_ge(act_done, C.at("ssd.silu3", i))
                for c in range(NCH):
                    cs = slice(c * P, (c + 1) * P)
                    mm = pe.matmul(PS[:, 1, cs], XS[:, 2, cs], XS[:, 3, cs], start=True, stop=True)
                mm.then_inc(pe_done, C.mark(pe_done, "ssd.cb"))
                pe.wait_ge(vec_done, C.at("ssd.xte", i))
                pe.wait_ge(act_done, C.at("ssd.bt", i))
                pe.wait_ge(act_done, C.at("ssd.z1", i))
                for c in range(NCH):
                    for d in range(2):
                        ch = ORDER[d][c]
                        cs = slice(ch * P, (ch + 1) * P)
                        if c < NCH - 1:
                            if c:
                                pe.wait_ge(vec_done, C.at(f"ssd.st{c - 1}{d}", i))
                            pe.matmul(PS[:, 4 + d, 0:256], BT[:, ch, :], XTE[:, d, ch, :], start=True,
                                      stop=True).then_inc(pe_done, C.mark(pe_done, f"ssd.s{c}{d}"))
                        pe.wait_ge(vec_done, C.at(f"ssd.m{c}{d}", i))
                        for e in range(4):
                            h = slice(64 * (e % 2), 64 * (e % 2) + 64)
                            o = PS[h, 2 + d, (e // 2) * P:(e // 2 + 1) * P]
                            ef = slice(e * 64, (e + 1) * 64)
                            mm = pe.matmul(o, XDT[:, d, ch, ef], MM_[:, d, e, :], start=True, stop=c == 0)
                            if c:
                                mm = pe.matmul(o, STT_[:, d, ef], FS[:, 4 * d + e, cs], start=False, stop=True)
                        mm.then_inc(pe_done, C.mark(pe_done, f"ssd.yo{c}{d}"))
                pe.wait_ge(act_done, C.at("ssd.sq", i))
                for m in range(2):
                    mm = pe.matmul(PS[:, 6, :], const("mean256"), SQG[:, m, :], start=m == 0, stop=m == 1)
                mm.then_inc(pe_done, C.mark(pe_done, "ssd.ms"))
            pe.wait_ge(vec_done, C.at("ssd.yb"))
            proj_pe(f"mo{l}", lambda k: YB[:, k, lo:T], 2, lo)
            leave((pe_done, w_used), f"mix{l}")

        def ssd_act(l, lo):
            enter(act, (act_done,), f"n1{l}")
            act.wait_ge(vec_done, C.at("ssd.z"))
            s(act.activation(DTw[1], DTw[0], ACT.Abs))
            s(act.activation(DTw[1], DTw[1], ACT.Exp, scale=-1.0), "ssd.e")
            act.wait_ge(side_loaded[1], C.at("ssd.params"))
            s(act.activation(ALOG, ALOG, ACT.Exp), "ssd.a")
            act.wait_ge(vec_done, C.at("ssd.acst"))
            act.wait_ge(scratch_stored, C.at("ssd.stored"))
            with C.loop(act, "ssd", 8) as i:
                act.wait_ge(vec_done, C.at("ssd.cp", i))
                act.wait_ge(pe_done, C.at("ssd.ms", i, 1))
                for q in range(4):
                    act.wait_ge(w_used, C.at(f"ssd.w{q}.used", i))
                    s(act.activation(XS[:, q, :], PS[:, q, :], ACT.Identity, scale=CP[:, 1, q:q + 1],
                                     bias=CP[:, 3, q:q + 1]), f"ssd.c{q}", i)
                for q in range(4):
                    act.wait_ge(vec_done, C.at(f"ssd.cv{q}", i))
                    s(act.activation(XS[:, q, :], XS[:, q, :], ACT.Silu), f"ssd.silu{q}", i)
                for q in range(2):
                    act.wait_ge(w_used, C.at(f"ssd.w{4 + q}.used", i))
                    s(act.activation(ZS[:, q, :], PS[:, 4 + q, :], ACT.Silu), f"ssd.z{q}", i)
                for q in range(2):
                    act.wait_ge(pe_done, C.at(f"ssd.xt{q}", i))
                    s(act.activation(XT[:, :, q * P:(q + 1) * P], PS[:, 6 + q, :].rearrange("p (c f) -> p c f", c=NCH),
                                     ACT.Copy), f"ssd.xtok{q}", i)
                act.wait_ge(pe_done, C.at("ssd.xt2", i))
                s(act.activation(BT[:, :, :], PS[:, 0, :].rearrange("p (c f) -> p c f", c=NCH), ACT.Copy), "ssd.bt", i)
                act.wait_ge(vec_done, C.at("ssd.te0", i))
                s(act.activation(TE[:, :, :, :], TE[:, :, :, :], ACT.Exp), "ssd.te", i)
                act.wait_ge(side_loaded[2], C.at("ssd.acbload", i))
                for r in range(8):
                    s(act.activation(FS[:, r, :], ACB[:, r, :], ACT.Exp), "ssd.fs" if r == 7 else None, i)
                for c in range(NCH):
                    for d in range(2):
                        act.wait_ge(vec_done, C.at(f"ssd.sg{c}{d}", i))
                        s(act.activation(SEGM[:, d, :, :], SEGM[:, d, :, :], ACT.Exp), f"ssd.ex{c}{d}", i)
                act.wait_ge(vec_done, C.at("ssd.yz", i))
                s(act.activation(SQG[:, :, :], YT_[:, :, :], ACT.Square), "ssd.sq", i)
                act.wait_ge(pe_done, C.at("ssd.ms", i))
                s(act.activation(RSG, PS[:, 6, :], ACT.Ln, bias=MC[:, 0:1]), None, i)
                s(act.activation(RSG, RSG, ACT.Exp, scale=-0.5), "ssd.rs", i)
            leave((act_done,), f"mix{l}")

        def ssd_vec(l, lo):
            enter(vec, (vec_done,), f"n1{l}")
            Z, E, R, S, S2, Q, DT, AC_ = DTw
            vec.wait_ge(side_loaded[1], C.at("ssd.params"))
            for h in range(2):
                ph = slice(64 * h, 64 * h + 64)
                v(vec.tensor_copy(DCOL[ph, :], DALL[ph, :].rearrange("p (m h) -> p h m", h=2)[:, h, :]))
            vec.wait_ge(w_used, C.at("ssd.wdt.used"))
            v(vec.tensor_scalar(Z, PS[0:64, 0, :], DTB, None, ALU.add), "ssd.z")
            vec.wait_ge(act_done, C.at("ssd.e"))
            v(vec.tensor_scalar(R, E, 2.0, None, ALU.add))
            v(vec.reciprocal(R, R))
            v(vec.tensor_tensor(S, E, R, ALU.mult))
            v(vec.tensor_tensor(S2, S, S, ALU.mult))
            v(vec.tensor_scalar(Q, S2, 1.0 / 15, None, ALU.mult))
            for n in (13, 11, 9, 7, 5, 3):
                v(vec.scalar_tensor_tensor(Q, Q, 1.0 / n, S2, ALU.add, ALU.mult))
            v(vec.scalar_tensor_tensor(Q, Q, 1.0, S, ALU.add, ALU.mult))
            v(vec.tensor_scalar(Z, Z, 0.0, None, ALU.max))
            v(vec.scalar_tensor_tensor(DT, Q, 2.0, Z, ALU.mult, ALU.add))
            vec.wait_ge(act_done, C.at("ssd.a"))
            v(vec.tensor_scalar(ALOG, ALOG, -1.0, None, ALU.mult))
            v(vec.tensor_scalar(S, DT, ALOG, None, ALU.mult))
            for c in range(NCH):
                cs = slice(c * P, (c + 1) * P)
                v(vec.tensor_tensor_scan(AC_[:, cs], const("ones")[0:64, :], S[:, cs], 0.0, ALU.mult, ALU.add))
            b3 = lambda ap: ap[32:64, :].rearrange("p (c t) -> p c t", c=NCH)
            v(vec.tensor_tensor(b3(Q), b3(AC_)[:, :, P - 1:P].broadcast_to([32, NCH, P]), b3(AC_), ALU.subtract))
            v(vec.tensor_tensor(b3(AC_), b3(Q), b3(S), ALU.add), "ssd.acs")
            for n, dst in ((1, DTT), (2, ACST)):
                vec.wait_ge(pe_done, C.at(f"ssd.tr{n}"))
                v(vec.tensor_copy(dst[:, :, :], PS[:, n, 0:256].rearrange("p (c h) -> p c h", c=NCH)),
                  "ssd.acst" if n == 2 else None)
            cw = columns(B_SSD, 0, P).rearrange("p (k m) -> p k m", k=4)
            with C.loop(vec, "ssd", 8) as i:
                v(vec.tensor_copy(CP[:, :, 0:2], cw[:, :, bass.ds(i * 2, 2)]), None, i)
                v(vec.tensor_copy(CP[:, :, 2], cw[:, :, i + 16]), None, i)
                v(vec.tensor_copy(CP[:, :, 3], cw[:, :, i + 24]), None, i)
                for d in range(2):
                    v(vec.tensor_copy(ACG[:, :, d, :], ACST[:, :, bass.ds(i * 4 + 32 * d, 4)]), None, i)
                    v(vec.tensor_copy(DTG[:, :, d, :], DTT[:, :, bass.ds(i * 4 + 32 * d, 4)]), None, i)
                v(vec.tensor_copy(DG, DCOL[:, bass.ds(i * 2, 2)]), None, i)
                v(vec.tensor_copy(NG, columns(B_SSDN, i * 2, 2)), "ssd.cp", i)
                for q in range(4):
                    vec.wait_ge(act_done, C.at(f"ssd.c{q}", i))
                    taps(XS[:, q, :], PS[:, q, :], CP[:, 0, q:q + 1], CP[:, 2, q:q + 1], 0, f"ssd.cv{q}", i)
                vec.wait_ge(side_loaded[2], C.at("ssd.acbload", i))
                for d in range(2):
                    ends = ACB[:, 4 * d:4 * d + 4, :].rearrange("p e (c t) -> p c e t", c=NCH)[:, :, :, END[d]]
                    v(vec.tensor_tensor(TE[:, d, :, :], ends, ACG[:, :, d, :], ALU.subtract),
                      "ssd.te0" if d else None, i)
                for q in range(2):
                    vec.wait_ge(act_done, C.at(f"ssd.xtok{q}", i))
                xt4 = XT[:, :, :].rearrange("p c (e f) -> p c e f", e=4)
                for d in range(2):
                    v(vec.tensor_tensor(XDT[:, d, :, :].rearrange("p c (e f) -> p c e f", e=4), xt4,
                                        DTG[:, :, d, :].unsqueeze(3).broadcast_to([P, NCH, 4, 64]), ALU.mult), None, i)
                vec.wait_ge(act_done, C.at("ssd.te", i))
                for d in range(2):
                    v(vec.tensor_tensor(XTE[:, d, :, :].rearrange("p c (e f) -> p c e f", e=4),
                                        XDT[:, d, :, :].rearrange("p c (e f) -> p c e f", e=4),
                                        TE[:, d, :, :].unsqueeze(3).broadcast_to([P, NCH, 4, 64]), ALU.mult), None, i)
                vec.wait_ge(pe_done, C.at("ssd.cb", i))
                for d in range(2):
                    v(vec.tensor_tensor(CBM[:, d, :, :], PS[:, 1, :].rearrange("p (c t) -> p c t", c=NCH),
                                        const(f"gi{d}").unsqueeze(1).broadcast_to([P, NCH, P]), ALU.mult), None, i)
                vec.wait_ge(act_done, C.at("ssd.fs", i))
                for d in range(2):
                    ends = FS[:, 4 * d:4 * d + 4, :].rearrange("p e (c t) -> p c e t", c=NCH)[:, :, :, END[d]]
                    v(vec.tensor_copy(CD[:, d, :, :], ends), None, i)
                v(vec.tensor_tensor(FS[:, :, :], FS[:, :, :], XS[:, 3, :].unsqueeze(1).broadcast_to([P, 8, T]),
                                    ALU.mult), "ssd.xte", i)

                def segs(c, d):
                    ch = ORDER[d][c]
                    for e in range(4):
                        v(vec.tensor_scalar(SEGM[:, d, e, :], ACB[:, 4 * d + e, ch * P:(ch + 1) * P],
                                            ACG[:, ch, d, e:e + 1], 0.0, ALU.subtract, ALU.min),
                          f"ssd.sg{c}{d}" if e == 3 else None, i)

                def gather(c, d):
                    ch = ORDER[d][c]
                    cs = slice(ch * P, (ch + 1) * P)
                    if c < NCH - 1:
                        vec.wait_ge(pe_done, C.at(f"ssd.yo{c}{d}", i))
                        if c:
                            v(vec.tensor_tensor(STT_[:, d, :].rearrange("p (e f) -> p e f", e=4),
                                                STT_[:, d, :].rearrange("p (e f) -> p e f", e=4),
                                                CD[:, d, ch, :].unsqueeze(2).broadcast_to([P, 4, 64]), ALU.mult),
                              None, i)
                            v(vec.tensor_tensor(STT_[:, d, :], STT_[:, d, :], PS[:, 4 + d, 0:256], ALU.add),
                              f"ssd.st{c}{d}", i)
                        else:
                            v(vec.tensor_copy(STT_[:, d, :], PS[:, 4 + d, 0:256]), f"ssd.st{c}{d}", i)
                    else:
                        vec.wait_ge(pe_done, C.at(f"ssd.yo{c}{d}", i))
                    y = PS[:, 2 + d, 0:256].rearrange("p (m t) -> p m t", m=2)
                    if c % 2 == 0:
                        v(vec.tensor_copy(YT_[:, :, cs], y), f"ssd.y{c}{d}", i)
                    else:
                        v(vec.tensor_tensor(YT_[:, :, cs], YT_[:, :, cs], y, ALU.add), f"ssd.y{c}{d}", i)

                steps = [(c, d) for c in range(NCH) for d in range(2)]
                for d in range(2):
                    segs(0, d)
                for n, (c, d) in enumerate(steps):
                    ch = ORDER[d][c]
                    vec.wait_ge(act_done, C.at(f"ssd.ex{c}{d}", i))
                    if c:
                        vec.wait_ge(pe_done, C.at(f"ssd.yo{c - 1}{d}", i))
                    v(vec.tensor_tensor(MM_[:, d, :, :], SEGM[:, d, :, :],
                                        CBM[:, d, ch, :].unsqueeze(1).broadcast_to([P, 4, P]), ALU.mult),
                      f"ssd.m{c}{d}", i)
                    if c < NCH - 1:
                        segs(c + 1, d)
                    if n:
                        gather(*steps[n - 1])
                gather(*steps[-1])
                for m in range(2):
                    v(vec.scalar_tensor_tensor(YT_[:, m, :], XS[:, m, :], DG[:, m:m + 1], YT_[:, m, :], ALU.mult,
                                               ALU.add), None, i)
                v(vec.tensor_tensor(YT_[:, :, :], YT_[:, :, :], ZS[:, :, :], ALU.mult), "ssd.yz", i)
                vec.wait_ge(act_done, C.at("ssd.rs", i))
                for m in range(2):
                    v(vec.scalar_tensor_tensor(YB[:, i * 2 + m, :], YT_[:, m, :], NG[:, m:m + 1], RSG, ALU.mult,
                                               ALU.mult), "ssd.yb" if m else None, i)
            proj_vec(f"mo{l}", l, 2, lo)
            leave((vec_done,), f"mix{l}")

        RKV = BIG[:, 0:12288].rearrange("p (n k t) -> p n k t", n=3, k=KD)
        XM = BIG[:, 12288:16384].rearrange("p (k t) -> p k t", k=KD)
        DX = BIG[:, 16384:20480].rearrange("p (k t) -> p k t", k=KD)
        _w = [0]

        def work(n):
            _w[0] += n
            assert _w[0] <= WORK_N
            return WORK[:, _w[0] - n:_w[0]]

        TH, AL, GS = work(512), work(512), work(512)
        W2S, A2S, G2S = work(P), work(P), work(P)
        SD = work(1024).rearrange("p (d t) -> p d t", d=2)
        AD = work(1024).rearrange("p (d t) -> p d t", d=2)
        AR = work(2048).rearrange("p (d n t) -> p d n t", d=2, n=2)
        ARS = work(2048).rearrange("p (d n t) -> p d n t", d=2, n=2)
        PN = work(1024).rearrange("p (d t) -> p d t", d=2)
        KK, KF, BV, YT, BS = (work(512) for _ in range(5))
        KBT = work(1024).rearrange("p (d c f) -> p d c f", d=2, c=NCH)
        BNT = work(1024).rearrange("p (d c f) -> p d c f", d=2, c=NCH)
        VTK = work(512).rearrange("p (c f) -> p c f", c=NCH)
        WS = work(256).rearrange("p (h d f) -> p h d f", h=2, d=2)
        US = work(256).rearrange("p (h d f) -> p h d f", h=2, d=2)
        STR = work(128).rearrange("p (d f) -> p d f", d=2)
        PCT, PCTS = (work(8).rearrange("p (d c) -> p d c", d=2) for _ in range(2))
        PC, PCN = work(10), work(10)
        free = [H[:, 512 * n:512 * n + 512] for n in range(8)] + [
            BIG[:, 12288 + 512 * n:12800 + 512 * n] for n in range(16)] + [work(512) for _ in range(6)]
        GM1, GM2 = ([[free.pop(0).rearrange("p (d n t) -> p d n t", d=2, n=2) for h in range(2)] for c in range(NCH)]
                    for _ in range(2))
        XTR = [free.pop(0) for c in range(NCH)]
        NB = [{n: free.pop(0) for n in (0, 2, 3, 4, 5)} for e in range(2)]
        quad = lambda ap: ap.rearrange("p (q t) -> p q t", q=4)
        IB = ((6, 7), (4, 5))
        END_R = (P - 1, 0)
        MIXES = (("r", 0), ("k", 2), ("v", 3))
        LORA = (("w", 1), ("a", 4), ("g", 5))
        LEVELS = ("lev8", "lev16", "lev32", "lev64")

        def trip_order(staging):
            first = [("I", 0, 0), ("I", 0, 1), ("T", 0), ("I", 0, 2), ("T", 1)] + [("I", 0, n) for n in range(3, 12)]
            chunks01 = [("C", c, n) for c in range(2) for n in range(3)]
            second = [("I", 1, 0), ("I", 1, 1)]
            for n in range(2, 12):
                second += chunks01[n - 2:n - 1] + [("I", 1, n)]
            third = [("C", 2, 0), ("C", 2, 1), ("C", 2, 2), ("C", 3, 0), ("C", 3, 1), ("C", 3, 2)]
            if staging:
                third = [("S", 0), third[0], ("S", 1), third[1], ("S", 2), third[2], ("S", 3), third[3], third[4],
                         ("S", 4), third[5]]
            return first + second + third

        def play(steps, i, tile, t, staging):
            for kind, *n in trip_order(staging):
                steps[kind](i, tile, t, *n)

        def rwkv_sp(l):
            j, t, b = l // 3, f"r{l}", f"r{l}b"
            for name, w in (("r", "rw_wr"), ("k", "rw_wk"), ("v", "rw_wv")):
                w = rows(a[w][j])
                with C.loop(sp, t + name, 4) as i:
                    for q in range(2):
                        load_unit(i, f"{t}.{name}{q}", unit(w, 0, 8, i * 256 + q * P))
            for name, w in (("w", "rw_w1"), ("a", "rw_a1")):
                load_unit(None, f"{t}.{name}",
                          (lambda slot: slot[:, :, 0:64], rows(a[w][j][0])), (lambda slot: slot[:, :, 64:P], rows(a[w][j][1])))
            load_unit(None, f"{t}.g", unit(rows(a["rw_g1"][j]), 0, 8, 0))
            enter(sp, (), f"n1{l}")
            w2 = a["rw_w2"][j].rearrange("d r n -> (d r) n")
            a2 = a["rw_a2"][j].rearrange("d r n -> (d r) n")

            def load_w2(label, col):
                sp.dma_start(W2S, w2[:, bass.ds(col, P)]).then_inc(side_loaded[3], C.mark(side_loaded[3], None, 16))
                sp.dma_start(A2S, a2[:, bass.ds(col, P)]).then_inc(side_loaded[3], C.mark(side_loaded[3], label, 16))

            def load_g2(label, col):
                sp.dma_start(G2S, a["rw_g2"][j][:, bass.ds(col, P)]).then_inc(g2_loaded, C.mark(g2_loaded, label, 16))

            load_w2(f"{t}p.s2", 0)
            with C.loop(sp, b, KD - 1) as i:
                sp.wait_ge(pe_done, C.at(f"{b}.post", i, 1))
                sp.sem_inc(loads_started, 1)
                load_g2(f"{b}.g2", i * P)
                sp.wait_ge(w2_used, C.at(f"{b}.wa", i, 1))
                sp.sem_inc(loads_started, 1)
                load_w2(f"{b}.s2", i * P + P)
            sp.wait_ge(pe_done, C.at(f"{b}.post"))
            load_g2(f"{t}z.g2", (KD - 1) * P)
            proj_sp(f"mo{l}", a["rw_wo"][j], 1)

        def rwkv_pe(l, lo):
            t0 = f"r{l}"
            enter(pe, (pe_done, w_used), f"n1{l}")
            for name, m in MIXES:
                pe.wait_ge(vec_done, C.at(f"{t0}.mix{m}"))
                with C.loop(pe, t0 + name, 4) as i:
                    for q in range(2):
                        pe.wait_ge(act_done, C.at(f"{t0}.{name}e{q}", i, 1))
                        use_unit(i, f"{t0}.{name}{q}", PS[:, q, :], lambda k: XM[:, k, :], 8, True, True)
                        if l == 0:
                            ride_pe(t0 + name, i, q, q == 0)
            for n, (name, m) in enumerate(LORA):
                pe.wait_ge(vec_done, C.at(f"{t0}.mix{m}"))
                use_unit(None, f"{t0}.{name}", PS[:, 2 + n, :], lambda k: XM[:, k, :], 8, True, True)
            pe.wait_ge(act_done, C.at(f"{t0}.ge"))

            def gram_kk(i, t, c, banks):
                for h in range(2):
                    hs = slice(64 * h, 64 * h + 64)
                    for d in range(2):
                        ch = ORDER[d][c]
                        cs = slice(ch * P, (ch + 1) * P)
                        mm = pe.matmul(PS[:, banks[h], 256 * d:256 * d + 256], AD[hs, d, cs], AR[hs, d, :, cs],
                                       start=True, stop=True)
                mm.then_inc(pe_done, C.mark(pe_done, f"{t}.g1{c}"))

            def gram_rest(i, t, c, banks):
                for h in range(2):
                    hs = slice(64 * h, 64 * h + 64)
                    for d in range(2):
                        ch = ORDER[d][c]
                        cs = slice(ch * P, (ch + 1) * P)
                        mm = pe.matmul(PS[:, 4 + h, d * P:(d + 1) * P], AR[hs, d, 0, cs], AD[hs, d, cs], start=True,
                                       stop=True)
                mm.then_inc(pe_done, C.mark(pe_done, f"{t}.gt{c}"))
                if c == 0:
                    pe.wait_ge(vec_done, C.at(f"{t}.prod", i))
                for h in range(2):
                    hs = slice(64 * h, 64 * h + 64)
                    for d in range(2):
                        ch = ORDER[d][c]
                        cs = slice(ch * P, (ch + 1) * P)
                        mm = pe.matmul(PS[:, banks[h], 256 * d:256 * d + 256], SD[hs, d, cs], AR[hs, d, :, cs],
                                       start=True, stop=True)
                mm.then_inc(pe_done, C.mark(pe_done, f"{t}.g2{c}"))

            def four(bank, lhs, rhs):
                for q in range(4):
                    qs = slice(q * P, (q + 1) * P)
                    mm = pe.matmul(PS[:, bank, qs], lhs[:, qs], rhs[:, qs], start=True, stop=True)
                return mm

            def invert(i, tile, t, pair, n):
                two = [(e, 2 * pair + e) for e in range(2)]
                if n == 0:
                    c = 2 * pair
                    if pair == 0:
                        pe.wait_ge(vec_done, C.at(f"{t}.prod1", i))
                        pe.wait_ge(pool_done, C.at(f"{t}.ar0", i))
                    else:
                        pe.wait_ge(vec_done, C.at(f"{t}.xf1", i))
                    gram_kk(i, t, c, (0, 1))
                    gram_rest(i, t, c, (2, 3))
                    gram_kk(i, t, c + 1, (6, 7))
                    pe.wait_ge(vec_done, C.at(f"{t}.ga{c}", i))
                    gram_rest(i, t, c + 1, (0, 1))
                elif n == 1:
                    for e, c in two:
                        pe.wait_ge(vec_done, C.at(f"{t}.ga{2 * pair + 1}", i))
                        pe.wait_ge(pool_done, C.at(f"{t}.dt{c}", i))
                        four(IB[e][0], XTR[c], NB[e][0])
                        four(IB[e][1], NB[e][0], XTR[c]).then_inc(pe_done, C.mark(pe_done, f"{t}.d2{c}"))
                elif n == 2:
                    for e, c in two:
                        pe.wait_ge(vec_done, C.at(f"{t}.u2{c}", i))
                        pe.wait_ge(act_done, C.at(f"{t}.d2t{c}", i))
                        four(IB[e][0], XTR[c], NB[e][4])
                        four(IB[e][1], NB[e][2], NB[e][3]).then_inc(pe_done, C.mark(pe_done, f"{t}.x1{c}"))
                elif n == 3:
                    for e, c in two:
                        pe.wait_ge(vec_done, C.at(f"{t}.x1v{c}", i))
                        pe.wait_ge(act_done, C.at(f"{t}.d4{c}", i))
                        four(IB[e][0], NB[e][3], NB[e][0]).then_inc(pe_done, C.mark(pe_done, f"{t}.x2{c}"))
                elif n % 2 == 0:
                    m = (n - 4) // 2
                    for e, c in two:
                        pe.wait_ge(vec_done, C.at(f"{t}.xv{m}{c}", i))
                        x = NB[e][2 + m % 2]
                        for q in range(4):
                            qs = slice(q * P, (q + 1) * P)
                            mm = pe.transpose(PS[:, IB[e][1], qs], x[:, qs], const("ident"))
                        mm.then_inc(pe_done, C.mark(pe_done, f"{t}.tr{m}{c}"))
                        pe.wait_ge(pool_done, C.at(f"{t}.o{m}{c}", i))
                        four(IB[e][0], NB[e][5 - m % 2], x).then_inc(pe_done, C.mark(pe_done, f"{t}.yy{m}{c}"))
                else:
                    m = (n - 5) // 2
                    for e, c in two:
                        pe.wait_ge(vec_done, C.at(f"{t}.yv{m}{c}", i))
                        pe.wait_ge(act_done, C.at(f"{t}.xt{m}{c}", i))
                        mm = four(IB[e][0], *((XTR[c], NB[e][0]) if m < 3 else (NB[e][0], XTR[c])))
                        mm.then_inc(pe_done, C.mark(pe_done, f"{t}.xx{m}{c}"))

            def chunk(i, tile, t, c, n):
                hd = [(h, d, ORDER[d][c], slice(64 * h, 64 * h + 64)) for h in range(2) for d in range(2)]
                if n == 0:
                    pe.wait_ge(vec_done, C.at(f"{t}." + {0: "gm3", 2: "xf3"}.get(c, f"y{c - 1}"), i))
                    for h, d, ch, hs in hd:
                        o = PS[:, h, 64 * d:64 * d + 64]
                        if c:
                            pe.matmul(o, AR[hs, d, 0, ch * P:(ch + 1) * P], STR[hs, d, :], start=True, stop=False)
                        mm = pe.matmul(o, GM2[c][h][:, d, 0, :], VTK[:, ch, hs], start=c == 0, stop=True)
                    mm.then_inc(pe_done, C.mark(pe_done, f"{t}.w{c}"))
                elif n == 1:
                    pe.wait_ge(act_done, C.at(f"{t}.ws{c}", i))
                    for h, d, ch, hs in hd:
                        q = 2 * h + d
                        mm = pe.matmul(PS[:, 2, 64 * q:64 * q + 64], XTR[c][:, q * P:(q + 1) * P], WS[:, h, d, :],
                                       start=True, stop=True)
                    mm.then_inc(pe_done, C.mark(pe_done, f"{t}.u{c}"))
                else:
                    pe.wait_ge(vec_done, C.at(f"{t}.us{c}", i))
                    for h, d, ch, hs in hd:
                        if c < NCH - 1:
                            o = PS[hs, 3, 64 * d:64 * d + 64]
                            pe.matmul(o, KBT[:, d, ch, hs], VTK[:, ch, hs], start=True, stop=False)
                            pe.matmul(o, BNT[:, d, ch, hs], US[:, h, d, :], start=False, stop=True)
                        o = PS[hs, h, d * P:(d + 1) * P]
                        pe.matmul(o, VTK[:, ch, hs], GM2[c][h][:, d, 1, :], start=True, stop=False)
                        if c:
                            pe.matmul(o, STR[hs, d, :], AR[hs, d, 1, ch * P:(ch + 1) * P], start=False, stop=False)
                        mm = pe.matmul(o, US[:, h, d, :], GM1[c][h][:, d, 1, :], start=False, stop=True)
                    mm.then_inc(pe_done, C.mark(pe_done, f"{t}.yp{c}"))

            def turn(i, tile, t, n):
                if n == 0:
                    pe.wait_ge(vec_done, C.at(f"{t}.gm1", i))
                    srcs = ((0, SD[:, 0]), (1, SD[:, 1]), (2, AD[:, 0]), (3, AD[:, 1]))
                else:
                    pe.wait_ge(act_done, C.at(f"{t}.t2e", i))
                    pe.matmul(PS[:, 1, :], const("blk"), BS, start=True, stop=True).then_inc(
                        pe_done, C.mark(pe_done, f"{t}.bs"))
                    srcs = ((0, YT),)
                for bank, src in srcs:
                    for c in range(NCH):
                        mm = pe.transpose(PS[:, bank, c * P:(c + 1) * P], src[:, c * P:(c + 1) * P], const("ident"))
                    mm.then_inc(pe_done, C.mark(pe_done, f"{t}.t{n}{bank}"))

            def stage(i, tile, t, n):
                if n == 0:
                    if not t.endswith("p"):
                        pe.wait_ge(vec_done, C.at(f"{t}.xf3", i))
                    pe.wait_ge(side_loaded[3], C.at(f"{t}.s2", i))
                    for d in range(2):
                        ds = slice(64 * d, 64 * d + 64)
                        mm = pe.matmul(PS[:, 4 + d, :], W2S[ds, :], TH[ds, :], start=True, stop=True)
                    mm.then_inc(pe_done, C.mark(pe_done, f"{t}.pw"))
                elif n == 1:
                    pe.wait_ge(act_done, C.at(f"{t}.s1", i))
                    for d in range(2):
                        ds = slice(64 * d, 64 * d + 64)
                        mm = pe.matmul(PS[:, 4 + d, :], A2S[ds, :], AL[ds, :], start=True, stop=True)
                    mm.then_inc(w2_used, C.mark(w2_used, f"{t}.wa"))
                elif n == 2:
                    pe.wait_ge(act_done, C.at(f"{t}.sa", i))
                    pe.matmul(PS[:, 4, :], const("blk"), KK, start=True, stop=True).then_inc(
                        pe_done, C.mark(pe_done, f"{t}.kks"))

            steps = {"I": invert, "C": chunk, "T": turn, "S": stage}

            def trip(i, tile, t, staging):
                play(steps, i, tile, t, staging)
                pe.wait_ge(vec_done, C.at(f"{t}.y3", i))
                pe.matmul(PS[:, 0, :], const("cent"), YT, start=True, stop=True).then_inc(
                    pe_done, C.mark(pe_done, f"{t}.ce"))
                pe.wait_ge(g2_loaded, C.at(f"{t}.g2", i))
                pe.matmul(PS[:, 2, :], G2S, GS, start=True, stop=True)
                pe.wait_ge(act_done, C.at(f"{t}.ysq", i))
                pe.matmul(PS[:, 1, :], const("blkmean"), NB[0][0], start=True, stop=True).then_inc(
                    pe_done, C.mark(pe_done, f"{t}.post"))

            for n in range(3):
                stage(None, 0, f"{t0}p", n)
            with C.loop(pe, f"{t0}b", KD - 1) as i:
                trip(i, i, f"{t0}b", True)
            trip(None, KD - 1, f"{t0}z", False)
            pe.wait_ge(vec_done, C.at(f"{t0}z.out"))
            proj_pe(f"mo{l}", lambda k: RKV[:, 0, k, lo:T], 1, lo)
            leave((pe_done, w_used), f"mix{l}")

        def rwkv_act(l, lo):
            t0 = f"r{l}"
            enter(act, (act_done,), f"n1{l}")
            for n, (name, m) in enumerate(MIXES):
                with C.loop(act, t0 + name, 4) as i:
                    for q in range(2):
                        act.wait_ge(w_used, C.at(f"{t0}.{name}{q}.used", i))
                        s(act.activation(RKV[:, n, i * 2 + q, :], PS[:, q, :], ACT.Copy), f"{t0}.{name}e{q}", i)
            for n, (dst, func) in enumerate(((TH, ACT.Tanh), (AL, ACT.Copy), (GS, ACT.Sigmoid))):
                name = LORA[n][0]
                act.wait_ge(w_used, C.at(f"{t0}.{name}.used"))
                s(act.activation(dst, PS[:, 2 + n, :], func), f"{t0}.{name}e")

            def invert(i, tile, t, pair, n):
                two = [(e, 2 * pair + e) for e in range(2)]
                cp = lambda dst, e, k, label: s(act.activation(dst, PS[:, IB[e][k], :], ACT.Copy), label, i)
                for e, c in two:
                    if n == 1:
                        act.wait_ge(pe_done, C.at(f"{t}.d2{c}", i))
                        cp(NB[e][3], e, 1, f"{t}.d2t{c}")
                    elif n == 2:
                        act.wait_ge(pe_done, C.at(f"{t}.x1{c}", i))
                        cp(NB[e][3], e, 1, f"{t}.d4{c}")
                    elif n >= 4 and n % 2 == 0:
                        m = (n - 4) // 2
                        act.wait_ge(pe_done, C.at(f"{t}.tr{m}{c}", i))
                        cp(XTR[c], e, 1, f"{t}.xt{m}{c}")

            def chunk(i, tile, t, c, n):
                if n == 0:
                    act.wait_ge(pe_done, C.at(f"{t}.w{c}", i))
                    s(act.activation(WS[:, :, :, :].rearrange("p h d f -> p h (d f)"), PS[:, 0:2, 0:P], ACT.Copy),
                      f"{t}.ws{c}", i)

            def turn(i, tile, t, n):
                if n == 0:
                    for bank, dst in enumerate((KBT[:, 0], KBT[:, 1], BNT[:, 0], BNT[:, 1])):
                        act.wait_ge(pe_done, C.at(f"{t}.t0{bank}", i))
                        s(act.activation(dst.rearrange("p c f -> p (c f)"), PS[:, bank, :], ACT.Copy),
                          {1: f"{t}.t2e", 3: f"{t}.t4e"}.get(bank), i)
                else:
                    act.wait_ge(pe_done, C.at(f"{t}.t10", i))
                    s(act.activation(VTK[:, :, :].rearrange("p c f -> p (c f)"), PS[:, 0, :], ACT.Copy),
                      f"{t}.vt", i)

            def stage(i, tile, t, n):
                if n == 0:
                    act.wait_ge(vec_done, C.at(f"{t}.kf", i))
                    s(act.activation(KK, KF, ACT.Square), f"{t}.kk2", i)
                elif n == 1:
                    act.wait_ge(pe_done, C.at(f"{t}.pw", i))
                    for d in range(2):
                        s(act.activation(SD[:, d, :], PS[:, 4 + d, :], ACT.Sigmoid, bias=PCN[:, d:d + 1]),
                          f"{t}.s{d}", i)
                elif n == 2:
                    act.wait_ge(w2_used, C.at(f"{t}.wa", i))
                    for d in range(2):
                        s(act.activation(AD[:, d, :], PS[:, 4 + d, :], ACT.Sigmoid, bias=PCN[:, 2 + d:3 + d]),
                          f"{t}.sa" if d else None, i)
                elif n == 3:
                    act.wait_ge(pe_done, C.at(f"{t}.kks", i))
                    s(act.activation(KK, PS[:, 4, :], ACT.Ln, bias=MC[:, 4:5]), None, i)
                    s(act.activation(KK, KK, ACT.Exp, scale=-0.5), None, i)
                elif n == 4:
                    act.wait_ge(vec_done, C.at(f"{t}.sums", i))
                    s(act.activation(PN[:, :, :], ARS[:, :, 1, :], ACT.Exp, scale=LOG_W, bias=MC[:, 3:4]), None, i)
                    for d in range(2):
                        ends = ARS[:, d, 1, :].rearrange("p (c t) -> p c t", c=NCH)[:, :, END_R[d]]
                        s(act.activation(PCTS[:, d, :], ends, ACT.Exp, scale=-LOG_W), None, i)
                    act.activation(ARS[:, :, :, :], ARS[:, :, :, :], ACT.Exp, scale=-LOG_W, bias=MC[:, 2:3]).then_inc(
                        staged, C.mark(staged, f"{t}.staged"))
                    act.wait_ge(staged, C.at(f"{t}.staged", i))

            steps = {"I": invert, "C": chunk, "T": turn, "S": stage}

            def trip(i, tile, t, staging):
                act.wait_ge(vec_done, C.at(f"{t}.prod1", i))
                s(act.activation(YT, RKV[:, 2, tile, :], ACT.Copy), f"{t}.vc", i)
                play(steps, i, tile, t, staging)
                act.wait_ge(pe_done, C.at(f"{t}.ce", i))
                s(act.activation(NB[0][0], PS[:, 0, :], ACT.Square), f"{t}.ysq", i)
                act.wait_ge(pe_done, C.at(f"{t}.post", i))
                s(act.activation(NB[0][2], PS[:, 1, :], ACT.Ln, bias=MC[:, 1:2]), None, i)
                s(act.activation(NB[0][2], NB[0][2], ACT.Exp, scale=-0.5), f"{t}.ry", i)

            for n in range(5):
                stage(None, 0, f"{t0}p", n)
            with C.loop(act, f"{t0}b", KD - 1) as i:
                trip(i, i, f"{t0}b", True)
            trip(None, KD - 1, f"{t0}z", False)
            leave((act_done,), f"mix{l}")

        def rwkv_pool(l):
            t0 = f"r{l}"
            if l == 0:
                enter(pool, (pool_done,), f"n1{l}")
                for n, (name, m) in enumerate(MIXES):
                    with C.loop(pool, t0 + name, 4) as i:
                        for slot in range(2):
                            ride_pool(t0 + name, 0, i, slot, i * 2 + (24 + 8 * n + slot))

            def kept(i, c, dst, mask, label):
                for h in range(2):
                    g(pool.tensor_tensor(dst[:, 256 * h:256 * h + 256].rearrange("p (q t) -> p q t", q=2),
                                         GM1[c][h][:, :, 0, :], const(mask).unsqueeze(1).broadcast_to([P, 2, P]),
                                         ALU.mult), label if h else None, i)

            def trip(i, t):
                pool.wait_ge(vec_done, C.at(f"{t}.kkn", i))
                g(pool.tensor_tensor(AR[:, :, 0, :], ARS[:, :, 0, :], KK.unsqueeze(1).broadcast_to([P, 2, T]),
                                     ALU.mult), f"{t}.ar0", i)
                for pair in range(2):
                    two = [(e, 2 * pair + e) for e in range(2)]
                    for e, c in two:
                        pool.wait_ge(vec_done, C.at(f"{t}.ga{c}", i))
                        kept(i, c, XTR[c], "mask8", f"{t}.dt{c}")
                    for e, c in two:
                        kept(i, c, NB[e][5], LEVELS[0], f"{t}.o0{c}")
                    for n in range(1, 4):
                        for e, c in two:
                            pool.wait_ge(pe_done, C.at(f"{t}.x1{c}" if n == 1 else f"{t}.yy{n - 2}{c}", i))
                            if n == 1:
                                pool.wait_ge(vec_done, C.at(f"{t}.x1v{c}", i))
                            kept(i, c, NB[e][5 - n % 2], LEVELS[n], f"{t}.o{n}{c}")

            with C.loop(pool, f"{t0}b", KD - 1) as i:
                trip(i, f"{t0}b")
            trip(None, f"{t0}z")
            leave((pool_done,), f"mix{l}")

        def rwkv_vec(l, lo):
            j, t0 = l // 3, f"r{l}"
            B = B_RW + j
            enter(vec, (vec_done,), f"n1{l}")
            h2 = H[:, :].rearrange("p (n t) -> p n t", t=SEG)
            d2 = BIG[:, 16384:20480].rearrange("p (n t) -> p n t", t=SEG)
            v(vec.tensor_tensor(d2[:, :, 1:SEG - 1], h2[:, :, 0:SEG - 2], h2[:, :, 2:SEG], ALU.add))
            v(vec.tensor_copy(d2[:, :, 0:1], h2[:, :, 1:2]))
            v(vec.tensor_copy(d2[:, :, SEG - 1:SEG], h2[:, :, SEG - 2:SEG - 1]))
            v(vec.scalar_tensor_tensor(d2[:, :, :], d2[:, :, :], 0.5, h2[:, :, :], ALU.mult, ALU.subtract))
            last = None
            for name, m in MIXES + LORA:
                if last:
                    vec.wait_ge(w_used, C.at(last))
                for k in range(KD):
                    v(vec.scalar_tensor_tensor(XM[:, k, :], DX[:, k, :], columns(B, 8 * m + k, 1), Hk[:, k, :],
                                               ALU.mult, ALU.add), f"{t0}.mix{m}" if k == KD - 1 else None)
                if l == 0 and (name, m) in MIXES:
                    with C.loop(vec, t0 + name, 4) as i:
                        ride_vec(t0 + name, 0, i, i * 2 + (24 + 8 * MIXES.index((name, m))), 2)
                    if name == "v":
                        norm_gain(0, 1)
                last = f"{t0}.{name}1.used" if (name, m) in MIXES else f"{t0}.{name}.used"
            vec.wait_ge(act_done, C.at(f"{t0}.ge"))
            vec.wait_ge(w_used, C.at(last))
            both = lambda ap: ap.unsqueeze(1).broadcast_to([P, 2, T])

            def invert(i, tile, t, pair, n):
                two = [(e, 2 * pair + e) for e in range(2)]
                bank = lambda e, k: PS[:, IB[e][k], :]
                flat = lambda ap: ap.rearrange("p d n t -> p (d n t)")
                if n == 0:
                    for e, c in two:
                        b1, b2 = ((0, 1), (2, 3)) if e == 0 else ((6, 7), (0, 1))
                        vec.wait_ge(pe_done, C.at(f"{t}.g1{c}", i))
                        for h in range(2):
                            v(vec.tensor_tensor(flat(GM1[c][h]), PS[:, b1[h], :], const("gs0", 4), ALU.mult), None, i)
                        vec.wait_ge(pe_done, C.at(f"{t}.gt{c}", i))
                        for h in range(2):
                            v(vec.tensor_tensor(NB[e][0][:, 256 * h:256 * h + 256], PS[:, 4 + h, 0:256],
                                                const("gt0", 2), ALU.mult), f"{t}.ga{c}" if h else None, i)
                        vec.wait_ge(pe_done, C.at(f"{t}.g2{c}", i))
                        for h in range(2):
                            v(vec.tensor_tensor(flat(GM2[c][h]), PS[:, b2[h], :], const("gs0", 4), ALU.mult),
                              f"{t}.gm{c}" if h else None, i)
                for e, c in two:
                    if n == 1:
                        vec.wait_ge(pe_done, C.at(f"{t}.d2{c}", i))
                        v(vec.tensor_copy(NB[e][2], bank(e, 0)), None, i)
                        v(vec.tensor_tensor(quad(NB[e][4]), quad(NB[e][2]),
                                            const("ident").unsqueeze(1).broadcast_to([P, 4, P]), ALU.add),
                          f"{t}.u2{c}", i)
                    elif n == 2:
                        vec.wait_ge(pe_done, C.at(f"{t}.x1{c}", i))
                        v(vec.tensor_tensor(NB[e][0], bank(e, 0), NB[e][4], ALU.add), f"{t}.x1v{c}", i)
                    elif n == 3:
                        vec.wait_ge(pe_done, C.at(f"{t}.x2{c}", i))
                        v(vec.tensor_tensor(NB[e][2], bank(e, 0), NB[e][0], ALU.add), f"{t}.xv0{c}", i)
                    elif n >= 4 and n % 2 == 0:
                        m = (n - 4) // 2
                        vec.wait_ge(pe_done, C.at(f"{t}.yy{m}{c}", i))
                        v(vec.tensor_copy(NB[e][0], bank(e, 0)), f"{t}.yv{m}{c}", i)
                    elif n >= 5:
                        m = (n - 5) // 2
                        vec.wait_ge(pe_done, C.at(f"{t}.xx{m}{c}", i))
                        if m < 3:
                            v(vec.tensor_tensor(NB[e][2 + (m + 1) % 2], bank(e, 0), NB[e][2 + m % 2], ALU.add),
                              f"{t}.xv{m + 1}{c}", i)
                        else:
                            v(vec.tensor_tensor(XTR[c], bank(e, 0), XTR[c], ALU.add), f"{t}.xf{c}", i)

            def chunk(i, tile, t, c, n):
                if n == 1:
                    vec.wait_ge(pe_done, C.at(f"{t}.u{c}", i))
                    v(vec.tensor_copy(US[:, :, :, :].rearrange("p h d f -> p (h d f)"), PS[:, 2, 0:256]),
                      f"{t}.us{c}", i)
                if n < 2:
                    return
                vec.wait_ge(pe_done, C.at(f"{t}.yp{c}", i))
                if c < NCH - 1:
                    s3 = PS[:, 3, 0:P].rearrange("p (d f) -> p d f", d=2)
                    if c:
                        v(vec.tensor_tensor(STR[:, :, :], STR[:, :, :], s3, ALU.add), None, i)
                    for d in range(2):
                        ch = ORDER[d][c]
                        v(vec.tensor_scalar(STR[:, d, :], STR[:, d, :] if c else s3[:, d, :], PCT[:, d, ch:ch + 1],
                                            None, ALU.mult), None, i)
                for h in range(2):
                    hs = slice(64 * h, 64 * h + 64)
                    for d in range(2):
                        ch = ORDER[d][c]
                        y, ps = YT[hs, ch * P:(ch + 1) * P], PS[hs, h, d * P:(d + 1) * P]
                        label = f"{t}.y{c}" if (h, d) == (1, 1) else None
                        if c % 2 == 0:
                            v(vec.tensor_copy(y, ps), label, i)
                        else:
                            v(vec.tensor_tensor(y, y, ps, ALU.add), label, i)

            def turn(i, tile, t, n):
                if n == 1:
                    vec.wait_ge(pe_done, C.at(f"{t}.bs", i))
                    v(vec.tensor_tensor(BV, RKV[:, 2, tile, :], PS[:, 1, :], ALU.mult), f"{t}.bv", i)

            def stage(i, tile, t, n):
                if n == 0:
                    nxt = tile if t.endswith("p") else tile + 1
                    v(vec.tensor_copy(PCN[:, 0:9], columns(B, 48, 72).rearrange("p (n c) -> p n c", c=8)[:, :, nxt]),
                      None, i)
                    v(vec.tensor_scalar(PCN[:, 9:10], PCN[:, 5:6], -1.0, 1.0, ALU.mult, ALU.add), None, i)
                    v(vec.tensor_scalar(KF, RKV[:, 1, nxt, :], PCN[:, 4:5], None, ALU.mult), f"{t}.kf", i)
                elif n == 2:
                    for d in range(2):
                        vec.wait_ge(act_done, C.at(f"{t}.s{d}", i))
                        for c in range(NCH):
                            cs = slice(c * P, (c + 1) * P)
                            v(vec.tensor_tensor_scan(ARS[:, d, 1, cs], const("ones"), SD[:, d, cs], 0.0, ALU.mult,
                                                     ALU.add), None, i)
                    v(vec.tensor_tensor(ARS[:, 0, 0, :], ARS[:, 0, 1, :], SD[:, 0, :], ALU.subtract), None, i)
                    c4 = lambda ap: ap.rearrange("p (c t) -> p c t", c=NCH)
                    v(vec.tensor_tensor(c4(ARS[:, 1, 0, :]), c4(ARS[:, 1, 1, :])[:, :, P - 1:P].broadcast_to([P, NCH, P]),
                                        c4(ARS[:, 1, 1, :]), ALU.subtract), None, i)
                    v(vec.tensor_tensor(ARS[:, 1, 1, :], ARS[:, 1, 0, :], SD[:, 1, :], ALU.add), f"{t}.sums", i)

            steps = {"I": invert, "C": chunk, "T": turn, "S": stage}

            def trip(i, tile, t, staging):
                vec.wait_ge(staged, C.at(f"{t0}b.staged", i, 1) if i is not None else C.at(f"{t0}b.staged"))
                v(vec.tensor_copy(PC, PCN), None, i)
                v(vec.tensor_copy(PCT[:, :, :], PCTS[:, :, :]), None, i)
                v(vec.tensor_tensor(KK, KK, KF, ALU.mult), f"{t}.kkn", i)
                v(vec.tensor_scalar(SD[:, :, :], AD[:, :, :], PC[:, 5:6], PC[:, 9:10], ALU.mult, ALU.add), None, i)
                v(vec.tensor_tensor(AD[:, :, :], AD[:, :, :], both(KK), ALU.mult), None, i)
                v(vec.scalar_tensor_tensor(AD[:, :, :], AD[:, :, :], -1.0, PN[:, :, :], ALU.mult, ALU.mult), None, i)
                v(vec.tensor_tensor(AR[:, :, 1, :], ARS[:, :, 1, :], both(RKV[:, 0, tile, :]), ALU.mult),
                  f"{t}.prod1", i)
                v(vec.tensor_tensor(SD[:, :, :], SD[:, :, :], both(RKV[:, 1, tile, :]), ALU.mult), None, i)
                v(vec.tensor_tensor(BS, SD[:, 0, :], SD[:, 1, :], ALU.add), None, i)
                v(vec.tensor_tensor(SD[:, :, :], SD[:, :, :], PN[:, :, :], ALU.mult), f"{t}.prod", i)
                v(vec.scalar_tensor_tensor(BS, BS, PC[:, 6:7], RKV[:, 0, tile, :], ALU.mult, ALU.mult), None, i)
                play(steps, i, tile, t, staging)
                vec.wait_ge(act_done, C.at(f"{t}.ry", i))
                v(vec.tensor_tensor(YT, NB[0][2], PS[:, 0, :], ALU.mult), None, i)
                v(vec.tensor_scalar(YT, YT, PC[:, 7:8], PC[:, 8:9], ALU.mult, ALU.add), None, i)
                v(vec.tensor_tensor(YT, YT, BV, ALU.add), None, i)
                v(vec.tensor_tensor(RKV[:, 0, tile, :], YT, PS[:, 2, :], ALU.mult), f"{t}.out", i)

            stage(None, 0, f"{t0}p", 0)
            stage(None, 0, f"{t0}p", 2)
            with C.loop(vec, f"{t0}b", KD - 1) as i:
                trip(i, i, f"{t0}b", True)
            trip(None, KD - 1, f"{t0}z", False)
            proj_vec(f"mo{l}", l, 1, lo)
            leave((vec_done,), f"mix{l}")

        MIX = {}
        MIX[2] = {'sp': attn_sp, 'pe': attn_pe, 'act': attn_act, 'vec': attn_vec, 'pool': attn_pool}
        MIX[1] = {'sp': ssd_sp, 'pe': ssd_pe, 'act': ssd_act, 'vec': ssd_vec, 'pool': ssd_pool}
        MIX[0] = MIX[3] = {'sp': rwkv_sp, 'pe': rwkv_pe, 'act': rwkv_act, 'vec': rwkv_vec, 'pool': rwkv_pool}
        MIX = {n: m for n, m in MIX.items() if n in only}


        block = ctx.enter_context(nc.Block())
        kinds = ["rwkv", "ssd", "attn", "rwkv"]

        def los(l):
            return SEG if l == DEPTH - 1 else 0

        def before(l):
            return "ada" if l == list(layers)[0] else f"ffn{l - 1}"

        @block.sync
        def _(sp):
            start_sp()
            ada_sp()
            for l in layers:
                if mixers and l in MIX:
                    MIX[l]["sp"](l)
                ffn_sp(l)
            end_sp()

        @block.gpsimd
        def _(pool):
            for l in layers:
                if mixers and l in MIX and "pool" in MIX[l]:
                    MIX[l]["pool"](l)
                ffn_pool(l, f"mix{l}" if mixers and l in MIX else before(l))

        @block.tensor
        def _(pe):
            start_pe()
            ada_pe()
            for l in layers:
                if mixers and l in MIX:
                    norm_pe(f"n1{l}", before(l), 0)
                    MIX[l]["pe"](l, los(l))
                norm_pe(f"n2{l}", f"mix{l}" if mixers and l in MIX else before(l), los(l))
                ffn_pe(l, los(l))
            norm_pe("nf", f"ffn{list(layers)[-1]}", SEG)
            end_pe("nf")

        @block.scalar
        def _(act):
            start_act()
            for l in layers:
                if mixers and l in MIX:
                    norm_act(f"n1{l}", before(l), 0, 2 * l, mod_shift(l, 0))
                    MIX[l]["act"](l, los(l))
                norm_act(f"n2{l}", f"mix{l}" if mixers and l in MIX else before(l), los(l), 2 * l + 1, mod_shift(l, 1))
                ffn_act(l, los(l))
            norm_act("nf", f"ffn{list(layers)[-1]}", SEG, 2 * DEPTH, lambda k, n: MS[:, 2 * DEPTH, k, 0:1])
            end_act("nf")

        @block.vector
        def _(vec):
            start_vec()
            ada_vec()
            for l in layers:
                if mixers and l in MIX:
                    norm_vec(f"n1{l}", before(l), 0)
                    MIX[l]["vec"](l, los(l))
                norm_vec(f"n2{l}", f"mix{l}" if mixers and l in MIX else before(l), los(l))
                ffn_vec(l, los(l))
            norm_vec("nf", f"ffn{list(layers)[-1]}", SEG)
    return C


_INS = ['x', 'c', 'ctx', 'c_ctx', 'ada_w', 'ada_b', 'norm1_g', 'norm2_g', 'ffn_w_in', 'ffn_conv', 'ffn_w_out',
        'final_g', 'rw_mu', 'rw_wr', 'rw_wk', 'rw_wv', 'rw_wo', 'rw_w0', 'rw_w1', 'rw_w2', 'rw_a0', 'rw_a1', 'rw_a2',
        'rw_g1', 'rw_g2', 'rw_kk', 'rw_ka', 'rw_rk', 'rw_ln_g', 'rw_ln_b', 'ssd_w_in', 'ssd_conv_w', 'ssd_conv_b',
        'ssd_dt_bias', 'ssd_a_log', 'ssd_d', 'ssd_norm_g', 'ssd_w_out', 'at_w_qkv', 'at_w_o', 'at_sink']


def shape_constants():
    import numpy as np
    f = np.float32
    r, c = np.arange(P)[:, None], np.arange(P)[None, :]
    same = lambda n: (r // n == c // n).astype(f)
    level = lambda n: ((r // (2 * n) == c // (2 * n)) & (r // n != c // n)).astype(f)
    m = {"ident": np.eye(P, dtype=f), "mean": np.full((P, P), 1.0 / D, f), "blk": same(64),
         "cent": np.eye(P, dtype=f) - same(64) / 64, "blkmean": same(64) / 64, "ones": np.ones((P, P), f),
         "mean256": np.full((P, P), 1.0 / 256, f),
         "mask8": same(8), "lev8": level(8), "lev16": level(16), "lev32": level(32), "lev64": level(64),
         "gs0": (r < c).astype(f), "gi0": (r <= c).astype(f), "gs1": (r > c).astype(f), "gi1": (r >= c).astype(f),
         "gt0": (r > c) * same(8), "gt1": (r < c) * same(8)}
    consts = np.concatenate([m[n] for n in CONST], 1)

    inv = (f(10000.0) ** (-np.arange(0, 32, 2, dtype=f) / f(32))).astype(f)
    tok = np.arange(SEQ)
    p = np.arange(P)
    pos = np.where((p % 64)[:, None] < 32, (tok // 64)[None, :], (tok % 64)[None, :]).astype(f)
    ang = (pos * inv[p % 16][:, None]).astype(f)
    cos, sin = np.cos(ang).astype(f), np.sin(ang).astype(f)
    rot = np.zeros((P, P), f)
    for q in range(P):
        if q % 32 < 16:
            rot[q + 16, q] = -1.0
        else:
            rot[q - 16, q] = 1.0
    dup = [np.zeros((P, P), f) for _ in range(2)]
    for h in range(2):
        for q in range(P):
            dup[h][64 * h + q % 64, q] = 1.0
    am = []
    for b in range(2):
        q = b * P + np.arange(P)[:, None]
        k = np.arange(SEQ)[None, :]
        am.append(np.where(np.abs(q - k) <= 128, f(0), f(NEG)))
    attn = np.concatenate([cos, sin, rot, dup[0], dup[1], rot @ dup[0], rot @ dup[1], am[0], am[1]], 1).astype(f)
    return consts, attn, dup, rot


def kernel(**inputs):
    import numpy as _np
    import concourse.bacc as _bacc
    from concourse import mybir as _mybir
    from concourse.bass_utils import run_bass_kernel_spmd as _run

    consts, attn, _, _ = shape_constants()
    extra = {"consts": consts, "attn_consts": attn}

    def build(draft):
        nc = _bacc.Bacc("TRN2", target_bir_lowering=False, num_devices=1)
        arrays, args = {}, {}
        for name in _INS + list(extra):
            arr = _np.ascontiguousarray(extra[name] if name in extra else inputs[name])
            arrays[f"in_{name}_dram"] = arr
            args[name] = nc.dram_tensor(f"in_{name}_dram", arr.shape, _mybir.dt.from_np(arr.dtype),
                                        kind="ExternalInput").ap()
        out = nc.dram_tensor("out_0_dram", (1, SEQ, D), F32, kind="ExternalOutput").ap()
        scratch = nc.dram_tensor("scratch_dram", (64, T), F32, kind="Internal").ap()
        counts = program(nc, args, out, draft, scratch, **OPTIONS)
        return nc, arrays, counts

    _, _, draft = build(None)
    nc, arrays, _ = build(draft)
    r = _run(nc, [arrays], core_ids=[0])
    return r.results[0]["out_0_dram"]


OPTIONS = {}
```

```python
from contextlib import ExitStack, contextmanager

import concourse.bass as bass
from concourse import mybir

P = 128
D = 1024
KD = D // P
CTX = 256
SEQ = 256
T = CTX + SEQ
SEG = 256
NCH = T // P
DEPTH = 4
F = 2816
NF = F // P
NMOD = 6 * D // P
EPS = 1e-6
WORK_N = 18400
GN_EPS = 64e-5
KK_EPS = 1e-12
LEAD = 256
LOG_W = 0.6065306597126334
MID = 38.8
INNER = 2048
NEG = -1.0e30
ORDER = [[0, 1, 2, 3], [1, 0, 3, 2]]

F32 = mybir.dt.float32
ACT = mybir.ActivationFunctionType
ALU = mybir.AluOpType
AX_X = mybir.AxisListType.X

CONST = ["ident", "mean", "blk", "cent", "blkmean", "ones", "mask8", "lev8", "lev16", "lev32", "lev64",
         "gs0", "gi0", "gs1", "gi1", "gt0", "gt1", "mean256"]
ATTN_CONST = ["cos0", "cos1", "sin0", "sin1", "rot", "dup0", "dup1", "duprot0", "duprot1",
              "am00", "am01", "am10", "am11"]


class Counts:

    def __init__(self, draft=None):
        self.draft = draft
        self.now, self.marks, self.loops, self.ends, self.loop_name = {}, {}, {}, {}, None

    def mark(self, sem, label, n=1):
        name = getname(sem)
        self.now[name] = self.now.get(name, 0) + n
        assert label is None or label not in self.marks, label
        if label is not None:
            self.marks[label] = (name, self.now[name], self.loop_name)
        return n

    def at(self, label, i=None, back=0):
        if self.draft is None:
            return 1
        name, value, loop = self.draft.marks[label]
        if loop is None:
            return value
        step, trips = self.draft.loops[loop][name]
        if i is None:
            return value + (trips - 1) * step
        value -= back * step
        assert value >= 1, (label, value)
        return i * step + value

    def here(self, sem, i=None):
        name = getname(sem)
        value = self.now.get(name, 0)
        if self.draft is None:
            return 1
        if self.loop_name is None:
            return value
        step, _ = self.draft.loops[self.loop_name][name]
        return i * step + value

    def end(self, sem, stage):
        self.ends[(getname(sem), stage)] = self.now.get(getname(sem), 0)

    def ended(self, sem, stage):
        return 1 if self.draft is None else self.draft.ends.get((getname(sem), stage), 0)

    @contextmanager
    def loop(self, eng, name, trips):
        before = dict(self.now)
        self.loop_name = name
        with eng.Fori(0, trips) as i:
            yield i
        self.loop_name = None
        for sem, v in list(self.now.items()):
            step = v - before.get(sem, 0)
            if step:
                self.loops.setdefault(name, {})[sem] = (step, trips)
                self.now[sem] = before.get(sem, 0) + trips * step


def getname(sem):
    return sem if isinstance(sem, str) else sem.name


def program(nc, a, out, draft, scratch, layers=range(DEPTH), mixers=True, only=range(DEPTH)):
    C = Counts(draft)
    ctx = ExitStack()
    with ctx:
        def sb(name, *shape):
            return ctx.enter_context(nc.sbuf_tensor(name, [P, *shape], F32))

        def sem(name):
            return ctx.enter_context(nc.semaphore(name))

        PS = ctx.enter_context(nc.psum_tensor("PS", [P, 8, 512], F32))
        X = sb("X", KD, T)
        H = sb("H", KD * T)
        Hk = H[:, :].rearrange("p (k t) -> p k t", k=KD)
        WR = sb("WR", 2, 8, P)
        BIG = sb("BIG", 20480)
        WORK = sb("WORK", WORK_N)
        K = sb("K", len(CONST) * P)
        PV = sb("PV", 1200)
        MOD = sb("MOD", DEPTH, NMOD, 2)
        MS = sb("MS", 2 * DEPTH + 1, KD, 2)
        MC = sb("MC", 5)
        SC = sb("SC", KD, 2)
        SEGS = (slice(0, SEG), slice(SEG, T))

        def const(name, n=1):
            c = CONST.index(name)
            return K[:, c * P:(c + n) * P]

        pe_done = sem("pe_done")
        w_used = sem("w_used")
        act_done = sem("act_done")
        vec_done = sem("vec_done")
        pool_done = sem("pool_done")
        w_loaded = [sem("w_loaded0"), sem("w_loaded1")]
        ada_loaded = [sem(f"ada_loaded{s}") for s in range(3)]
        ride_loaded = sem("ride_loaded")
        in_loaded = sem("in_loaded")
        vec_loaded = sem("vec_loaded")
        side_loaded = [sem(f"side_loaded{s}") for s in range(4)]
        stored = sem("stored")
        scratch_stored = sem("scratch_stored")
        g2_loaded = sem("g2_loaded")
        loads_started = sem("loads_started")
        staged = sem("staged")
        primed = sem("primed")
        kk_rows = sem("kk_rows")
        w2_used = sem("w2_used")
        PROGRESS = (pe_done, w_used, act_done, vec_done, pool_done)

        pe, act, vec, pool, sp = nc.tensor, nc.scalar, nc.vector, nc.gpsimd, nc.sync

        def enter(eng, own, stage):
            for s in PROGRESS:
                if s not in own and C.ended(s, stage) > 0:
                    eng.wait_ge(s, C.ended(s, stage))

        def leave(own, stage):
            for s in own:
                C.end(s, stage)

        def v(ins, label=None, i=None):
            ins.then_inc(vec_done, C.mark(vec_done, label))
            vec.wait_ge(vec_done, C.here(vec_done, i))

        def s(ins, label=None, i=None):
            ins.then_inc(act_done, C.mark(act_done, label))
            act.wait_ge(act_done, C.here(act_done, i))

        def g(ins, label=None, i=None):
            ins.then_inc(pool_done, C.mark(pool_done, label))
            pool.wait_ge(pool_done, C.here(pool_done, i))

        def load_unit(i, label, *parts):
            slot = C.now.get("unit", 0) % 2
            sp.wait_ge(w_used, C.here("unit", i) + 1)
            sp.sem_inc(loads_started, 1)
            C.mark("unit", None)
            for n, (dst, src) in enumerate(parts):
                last = n == len(parts) - 1
                sp.dma_start(dst(WR[:, slot]), src).then_inc(
                    w_loaded[slot], C.mark(w_loaded[slot], label if last else None, 16))

        def rows(w):
            return w.rearrange("(k p) n -> p k n", p=P)

        def unit(w, k0, nk, c0, nc_=P):
            return (lambda slot: slot[:, 0:nk, 0:nc_], w[:, k0:k0 + nk, bass.ds(c0, nc_)])

        def use_unit(i, label, outs, rhs, nk, first, last, m=P):
            slot = C.now.get("w_unit_pe", 0) % 2
            C.mark("w_unit_pe", None)
            pe.wait_ge(w_loaded[slot], C.at(label, i))
            for k in range(nk):
                mm = pe.matmul(outs, WR[:, slot, k, 0:m], rhs(k), start=first and k == 0, stop=last and k == nk - 1)
            mm.then_inc(w_used, C.mark(w_used, label + ".used"))

        ST = BIG[:, 0:17 * P].rearrange("p (b c) -> p b c", c=P)
        XIN = BIG[:, 4096:8192].rearrange("p (c d) -> p c d", d=D)

        flat1 = lambda ap: ap.rearrange("(r c) -> r c", c=P)
        flat2 = lambda ap: ap.rearrange("a (r c) -> (a r) c", c=P)
        blocks = []
        for l in range(DEPTH):
            blocks.append([flat1(a["ada_b"][l]), flat1(a["norm1_g"][l]), flat1(a["norm2_g"][l])]
                          + ([flat1(a["final_g"])] if l == 0 else []))
            conv = flat2(a["ffn_conv"][l])
            blocks += [[conv[0:66]], [conv[66:132]]]
        for j in range(2):
            blocks.append([flat2(a["rw_mu"][j]), flat2(a["rw_w0"][j]), flat2(a["rw_a0"][j]), flat1(a["rw_kk"][j]),
                           flat1(a["rw_ka"][j]), flat1(a["rw_rk"][j].rearrange("h n -> (h n)")),
                           flat1(a["rw_ln_g"][j]), flat1(a["rw_ln_b"][j])])
        blocks.append([flat2(a["ssd_conv_w"][0]), flat1(a["ssd_conv_b"][0])])
        blocks.append([flat1(a["ssd_norm_g"][0])])
        blocks.append([flat1(a["c_ctx"]), flat1(a["c"][0])])
        B_RW, B_SSD, B_SSDN, B_C = 12, 14, 15, 16
        nrows = [sum(x.shape[0] for x in b) for b in blocks]
        first_column = [sum(nrows[:b]) for b in range(len(blocks) + 1)]
        assert first_column[-1] <= 1200

        def columns(b, c0, n):
            return PV[:, bass.ds(c0 + first_column[b], n)]

        def start_sp():
            sp.dma_start(K[:, :], a["consts"]).then_inc(vec_loaded, C.mark(vec_loaded, "consts", 16))
            for b, parts in enumerate(blocks):
                r = 0
                for n, part in enumerate(parts):
                    sp.dma_start(ST[r:r + part.shape[0], b, :], part).then_inc(
                        vec_loaded, C.mark(vec_loaded, "params" if (b, n) == (16, len(parts) - 1) else None, 16))
                    r += part.shape[0]
            sp.dma_start(XIN[:, 0:2, :], a["ctx"][0].rearrange("(c p) d -> p c d", p=P)).then_inc(
                in_loaded, C.mark(in_loaded, None, 16))
            sp.dma_start(XIN[:, 2:4, :], a["x"][0].rearrange("(c p) d -> p c d", p=P)).then_inc(
                in_loaded, C.mark(in_loaded, "inputs", 16))

        def start_pe():
            pe.wait_ge(vec_loaded, C.at("params"))
            for b in range(17):
                mm = pe.transpose(PS[:, b // 4, (b % 4) * P:(b % 4) * P + nrows[b]], ST[0:nrows[b], b, :],
                                  const("ident")[0:nrows[b], 0:nrows[b]])
                if b == 0:
                    mm.then_inc(w_used, C.mark(w_used, None, 2))
                else:
                    mm.then_inc(pe_done, C.mark(pe_done, f"par{b}", LEAD if b == 1 else 1))
            pe.wait_ge(in_loaded, C.at("inputs"))
            for k in range(KD):
                bank = 5 + k % 3
                if k >= 3:
                    pe.wait_ge(act_done, C.at(f"x{k - 3}"))
                for c in range(NCH):
                    mm = pe.transpose(PS[:, bank, c * P:(c + 1) * P], XIN[:, c, k * P:(k + 1) * P], const("ident"))
                mm.then_inc(pe_done, C.mark(pe_done, f"xt{k}"))
            leave((pe_done, w_used), "start")

        def start_act():
            act.wait_ge(pe_done, C.at("par16"))
            act.wait_ge(vec_done, C.at("columns"))
            act.activation(SC[:, :, 0], columns(B_C, 0, KD), ACT.Silu).then_inc(act_done, C.mark(act_done, None, LEAD))
            s(act.activation(SC[:, :, 1], columns(B_C, KD, KD), ACT.Silu), "silu_c")
            for k in range(KD):
                act.wait_ge(pe_done, C.at(f"xt{k}"))
                s(act.activation(X[:, k, :], PS[:, 5 + k % 3, :], ACT.Copy), f"x{k}")
            leave((act_done,), "start")

        def start_vec():
            vec.memset(MC[:, :], 0.0).then_inc(vec_done, C.mark(vec_done, None, LEAD))
            vec.wait_ge(vec_done, LEAD)
            for n, value in enumerate((EPS, GN_EPS, MID, -MID, KK_EPS)):
                v(vec.memset(MC[:, n:n + 1], value))
            v(vec.memset(MS[:, :, :, :], 0.0))
            vec.wait_ge(w_used, 2)
            vec.wait_ge(pe_done, C.at("par16"))
            for b in range(17):
                v(vec.tensor_copy(columns(b, 0, nrows[b]), PS[:, b // 4, (b % 4) * P:(b % 4) * P + nrows[b]]),
                  "columns" if b == 16 else None)
            leave((vec_done,), "start")

        ADA = BIG[:, 0:12288].rearrange("p (s k c) -> p s k c", s=3, k=KD)
        AW = WORK[:, 4096:8192]
        ACC = WORK[:, 8192:10240].rearrange("p (b s c) -> p b s c", b=2, s=2)
        SS, XSQ = WORK[:, 12288:12800], WORK[:, 12800:13312]
        ABANK = 7

        def ada_sp():
            enter(sp, (), "start")
            w = rows(a["ada_w"][0])
            with C.loop(sp, "ada", 2) as i:
                for q in range(3):
                    sp.wait_ge(*((pe_done, C.at("ada.2", i, 1)) if q == 2 else (vec_done, C.at(f"ada.acc{q}", i, 1))))
                    sp.sem_inc(loads_started, 1)
                    sp.dma_start(ADA[:, q], w[:, :, bass.ds(i * 1536 + q * 512, 512)]).then_inc(
                        ada_loaded[q], C.mark(ada_loaded[q], f"ada.load{q}", 16))

        def over_inputs(acc, src, label, i):
            for s in range(2):
                for k in range(KD):
                    by = SC[:, k, s:s + 1]
                    if k == 0:
                        v(vec.tensor_scalar(acc[:, s], src(k), by, None, ALU.mult), None, i)
                    else:
                        v(vec.scalar_tensor_tensor(acc[:, s], src(k), by, acc[:, s], ALU.mult, ALU.add),
                          label if (s, k) == (1, KD - 1) else None, i)

        def over_partitions(bank, acc, n):
            for m in range(n):
                for s in range(2):
                    mm = pe.matmul(PS[:, bank, 2 * m + s:2 * m + s + 1], acc[:, s, m * P:(m + 1) * P],
                                   const("ones")[:, 0:1], start=True, stop=True)
            return mm

        def ada_pe():
            pe.wait_ge(act_done, C.at("silu_c"))
            with C.loop(pe, "ada", 2) as i:
                pe.wait_ge(vec_done, C.at("ada.sum2", i, 1))
                pe.wait_ge(ada_loaded[2], C.at("ada.load2", i))
                for m in range(4):
                    for k in range(KD):
                        mm = pe.matmul(PS[:, 2, 2 * m:2 * m + 2], ADA[:, 2, k, m * P:(m + 1) * P], SC[:, k, :],
                                       start=k == 0, stop=k == KD - 1)
                mm.then_inc(pe_done, C.mark(pe_done, "ada.2"))
                for q in range(2):
                    pe.wait_ge(vec_done, C.at(f"ada.acc{q}", i))
                    over_partitions(q, ACC[:, q], 4).then_inc(pe_done, C.mark(pe_done, f"ada.{q}"))
            leave((pe_done, w_used), "ada")

        def mod_rows(l, tile, n, ps, label, i):
            bias = columns(3 * l, tile, n).unsqueeze(2).broadcast_to([P, n, 2])
            v(vec.tensor_tensor(MOD[:, l, bass.ds(tile, n), :], ps.rearrange("p (t s) -> p t s", s=2), bias, ALU.add),
              label, i)

        def norm_gain(l, n):
            gain = columns(3 * l, 48 + 8 * n, 8).unsqueeze(2).broadcast_to([P, KD, 2])
            v(vec.scalar_tensor_tensor(MS[:, 2 * l + n, :, :], MOD[:, l, 24 * n + 8:24 * n + 16, :], 1.0, gain,
                                       ALU.add, ALU.mult))

        def add_square(x, lo, i=None):
            v(vec.tensor_tensor(XSQ[:, lo:T], x, x, ALU.mult), None, i)
            v(vec.tensor_tensor(SS[:, lo:T], SS[:, lo:T], XSQ[:, lo:T], ALU.add), None, i)

        def ada_vec():
            enter(vec, (vec_done,), "start")
            v(vec.memset(SS, 0.0))
            for k in range(KD):
                add_square(X[:, k, :], 0)
            with C.loop(vec, "ada", 2) as i:
                for q in range(2):
                    vec.wait_ge(ada_loaded[q], C.at(f"ada.load{q}", i))
                    over_inputs(ACC[:, q], lambda k: ADA[:, q, k, :], f"ada.acc{q}", i)
                for q in (2, 0, 1):
                    vec.wait_ge(pe_done, C.at(f"ada.{q}", i))
                    mod_rows(0, i * 12 + 4 * q, 4, PS[:, q, 0:8], f"ada.sum{q}", i)
            norm_gain(0, 0)
            v(vec.tensor_copy(MS[:, 2 * DEPTH, :, 1], columns(0, 64, 8)))
            leave((vec_done,), "ada")

        def ride_pool(tag, l, i, n, tile):
            pool.wait_ge(vec_done, C.at(f"{tag}.acc", i, 1))
            pool.sem_inc(loads_started, 1)
            pool.dma_start(AW[:, 0:KD * n * P].rearrange("p (k c) -> p k c", k=KD),
                           rows(a["ada_w"][l])[:, :, bass.ds(tile * P, n * P)]).then_inc(
                ride_loaded, C.mark(ride_loaded, f"{tag}.al", 16))

        def ride_sum(tag, i, n):
            vec.wait_ge(ride_loaded, C.at(f"{tag}.al", i))
            over_inputs(ACC[:, 0, :, 0:n * P], lambda k: AW[:, k * n * P:(k + 1) * n * P], f"{tag}.acc", i)

        def ride_pe(tag, i, n):
            pe.wait_ge(vec_done, C.at(f"{tag}.acc", i))
            over_partitions(ABANK, ACC[:, 0], n).then_inc(pe_done, C.mark(pe_done, f"{tag}.a"))

        def ride_vec(tag, l, i, tile, n):
            vec.wait_ge(pe_done, C.at(f"{tag}.a", i))
            mod_rows(l, tile, n, PS[:, ABANK, 0:2 * n], f"{tag}.am", i)

        RS = WORK[:, 1024:1536]
        TMP = WORK[:, 1536:3584].rearrange("p (b t) -> p b t", b=4)

        def norm_pe(tag, prev, lo):
            enter(pe, (pe_done, w_used), prev)
            pe.matmul(PS[:, 0, lo:T], const("mean"), SS[:, lo:T], start=True, stop=True).then_inc(
                pe_done, C.mark(pe_done, f"{tag}.ms"))
            leave((pe_done, w_used), tag)

        def norm_act(tag, prev, lo, gain, shift):
            enter(act, (act_done,), prev)
            act.wait_ge(pe_done, C.at(f"{tag}.ms"))
            s(act.activation(RS[:, lo:T], PS[:, 0, lo:T], ACT.Ln, bias=MC[:, 0:1]))
            s(act.activation(RS[:, lo:T], RS[:, lo:T], ACT.Exp, scale=-0.5), f"{tag}.rs")
            for k in range(0, KD, 2):
                act.wait_ge(vec_done, C.at(f"{tag}.t{k}"))
                for n in range(2):
                    if n == 0 and lo:
                        continue
                    s(act.activation(Hk[:, k, SEGS[n]], TMP[:, k % 4, SEGS[n]], ACT.Identity,
                                     scale=MS[:, gain, k, n:n + 1], bias=shift(k, n)), f"{tag}.h{k}" if n else None)
            leave((act_done,), tag)

        def norm_vec(tag, prev, lo, gain, shift):
            enter(vec, (vec_done,), prev)
            vec.wait_ge(act_done, C.at(f"{tag}.rs"))
            for k in range(KD):
                if k >= 4 and k % 2 == 0:
                    vec.wait_ge(act_done, C.at(f"{tag}.h{k - 4}"))
                v(vec.tensor_tensor(TMP[:, k % 4, lo:T], X[:, k, lo:T], RS[:, lo:T], ALU.mult), f"{tag}.t{k}")
                for n in range(2):
                    if k % 2 and not (n == 0 and lo):
                        v(vec.tensor_scalar(Hk[:, k, SEGS[n]], TMP[:, k % 4, SEGS[n]], MS[:, gain, k, n:n + 1],
                                            shift(k, n), ALU.mult, ALU.add))
            leave((vec_done,), tag)

        def mod_shift(l, n2):
            return lambda k, n: MOD[:, l, 24 * n2 + k, n:n + 1]

        G = BIG[:, 0:NF * T].rearrange("p (f t) -> p f t", f=NF)
        CV = WORK[:, 0:2048].rearrange("p (q h t) -> p q h t", q=2, h=2)
        SG = WORK[:, 2048:3072].rearrange("p (q t) -> p q t", q=2)
        CW = WORK[:, 3072:3204]
        CWj = WORK[:, 3204:3216].rearrange("p (q h t) -> p q h t", q=2, h=2)

        def ffn_sp(l):
            w = rows(a["ffn_w_in"][l])
            with C.loop(sp, f"f{l}", NF // 2) as i:
                for q in range(2):
                    for h in range(2):
                        load_unit(i, f"f{l}.w{q}{h}", unit(w, 0, 8, i * 256 + q * P + h * F))
            w = rows(a["ffn_w_out"][l])
            with C.loop(sp, f"fo{l}", KD // 2) as i:
                for q in range(2):
                    for r in range(3):
                        load_unit(i, f"fo{l}.w{q}{r}", unit(w, 8 * r, 8 if r < 2 else 6, i * 256 + q * P))

        def ffn_pe(l, lo):
            enter(pe, (pe_done, w_used), f"n2{l}")
            with C.loop(pe, f"f{l}", NF // 2) as i:
                for q in range(2):
                    for h in range(2):
                        pe.wait_ge(vec_done, C.at(f"f{l}.cv{q}{h}", i, 1))
                        use_unit(i, f"f{l}.w{q}{h}", PS[:, 2 * q + h, lo:T], lambda k: Hk[:, k, lo:T], 8, True, True)
                if l + 1 < DEPTH:
                    ride_pe(f"f{l}", i, 4)
            pe.wait_ge(vec_done, C.at(f"f{l}.g1"))
            with C.loop(pe, f"fo{l}", KD // 2) as i:
                for q in range(2):
                    pe.wait_ge(vec_done, C.at(f"fo{l}.x{q}", i, 1))
                    for r in range(3):
                        nk = 8 if r < 2 else 6
                        use_unit(i, f"fo{l}.w{q}{r}", PS[:, 4 + q, lo:T], lambda k: G[:, 8 * r + k, lo:T], nk,
                                 r == 0, r == 2)
                if l + 1 < DEPTH:
                    ride_pe(f"fo{l}", i, 1)
            leave((pe_done, w_used), f"ffn{l}")

        def ffn_pool(l, prev):
            if l + 1 == DEPTH:
                return
            enter(pool, (pool_done,), prev)
            with C.loop(pool, f"f{l}", NF // 2) as i:
                ride_pool(f"f{l}", l + 1, i, 4, i * 4)
            with C.loop(pool, f"fo{l}", KD // 2) as i:
                ride_pool(f"fo{l}", l + 1, i, 1, i + 44)

        def ffn_act(l, lo):
            enter(act, (act_done,), f"n2{l}")
            act.wait_ge(vec_done, C.at(f"f{l}.cw"))
            with C.loop(act, f"f{l}", NF // 2) as i:
                for q in range(2):
                    act.wait_ge(vec_done, C.at(f"f{l}.cwj", i))
                    for h in range(2):
                        act.wait_ge(w_used, C.at(f"f{l}.w{q}{h}.used", i))
                        if h == 0:
                            act.wait_ge(vec_done, C.at(f"f{l}.g{q}", i, 1))
                        s(act.activation(CV[:, q, h, lo:T], PS[:, 2 * q + h, lo:T], ACT.Copy,
                                         scale=CWj[:, q, h, 1:2]), f"f{l}.c{q}{h}", i)
                for q in range(2):
                    act.wait_ge(vec_done, C.at(f"f{l}.cv{q}1", i))
                    s(act.activation(SG[:, q, lo:T], CV[:, q, 1, lo:T], ACT.Silu), f"f{l}.sg{q}", i)
            leave((act_done,), f"ffn{l}")

        def seg2(ap, lo, x0, x1):
            return ap[:, lo:T].rearrange("p (s t) -> p s t", t=SEG)[:, :, x0:x1]

        def taps(dst, src, w0, w2, lo, label=None, i=None):
            v(vec.scalar_tensor_tensor(seg2(dst, lo, 1, SEG), seg2(src, lo, 0, SEG - 1), w0, seg2(dst, lo, 1, SEG),
                                       ALU.mult, ALU.add), None, i)
            v(vec.scalar_tensor_tensor(seg2(dst, lo, 0, SEG - 1), seg2(src, lo, 1, SEG), w2,
                                       seg2(dst, lo, 0, SEG - 1), ALU.mult, ALU.add), label, i)

        def ffn_vec(l, lo):
            enter(vec, (vec_done,), f"n2{l}")
            v(vec.tensor_copy(CW[:, 0:66], columns(3 * l + 1, 0, 66)))
            v(vec.tensor_copy(CW[:, 66:132], columns(3 * l + 2, 0, 66)), f"f{l}.cw")
            taps3 = CW[:, 0:132].rearrange("p (t h f) -> p h f t", t=3, h=2)
            with C.loop(vec, f"f{l}", NF // 2) as i:
                if l + 1 < DEPTH:
                    ride_sum(f"f{l}", i, 4)
                vec.wait_ge(act_done, C.at(f"f{l}.c11", i, 1))
                for h in range(2):
                    v(vec.tensor_copy(CWj[:, :, h, :], taps3[:, h, bass.ds(i * 2, 2), :]), f"f{l}.cwj" if h else None, i)
                for q in range(2):
                    for h in range(2):
                        vec.wait_ge(act_done, C.at(f"f{l}.c{q}{h}", i))
                        taps(CV[:, q, h, :], PS[:, 2 * q + h, :], CWj[:, q, h, 0:1], CWj[:, q, h, 2:3], lo,
                             f"f{l}.cv{q}{h}", i)
                for q in range(2):
                    vec.wait_ge(act_done, C.at(f"f{l}.sg{q}", i))
                    v(vec.tensor_tensor(G[:, i * 2 + q, lo:T], CV[:, q, 0, lo:T], SG[:, q, lo:T], ALU.mult),
                      f"f{l}.g{q}", i)
                if l + 1 < DEPTH:
                    ride_vec(f"f{l}", l + 1, i, i * 4, 4)
            v(vec.memset(SS, 0.0))
            with C.loop(vec, f"fo{l}", KD // 2) as i:
                if l + 1 < DEPTH:
                    ride_sum(f"fo{l}", i, 1)
                for q in range(2):
                    vec.wait_ge(w_used, C.at(f"fo{l}.w{q}2.used", i))
                    residual(i, q, PS[:, 4 + q, :], l, 5, lo, f"fo{l}.x{q}")
                if l + 1 < DEPTH:
                    ride_vec(f"fo{l}", l + 1, i, i + 44, 1)
            if l + 1 < DEPTH:
                norm_gain(l + 1, 0)
                norm_gain(l + 1, 1)
            leave((vec_done,), f"ffn{l}")

        def residual(i, q, ps, l, which, lo, label):
            for n in range(2):
                if n == 0 and lo:
                    continue
                m = i * 2 + q
                v(vec.scalar_tensor_tensor(X[:, m, SEGS[n]], ps[:, SEGS[n]], MOD[:, l, which * 8 + m, n:n + 1],
                                           X[:, m, SEGS[n]], ALU.mult, ALU.add), label if n else None, i)
            add_square(X[:, m, lo:T], lo, i)

        def proj_sp(tag, w, units):
            w = rows(w)
            with C.loop(sp, tag, KD // 2) as i:
                for q in range(2):
                    for r in range(units):
                        load_unit(i, f"{tag}.w{q}{r}", unit(w, 8 * r, 8, i * 256 + q * P))

        def proj_pe(tag, rhs, units, lo):
            with C.loop(pe, tag, KD // 2) as i:
                for q in range(2):
                    pe.wait_ge(vec_done, C.at(f"{tag}.x{q}", i, 1))
                    for r in range(units):
                        use_unit(i, f"{tag}.w{q}{r}", PS[:, q, lo:T], lambda k: rhs(8 * r + k), 8, r == 0,
                                 r == units - 1)

        def proj_vec(tag, l, units, lo):
            v(vec.memset(SS, 0.0))
            with C.loop(vec, tag, KD // 2) as i:
                for q in range(2):
                    vec.wait_ge(w_used, C.at(f"{tag}.w{q}{units - 1}.used", i))
                    residual(i, q, PS[:, q, :], l, 2, lo, f"{tag}.x{q}")

        OUT = BIG[:, 0:2048].rearrange("p (c d) -> p c d", d=D)

        def end_pe(prev):
            enter(pe, (pe_done, w_used), prev)
            for c in range(2):
                for h in range(2):
                    for k in range(4):
                        mm = pe.transpose(PS[:, 2 * c + h, k * P:(k + 1) * P],
                                          Hk[:, 4 * h + k, (2 + c) * P:(3 + c) * P], const("ident"))
                    mm.then_inc(pe_done, C.mark(pe_done, f"out{c}{h}"))

        def end_act(prev):
            enter(act, (act_done,), prev)
            for c in range(2):
                for h in range(2):
                    act.wait_ge(pe_done, C.at(f"out{c}{h}"))
                    s(act.activation(OUT[:, c, h * 512:(h + 1) * 512], PS[:, 2 * c + h, :], ACT.Copy), f"o{c}{h}")

        def end_sp():
            for c in range(2):
                sp.wait_ge(act_done, C.at(f"o{c}1"))
                sp.dma_start(out[0, c * P:(c + 1) * P, :], OUT[:, c, :]).then_inc(stored, C.mark(stored, None, 16))
            sp.wait_ge(stored, C.here(stored))

        QKV = BIG[:, 0:6144].rearrange("p (m t) -> p m t", m=12)
        AO = BIG[:, 6144:10240].rearrange("p (m t) -> p m t", m=KD)
        VTOK = BIG[:, 10240:11264].rearrange("p (c d) -> p c d", c=NCH)
        KDUP = BIG[:, 11264:13312].rearrange("p (g t) -> p g t", g=4)
        AC = BIG[:, 13312:13312 + 13 * P]
        SINK = BIG[:, 15104:15120]
        COS, SIN, ROT = AC[:, 0:256], AC[:, 256:512], AC[:, 512:640]
        DUP = [AC[:, (5 + h) * P:(6 + h) * P] for h in range(2)]
        DUPROT = [AC[:, (7 + h) * P:(8 + h) * P] for h in range(2)]
        AMASK = [AC[:, (9 + 2 * b) * P:(11 + 2 * b) * P] for b in range(2)]
        RT = WORK[:, 0:1024].rearrange("p (b t) -> p b t", t=SEG)
        PX = WORK[:, 1024:3072].rearrange("p (e t) -> p e t", e=4)
        PT = WORK[:, 3072:5120].rearrange("p (e t) -> p e t", e=4)
        KG = WORK[:, 5120:5632]
        QG = WORK[:, 5632:6656].rearrange("p (m t) -> p m t", m=2)
        VG = WORK[:, 6656:6912].rearrange("p (c d) -> p c d", c=NCH)
        SM = WORK[:, 6912:6948]
        MX, NM, RSUM, ES, RD, SKG, MX8 = (SM[:, 4 * n:4 * n + 4] for n in range(7))

        def attn_pool(l):
            enter(pool, (), f"n1{l}")
            pool.dma_start(AC, a["attn_consts"]).then_inc(side_loaded[0], C.mark(side_loaded[0], None, 16))
            pool.dma_start(SINK, a["at_sink"][0].partition_broadcast(P)).then_inc(
                side_loaded[0], C.mark(side_loaded[0], "attn.consts", 16))

        def attn_sp(l):
            w = rows(a["at_w_qkv"][0])
            with C.loop(sp, "qkv", 6) as i:
                for q in range(2):
                    load_unit(i, f"qkv.w{q}", unit(w, 0, 8, i * 256 + q * P))
            proj_sp(f"mo{l}", a["at_w_o"][0], 1)

        def attn_pe(l, lo):
            enter(pe, (pe_done, w_used), f"n1{l}")
            with C.loop(pe, "qkv", 6) as i:
                for q in range(2):
                    pe.wait_ge(act_done, C.at(f"qkv.e{q}", i, 1))
                    use_unit(i, f"qkv.w{q}", PS[:, q, :], lambda k: Hk[:, k, :], 8, True, True)
            pe.wait_ge(act_done, C.at("qkv.e1"))
            pe.wait_ge(side_loaded[0], C.at("attn.consts"))
            with C.loop(pe, "rope", 4) as i:
                for q in range(2):
                    pe.wait_ge(vec_done, C.at(f"rope.t{q}", i, 1))
                    pe.matmul(PS[:, 2 + q, 0:SEG], ROT, QKV[:, i * 2 + q, SEG:T], start=True,
                              stop=True).then_inc(pe_done, C.mark(pe_done, f"rope.r{q}"))
            for kv in range(4):
                pe.matmul(PS[:, 4 + kv % 2, :], DUP[kv % 2], QKV[:, 8 + kv // 2, :], start=True, stop=True)
                if kv >= 2:
                    pe.wait_ge(vec_done, C.at(f"kd{kv - 2}"))
                pe.matmul(PS[:, 6 + kv % 2, 0:SEG], DUPROT[kv % 2], QKV[:, 8 + kv // 2, SEG:T], start=True,
                          stop=True).then_inc(pe_done, C.mark(pe_done, f"kr{kv}"))
                if kv == 1:
                    pe.wait_ge(vec_done, C.at("kd1"))
            for m in range(2):
                for c in range(NCH):
                    mm = pe.transpose(PS[:, m, c * P:(c + 1) * P], QKV[:, 10 + m, c * P:(c + 1) * P], const("ident"))
                mm.then_inc(pe_done, C.mark(pe_done, f"vt{m}"))
            with C.loop(pe, "heads", 4) as i:
                pe.wait_ge(vec_done, C.at("heads.in", i))
                pe.wait_ge(act_done, C.at("heads.in.a", i))
                def scores(b):
                    nk = SEG if b < 2 else T
                    for e in range(4):
                        h = slice(64 * (e % 2), 64 * (e % 2) + 64)
                        pe.matmul(PS[:, e, 0:nk], QG[h, e // 2, b * P:(b + 1) * P], KG[h, 0:nk], start=True,
                                  stop=True).then_inc(pe_done, C.mark(pe_done, f"heads.s{b}{e}"))

                scores(0)
                for b in range(4):
                    nk = SEG if b < 2 else T
                    if b < 3:
                        pe.wait_ge(act_done, C.at(f"heads.ex{b}3", i))
                        scores(b + 1)
                    for e in range(4):
                        pe.wait_ge(vec_done, C.at(f"heads.p{b}{e}", i))
                        for kc in range(nk // P):
                            mm = pe.transpose(PS[:, 4 + e, kc * P:(kc + 1) * P], PX[:, e, kc * P:(kc + 1) * P],
                                              const("ident"))
                        mm.then_inc(pe_done, C.mark(pe_done, f"heads.pt{b}{e}"))
                    for e in range(4):
                        pe.wait_ge(act_done, C.at(f"heads.pc{b}{e}", i))
                        h = slice(64 * (e % 2), 64 * (e % 2) + 64)
                        for kc in range(nk // P):
                            mm = pe.matmul(PS[h, 4 + e // 2, 0:P], VG[:, kc, :], PT[:, e, kc * P:(kc + 1) * P],
                                           start=kc == 0, stop=kc == nk // P - 1)
                    mm.then_inc(pe_done, C.mark(pe_done, f"heads.ov{b}"))
            pe.wait_ge(vec_done, C.at("heads.o3"))
            proj_pe(f"mo{l}", lambda k: AO[:, k, lo:T], 1, lo)
            leave((pe_done, w_used), f"mix{l}")

        def attn_act(l, lo):
            enter(act, (act_done,), f"n1{l}")
            with C.loop(act, "qkv", 6) as i:
                for q in range(2):
                    act.wait_ge(w_used, C.at(f"qkv.w{q}.used", i))
                    s(act.activation(QKV[:, i * 2 + q, :], PS[:, q, :], ACT.Copy), f"qkv.e{q}", i)
            for m in range(2):
                act.wait_ge(pe_done, C.at(f"vt{m}"))
                s(act.activation(VTOK[:, :, m * P:(m + 1) * P], PS[:, m, :].rearrange("p (c d) -> p c d", c=NCH),
                                 ACT.Copy), f"vtok{m}")
            act.wait_ge(vec_done, C.at("kd3"))
            act.wait_ge(vec_done, C.at("rope.q1"))
            with C.loop(act, "heads", 4) as i:
                act.wait_ge(pe_done, C.at("heads.ov3", i, 1))
                s(act.activation(KG, KDUP[:, i, :], ACT.Copy), None, i)
                s(act.activation(VG[:, :, :], VTOK[:, :, bass.ds(i * 64, 64)], ACT.Copy), "heads.in.a", i)
                for b in range(4):
                    nk = SEG if b < 2 else T
                    act.wait_ge(vec_done, C.at(f"heads.nm{b}", i))
                    for e in range(4):
                        s(act.activation(PX[:, e, 0:nk], PS[:, e, 0:nk], ACT.Exp, bias=NM[:, e:e + 1], scale=0.125,
                                         accum_out=RSUM[:, e:e + 1]), f"heads.ex{b}{e}", i)
                    s(act.activation(ES, ES, ACT.Exp), f"heads.es{b}", i)
                    for e in range(4):
                        act.wait_ge(pe_done, C.at(f"heads.pt{b}{e}", i))
                        s(act.activation(PT[:, e, 0:nk], PS[:, 4 + e, 0:nk], ACT.Copy), f"heads.pc{b}{e}", i)
            leave((act_done,), f"mix{l}")

        def attn_vec(l, lo):
            enter(vec, (vec_done,), f"n1{l}")
            vec.wait_ge(side_loaded[0], C.at("attn.consts"))
            vec.wait_ge(act_done, C.at("qkv.e1"))
            with C.loop(vec, "rope", 4) as i:
                for q in range(2):
                    m = i * 2 + q
                    vec.wait_ge(pe_done, C.at(f"rope.r{q}", i))
                    v(vec.tensor_tensor(RT[:, q, :], PS[:, 2 + q, 0:SEG], SIN, ALU.mult), f"rope.t{q}", i)
                    v(vec.tensor_tensor(QKV[:, m, SEG:T], QKV[:, m, SEG:T], COS, ALU.mult), None, i)
                    v(vec.tensor_tensor(QKV[:, m, SEG:T], QKV[:, m, SEG:T], RT[:, q, :], ALU.add), f"rope.q{q}", i)
            for kv in range(4):
                vec.wait_ge(pe_done, C.at(f"kr{kv}"))
                v(vec.tensor_tensor(RT[:, 2, :], PS[:, 6 + kv % 2, 0:SEG], SIN, ALU.mult))
                v(vec.tensor_tensor(RT[:, 3, :], PS[:, 4 + kv % 2, SEG:T], COS, ALU.mult))
                v(vec.tensor_copy(KDUP[:, kv, 0:SEG], PS[:, 4 + kv % 2, 0:SEG]))
                v(vec.tensor_tensor(KDUP[:, kv, SEG:T], RT[:, 2, :], RT[:, 3, :], ALU.add), f"kd{kv}")
            with C.loop(vec, "heads", 4) as i:
                vec.wait_ge(pe_done, C.at("heads.ov3", i, 1))
                v(vec.tensor_copy(QG[:, :, :], QKV[:, bass.ds(i * 2, 2), :]), None, i)
                v(vec.tensor_copy(SKG, SINK[:, bass.ds(i * 4, 4)]), "heads.in", i)
                def maxima(b):
                    nk = SEG if b < 2 else T
                    for e in range(4):
                        vec.wait_ge(pe_done, C.at(f"heads.s{b}{e}", i))
                        if b >= 2:
                            v(vec.tensor_tensor(PS[:, e, SEG:T], PS[:, e, SEG:T], AMASK[b - 2], ALU.add), None, i)
                        v(vec.reduce_max(MX[:, e:e + 1], PS[:, e, 0:nk], AX_X), None, i)
                    v(vec.tensor_scalar(MX8, MX, 0.125, None, ALU.mult), None, i)
                    v(vec.tensor_tensor(MX8, MX8, SKG, ALU.max), None, i)
                    v(vec.tensor_tensor(ES, SKG, MX8, ALU.subtract), None, i)
                    v(vec.tensor_scalar(NM, MX8, -1.0, None, ALU.mult), f"heads.nm{b}", i)

                maxima(0)
                for b in range(4):
                    nk = SEG if b < 2 else T
                    vec.wait_ge(act_done, C.at(f"heads.es{b}", i))
                    v(vec.tensor_tensor(RD, RSUM, ES, ALU.add), None, i)
                    v(vec.reciprocal(RD, RD), None, i)
                    for e in range(4):
                        v(vec.tensor_scalar(PX[:, e, 0:nk], PX[:, e, 0:nk], RD[:, e:e + 1], None, ALU.mult),
                          f"heads.p{b}{e}", i)
                    if b < 3:
                        maxima(b + 1)
                    vec.wait_ge(pe_done, C.at(f"heads.ov{b}", i))
                    v(vec.tensor_copy(AO[:, bass.ds(i * 2, 2), b * P:(b + 1) * P], PS[:, 4:6, 0:P]),
                      f"heads.o{b}", i)
            proj_vec(f"mo{l}", l, 1, lo)
            leave((vec_done,), f"mix{l}")

        YB = BIG[:, 0:8192].rearrange("p (m t) -> p m t", m=16)
        ACB = BIG[:, 8192:12288].rearrange("p (r t) -> p r t", r=8)
        FS = BIG[:, 12288:16384].rearrange("p (r t) -> p r t", r=8)
        XT = BIG[:, 16384:17408].rearrange("p (c f) -> p c f", c=NCH)
        BT = BIG[:, 17408:17920].rearrange("p (c f) -> p c f", c=NCH)
        XDT = BIG[:, 17920:19968].rearrange("p (d c f) -> p d c f", d=2, c=NCH)
        DCOL = BIG[:, 19968:19984]
        DTB, ALOG = BIG[0:64, 19984:19985], BIG[0:64, 19985:19986]
        DALL = BIG[:, 20000:20032]
        DTw = [BIG[0:64, 12288 + 512 * n:12800 + 512 * n] for n in range(8)]
        XTE = WORK[:, 0:2048].rearrange("p (d c f) -> p d c f", d=2, c=NCH)
        XS = WORK[:, 2048:4096].rearrange("p (m t) -> p m t", m=4)
        ZS = WORK[:, 4096:5120].rearrange("p (m t) -> p m t", m=2)
        CBM = WORK[:, 5120:6144].rearrange("p (d c t) -> p d c t", d=2, c=NCH)
        SEGM = WORK[:, 6144:7168].rearrange("p (b e t) -> p b e t", b=2, e=4)
        MM_ = WORK[:, 7168:8192].rearrange("p (b e t) -> p b e t", b=2, e=4)
        YT_ = WORK[:, 8192:9216].rearrange("p (m t) -> p m t", m=2)
        STT_ = WORK[:, 9216:9728].rearrange("p (d f) -> p d f", d=2)
        DTT = WORK[:, 9728:9984].rearrange("p (c h) -> p c h", c=NCH)
        ACST = WORK[:, 9984:10240].rearrange("p (c h) -> p c h", c=NCH)
        TE = WORK[:, 10240:10272].rearrange("p (d c e) -> p d c e", d=2, c=NCH)
        CD = WORK[:, 10272:10304].rearrange("p (d c e) -> p d c e", d=2, c=NCH)
        ACG = WORK[:, 10304:10336].rearrange("p (c d e) -> p c d e", d=2, c=NCH)
        DTG = WORK[:, 10336:10368].rearrange("p (c d e) -> p c d e", d=2, c=NCH)
        CP = WORK[:, 10368:10384].rearrange("p (k m) -> p k m", k=4)
        DG, NG = WORK[:, 10384:10386], WORK[:, 10386:10388]
        SQG = WORK[:, 10400:11424].rearrange("p (m t) -> p m t", m=2)
        RSG = WORK[:, 11424:11936]
        END = (P - 1, 0)

        def ssd_pool(l):
            enter(pool, (pool_done,), f"n1{l}")
            pool.dma_start(DALL, a["ssd_d"][0].partition_broadcast(P)).then_inc(
                side_loaded[1], C.mark(side_loaded[1], None, 16))
            pool.dma_start(DTB, a["ssd_dt_bias"][0].rearrange("d h -> (d h)").unsqueeze(1)).then_inc(
                side_loaded[1], C.mark(side_loaded[1], None, 16))
            pool.dma_start(ALOG, a["ssd_a_log"][0].rearrange("d h -> (d h)").unsqueeze(1)).then_inc(
                side_loaded[1], C.mark(side_loaded[1], "ssd.params", 16))
            pool.wait_ge(vec_done, C.at("ssd.acs"))
            pool.dma_start(scratch, DTw[7]).then_inc(scratch_stored, C.mark(scratch_stored, "ssd.stored", 16))
            pool.wait_ge(scratch_stored, C.at("ssd.stored"))
            by_group = scratch.rearrange("(d g e) t -> g d e t", d=2, e=4)
            with C.loop(pool, "ssd", 8) as i:
                pool.wait_ge(vec_done, C.at("ssd.sg31", i, 1))
                pool.wait_ge(act_done, C.at("ssd.fs", i, 1))
                pool.dma_start(ACB[:, :, :].rearrange("p (d e) t -> p d e t", d=2),
                               by_group[i].partition_broadcast(P)).then_inc(
                    side_loaded[2], C.mark(side_loaded[2], "ssd.acbload", 16))
                pool.wait_ge(act_done, C.at("ssd.te", i))
                pool.wait_ge(vec_done, C.at("ssd.xdt", i))
                for d in range(2):
                    g(pool.tensor_tensor(XTE[:, d, :, :].rearrange("p c (e f) -> p c e f", e=4),
                                         XDT[:, d, :, :].rearrange("p c (e f) -> p c e f", e=4),
                                         TE[:, d, :, :].unsqueeze(3).broadcast_to([P, NCH, 4, 64]), ALU.mult),
                      "ssd.xte" if d else None, i)
                pool.wait_ge(act_done, C.at("ssd.fs", i))
                pool.wait_ge(vec_done, C.at("ssd.cd", i))
                for d in range(2):
                    g(pool.tensor_tensor(FS[:, 4 * d:4 * d + 4, :], FS[:, 4 * d:4 * d + 4, :],
                                         XS[:, 3, :].unsqueeze(1).broadcast_to([P, 4, T]), ALU.mult),
                      "ssd.fsc" if d else None, i)
            leave((pool_done,), f"mix{l}")

        def ssd_sp(l):
            w = rows(a["ssd_w_in"][0])
            load_unit(None, "ssd.wdt", unit(w, 0, 8, INNER + 4096, 64))
            with C.loop(sp, "ssd", 8) as i:
                for q, c0 in enumerate((i * 256 + INNER, i * 256 + (INNER + P), i * P + 2 * INNER,
                                        i * P + 2 * INNER + 1024, i * 256, i * 256 + P)):
                    load_unit(i, f"ssd.w{q}", unit(w, 0, 8, c0))
            proj_sp(f"mo{l}", a["ssd_w_out"][0], 2)

        def ssd_pe(l, lo):
            enter(pe, (pe_done, w_used), f"n1{l}")
            use_unit(None, "ssd.wdt", PS[0:64, 0, :], lambda k: Hk[:, k, :], 8, True, True, 64)
            pe.wait_ge(vec_done, C.at("ssd.acs"))
            for n, src in ((1, DTw[6]), (2, DTw[7])):
                for c in range(NCH):
                    mm = pe.transpose(PS[:, n, c * 64:(c + 1) * 64], src[:, c * P:(c + 1) * P],
                                      const("ident")[0:64, 0:64])
                mm.then_inc(pe_done, C.mark(pe_done, f"ssd.tr{n}"))
            pe.wait_ge(vec_done, C.at("ssd.acst"))
            with C.loop(pe, "ssd", 8) as i:
                pe.wait_ge(vec_done, C.at("ssd.y31", i, 1))
                for q in range(5):
                    use_unit(i, f"ssd.w{q}", PS[:, q, :], lambda k: Hk[:, k, :], 8, True, True)
                for q in range(3):
                    pe.wait_ge(act_done, C.at(f"ssd.silu{q}", i))
                    for c in range(NCH):
                        mm = pe.transpose(PS[:, (6, 7, 0)[q], c * P:(c + 1) * P], XS[:, q, c * P:(c + 1) * P],
                                          const("ident"))
                    mm.then_inc(pe_done, C.mark(pe_done, f"ssd.xt{q}"))
                pe.wait_ge(act_done, C.at("ssd.silu3", i))
                for c in range(NCH):
                    cs = slice(c * P, (c + 1) * P)
                    mm = pe.matmul(PS[:, 1, cs], XS[:, 2, cs], XS[:, 3, cs], start=True, stop=True)
                mm.then_inc(pe_done, C.mark(pe_done, "ssd.cb"))
                use_unit(i, "ssd.w5", PS[:, 5, :], lambda k: Hk[:, k, :], 8, True, True)
                pe.wait_ge(pool_done, C.at("ssd.xte", i))
                pe.wait_ge(act_done, C.at("ssd.bt", i))
                pe.wait_ge(act_done, C.at("ssd.z1", i))
                for c in range(NCH):
                    for d in range(2):
                        ch = ORDER[d][c]
                        cs = slice(ch * P, (ch + 1) * P)
                        if c < NCH - 1:
                            if c:
                                pe.wait_ge(vec_done, C.at(f"ssd.st{c - 1}{d}", i))
                            pe.matmul(PS[:, 4 + d, 0:256], BT[:, ch, :], XTE[:, d, ch, :], start=True,
                                      stop=True).then_inc(pe_done, C.mark(pe_done, f"ssd.s{c}{d}"))
                        if (c, d) == (1, 0):
                            pe.wait_ge(pool_done, C.at("ssd.fsc", i))
                        pe.wait_ge(vec_done, C.at(f"ssd.m{c}{d}", i))
                        for e in range(4):
                            h = slice(64 * (e % 2), 64 * (e % 2) + 64)
                            o = PS[h, 2 + d, (e // 2) * P:(e // 2 + 1) * P]
                            ef = slice(e * 64, (e + 1) * 64)
                            mm = pe.matmul(o, XDT[:, d, ch, ef], MM_[:, d, e, :], start=True, stop=c == 0)
                            if c:
                                mm = pe.matmul(o, STT_[:, d, ef], FS[:, 4 * d + e, cs], start=False, stop=True)
                        mm.then_inc(pe_done, C.mark(pe_done, f"ssd.yo{c}{d}"))
                pe.wait_ge(act_done, C.at("ssd.sq", i))
                for m in range(2):
                    mm = pe.matmul(PS[:, 6, :], const("mean256"), SQG[:, m, :], start=m == 0, stop=m == 1)
                mm.then_inc(pe_done, C.mark(pe_done, "ssd.ms"))
            pe.wait_ge(vec_done, C.at("ssd.yb"))
            proj_pe(f"mo{l}", lambda k: YB[:, k, lo:T], 2, lo)
            leave((pe_done, w_used), f"mix{l}")

        def ssd_act(l, lo):
            enter(act, (act_done,), f"n1{l}")
            act.wait_ge(vec_done, C.at("ssd.z"))
            s(act.activation(DTw[1], DTw[0], ACT.Abs))
            s(act.activation(DTw[1], DTw[1], ACT.Exp, scale=-1.0), "ssd.e")
            act.wait_ge(side_loaded[1], C.at("ssd.params"))
            s(act.activation(ALOG, ALOG, ACT.Exp), "ssd.a")
            act.wait_ge(vec_done, C.at("ssd.acst"))
            act.wait_ge(scratch_stored, C.at("ssd.stored"))
            with C.loop(act, "ssd", 8) as i:
                act.wait_ge(vec_done, C.at("ssd.cp", i))
                act.wait_ge(pe_done, C.at("ssd.ms", i, 1))
                for q in range(4):
                    act.wait_ge(w_used, C.at(f"ssd.w{q}.used", i))
                    s(act.activation(XS[:, q, :], PS[:, q, :], ACT.Identity, scale=CP[:, 1, q:q + 1],
                                     bias=CP[:, 3, q:q + 1]), f"ssd.c{q}", i)
                for q in range(4):
                    act.wait_ge(vec_done, C.at(f"ssd.cv{q}", i))
                    s(act.activation(XS[:, q, :], XS[:, q, :], ACT.Silu), f"ssd.silu{q}", i)
                act.wait_ge(w_used, C.at("ssd.w4.used", i))
                s(act.activation(ZS[:, 0, :], PS[:, 4, :], ACT.Silu), "ssd.z0", i)
                for q in range(2):
                    act.wait_ge(pe_done, C.at(f"ssd.xt{q}", i))
                    s(act.activation(XT[:, :, q * P:(q + 1) * P], PS[:, 6 + q, :].rearrange("p (c f) -> p c f", c=NCH),
                                     ACT.Copy), f"ssd.xtok{q}", i)
                act.wait_ge(pe_done, C.at("ssd.xt2", i))
                s(act.activation(BT[:, :, :], PS[:, 0, :].rearrange("p (c f) -> p c f", c=NCH), ACT.Copy), "ssd.bt", i)
                act.wait_ge(vec_done, C.at("ssd.te0", i))
                s(act.activation(TE[:, :, :, :], TE[:, :, :, :], ACT.Exp), "ssd.te", i)
                act.wait_ge(side_loaded[2], C.at("ssd.acbload", i))
                for r in range(8):
                    s(act.activation(FS[:, r, :], ACB[:, r, :], ACT.Exp), "ssd.fs" if r == 7 else None, i)
                act.wait_ge(w_used, C.at("ssd.w5.used", i))
                s(act.activation(ZS[:, 1, :], PS[:, 5, :], ACT.Silu), "ssd.z1", i)
                for c in range(NCH):
                    for d in range(2):
                        act.wait_ge(vec_done, C.at(f"ssd.sg{c}{d}", i))
                        s(act.activation(SEGM[:, d, :, :], SEGM[:, d, :, :], ACT.Exp), f"ssd.ex{c}{d}", i)
                act.wait_ge(vec_done, C.at("ssd.yz", i))
                s(act.activation(SQG[:, :, :], YT_[:, :, :], ACT.Square), "ssd.sq", i)
                act.wait_ge(pe_done, C.at("ssd.ms", i))
                s(act.activation(RSG, PS[:, 6, :], ACT.Ln, bias=MC[:, 0:1]), None, i)
                s(act.activation(RSG, RSG, ACT.Exp, scale=-0.5), "ssd.rs", i)
            leave((act_done,), f"mix{l}")

        def ssd_vec(l, lo):
            enter(vec, (vec_done,), f"n1{l}")
            Z, E, R, S, S2, Q, DT, AC_ = DTw
            vec.wait_ge(side_loaded[1], C.at("ssd.params"))
            for h in range(2):
                ph = slice(64 * h, 64 * h + 64)
                v(vec.tensor_copy(DCOL[ph, :], DALL[ph, :].rearrange("p (m h) -> p h m", h=2)[:, h, :]))
            vec.wait_ge(w_used, C.at("ssd.wdt.used"))
            v(vec.tensor_scalar(Z, PS[0:64, 0, :], DTB, None, ALU.add), "ssd.z")
            vec.wait_ge(act_done, C.at("ssd.e"))
            v(vec.tensor_scalar(R, E, 2.0, None, ALU.add))
            v(vec.reciprocal(R, R))
            v(vec.tensor_tensor(S, E, R, ALU.mult))
            v(vec.tensor_tensor(S2, S, S, ALU.mult))
            v(vec.tensor_scalar(Q, S2, 1.0 / 15, None, ALU.mult))
            for n in (13, 11, 9, 7, 5, 3):
                v(vec.scalar_tensor_tensor(Q, Q, 1.0 / n, S2, ALU.add, ALU.mult))
            v(vec.scalar_tensor_tensor(Q, Q, 1.0, S, ALU.add, ALU.mult))
            v(vec.tensor_scalar(Z, Z, 0.0, None, ALU.max))
            v(vec.scalar_tensor_tensor(DT, Q, 2.0, Z, ALU.mult, ALU.add))
            vec.wait_ge(act_done, C.at("ssd.a"))
            v(vec.tensor_scalar(ALOG, ALOG, -1.0, None, ALU.mult))
            v(vec.tensor_scalar(S, DT, ALOG, None, ALU.mult))
            for c in range(NCH):
                cs = slice(c * P, (c + 1) * P)
                v(vec.tensor_tensor_scan(AC_[:, cs], const("ones")[0:64, :], S[:, cs], 0.0, ALU.mult, ALU.add))
            b3 = lambda ap: ap[32:64, :].rearrange("p (c t) -> p c t", c=NCH)
            v(vec.tensor_tensor(b3(Q), b3(AC_)[:, :, P - 1:P].broadcast_to([32, NCH, P]), b3(AC_), ALU.subtract))
            v(vec.tensor_tensor(b3(AC_), b3(Q), b3(S), ALU.add), "ssd.acs")
            for n, dst in ((1, DTT), (2, ACST)):
                vec.wait_ge(pe_done, C.at(f"ssd.tr{n}"))
                v(vec.tensor_copy(dst[:, :, :], PS[:, n, 0:256].rearrange("p (c h) -> p c h", c=NCH)),
                  "ssd.acst" if n == 2 else None)
            cw = columns(B_SSD, 0, P).rearrange("p (k m) -> p k m", k=4)
            with C.loop(vec, "ssd", 8) as i:
                v(vec.tensor_copy(CP[:, :, 0:2], cw[:, :, bass.ds(i * 2, 2)]), None, i)
                v(vec.tensor_copy(CP[:, :, 2], cw[:, :, i + 16]), None, i)
                v(vec.tensor_copy(CP[:, :, 3], cw[:, :, i + 24]), None, i)
                for d in range(2):
                    v(vec.tensor_copy(ACG[:, :, d, :], ACST[:, :, bass.ds(i * 4 + 32 * d, 4)]), None, i)
                    v(vec.tensor_copy(DTG[:, :, d, :], DTT[:, :, bass.ds(i * 4 + 32 * d, 4)]), None, i)
                v(vec.tensor_copy(DG, DCOL[:, bass.ds(i * 2, 2)]), None, i)
                v(vec.tensor_copy(NG, columns(B_SSDN, i * 2, 2)), "ssd.cp", i)
                for q in range(4):
                    vec.wait_ge(act_done, C.at(f"ssd.c{q}", i))
                    taps(XS[:, q, :], PS[:, q, :], CP[:, 0, q:q + 1], CP[:, 2, q:q + 1], 0, f"ssd.cv{q}", i)
                vec.wait_ge(side_loaded[2], C.at("ssd.acbload", i))
                for d in range(2):
                    ends = ACB[:, 4 * d:4 * d + 4, :].rearrange("p e (c t) -> p c e t", c=NCH)[:, :, :, END[d]]
                    v(vec.tensor_tensor(TE[:, d, :, :], ends, ACG[:, :, d, :], ALU.subtract),
                      "ssd.te0" if d else None, i)

                def segs(c, d):
                    ch = ORDER[d][c]
                    for e in range(4):
                        v(vec.tensor_scalar(SEGM[:, d, e, :], ACB[:, 4 * d + e, ch * P:(ch + 1) * P],
                                            ACG[:, ch, d, e:e + 1], 0.0, ALU.subtract, ALU.min),
                          f"ssd.sg{c}{d}" if e == 3 else None, i)

                for d in range(2):
                    segs(0, d)
                for q in range(2):
                    vec.wait_ge(act_done, C.at(f"ssd.xtok{q}", i))
                xt4 = XT[:, :, :].rearrange("p c (e f) -> p c e f", e=4)
                for d in range(2):
                    v(vec.tensor_tensor(XDT[:, d, :, :].rearrange("p c (e f) -> p c e f", e=4), xt4,
                                        DTG[:, :, d, :].unsqueeze(3).broadcast_to([P, NCH, 4, 64]), ALU.mult),
                      "ssd.xdt" if d else None, i)
                vec.wait_ge(pe_done, C.at("ssd.cb", i))
                for d in range(2):
                    v(vec.tensor_tensor(CBM[:, d, :, :], PS[:, 1, :].rearrange("p (c t) -> p c t", c=NCH),
                                        const(f"gi{d}").unsqueeze(1).broadcast_to([P, NCH, P]), ALU.mult), None, i)
                vec.wait_ge(act_done, C.at("ssd.fs", i))
                for d in range(2):
                    ends = FS[:, 4 * d:4 * d + 4, :].rearrange("p e (c t) -> p c e t", c=NCH)[:, :, :, END[d]]
                    v(vec.tensor_copy(CD[:, d, :, :], ends), "ssd.cd" if d else None, i)

                def gather(c, d):
                    ch = ORDER[d][c]
                    cs = slice(ch * P, (ch + 1) * P)
                    if c < NCH - 1:
                        vec.wait_ge(pe_done, C.at(f"ssd.yo{c}{d}", i))
                        if c:
                            v(vec.tensor_tensor(STT_[:, d, :].rearrange("p (e f) -> p e f", e=4),
                                                STT_[:, d, :].rearrange("p (e f) -> p e f", e=4),
                                                CD[:, d, ch, :].unsqueeze(2).broadcast_to([P, 4, 64]), ALU.mult),
                              None, i)
                            v(vec.tensor_tensor(STT_[:, d, :], STT_[:, d, :], PS[:, 4 + d, 0:256], ALU.add),
                              f"ssd.st{c}{d}", i)
                        else:
                            v(vec.tensor_copy(STT_[:, d, :], PS[:, 4 + d, 0:256]), f"ssd.st{c}{d}", i)
                    else:
                        vec.wait_ge(pe_done, C.at(f"ssd.yo{c}{d}", i))
                    y = PS[:, 2 + d, 0:256].rearrange("p (m t) -> p m t", m=2)
                    if c % 2 == 0:
                        v(vec.tensor_copy(YT_[:, :, cs], y), f"ssd.y{c}{d}", i)
                    else:
                        v(vec.tensor_tensor(YT_[:, :, cs], YT_[:, :, cs], y, ALU.add), f"ssd.y{c}{d}", i)

                steps = [(c, d) for c in range(NCH) for d in range(2)]
                for n, (c, d) in enumerate(steps):
                    ch = ORDER[d][c]
                    vec.wait_ge(act_done, C.at(f"ssd.ex{c}{d}", i))
                    if c:
                        vec.wait_ge(pe_done, C.at(f"ssd.yo{c - 1}{d}", i))
                    v(vec.tensor_tensor(MM_[:, d, :, :], SEGM[:, d, :, :],
                                        CBM[:, d, ch, :].unsqueeze(1).broadcast_to([P, 4, P]), ALU.mult),
                      f"ssd.m{c}{d}", i)
                    if c < NCH - 1:
                        segs(c + 1, d)
                    if n:
                        gather(*steps[n - 1])
                gather(*steps[-1])
                for m in range(2):
                    v(vec.scalar_tensor_tensor(YT_[:, m, :], XS[:, m, :], DG[:, m:m + 1], YT_[:, m, :], ALU.mult,
                                               ALU.add), None, i)
                v(vec.tensor_tensor(YT_[:, :, :], YT_[:, :, :], ZS[:, :, :], ALU.mult), "ssd.yz", i)
                vec.wait_ge(act_done, C.at("ssd.rs", i))
                for m in range(2):
                    v(vec.scalar_tensor_tensor(YB[:, i * 2 + m, :], YT_[:, m, :], NG[:, m:m + 1], RSG, ALU.mult,
                                               ALU.mult), "ssd.yb" if m else None, i)
            proj_vec(f"mo{l}", l, 2, lo)
            leave((vec_done,), f"mix{l}")

        RKV = BIG[:, 0:12288].rearrange("p (n k t) -> p n k t", n=3, k=KD)
        XM = [m.rearrange("p (k t) -> p k t", k=KD)
              for m in (BIG[:, 12288:16384], WORK[:, 13312:17408])]
        DX = BIG[:, 16384:20480].rearrange("p (k t) -> p k t", k=KD)
        _w = [0]

        def work(n):
            _w[0] += n
            assert _w[0] <= WORK_N
            return WORK[:, _w[0] - n:_w[0]]

        TH, AL, GS = work(512), work(512), work(512)
        W2S, A2S, G2S = work(P), work(P), work(P)
        SD = work(1024).rearrange("p (d t) -> p d t", d=2)
        AD = work(1024).rearrange("p (d t) -> p d t", d=2)
        AR = work(2048).rearrange("p (d n t) -> p d n t", d=2, n=2)
        ARS = work(2048).rearrange("p (d n t) -> p d n t", d=2, n=2)
        PN = work(1024).rearrange("p (d t) -> p d t", d=2)
        KK, KF, BV, YT, BS = (work(512) for _ in range(5))
        KBT = work(1024).rearrange("p (d c f) -> p d c f", d=2, c=NCH)
        BNT = work(1024).rearrange("p (d c f) -> p d c f", d=2, c=NCH)
        VTK = work(512).rearrange("p (c f) -> p c f", c=NCH)
        WS = work(256).rearrange("p (h d f) -> p h d f", h=2, d=2)
        US = work(256).rearrange("p (h d f) -> p h d f", h=2, d=2)
        STR = [work(128).rearrange("p (d f) -> p d f", d=2) for _ in range(2)]
        PCT, PCTS = (work(8).rearrange("p (d c) -> p d c", d=2) for _ in range(2))
        PC, PCN = work(10), work(10)
        free = [H[:, 512 * n:512 * n + 512] for n in range(8)] + [
            BIG[:, 12288 + 512 * n:12800 + 512 * n] for n in range(16)] + [work(512) for _ in range(6)]
        GM1, GM2 = ([[free.pop(0).rearrange("p (d n t) -> p d n t", d=2, n=2) for h in range(2)] for c in range(NCH)]
                    for _ in range(2))
        XTR = [free.pop(0) for c in range(NCH)]
        NB = [{n: free.pop(0) for n in (0, 2, 3, 4, 5)} for e in range(2)]
        quad = lambda ap: ap.rearrange("p (q t) -> p q t", q=4)
        IB = ((6, 7), (4, 5))
        END_R = (P - 1, 0)
        MIXES = (("r", 0), ("k", 2), ("v", 3))
        LORA = (("w", 1), ("a", 4), ("g", 5))
        LEVELS = ("lev8", "lev16", "lev32", "lev64")

        def trip_order(staging):
            first = [("I", 0, 0), ("I", 0, 1), ("T", 0), ("I", 0, 2), ("T", 1)] + [("I", 0, n) for n in range(3, 12)]
            chunks01 = [("C", c, n) for c in range(2) for n in range(3)]
            second = [("I", 1, 0), ("I", 1, 1)]
            for n in range(2, 12):
                second += chunks01[n - 2:n - 1]
                if staging and n < 8:
                    second += [("S", n - 2)]
                second += [("I", 1, n)]
            third = [("C", c, n) for c in (2, 3) for n in range(3)]
            return first + second + third

        def play(steps, i, tile, t, staging):
            for kind, *n in trip_order(staging):
                steps[kind](i, tile, t, *n)

        def rwkv_sp(l):
            j, t, b = l // 3, f"r{l}", f"r{l}b"
            for name, w in (("r", "rw_wr"), ("k", "rw_wk"), ("v", "rw_wv")):
                w = rows(a[w][j])
                with C.loop(sp, t + name, 4) as i:
                    for q in range(2):
                        load_unit(i, f"{t}.{name}{q}", unit(w, 0, 8, i * 256 + q * P))
            for name, w in (("w", "rw_w1"), ("a", "rw_a1")):
                load_unit(None, f"{t}.{name}",
                          (lambda slot: slot[:, :, 0:64], rows(a[w][j][0])), (lambda slot: slot[:, :, 64:P], rows(a[w][j][1])))
            load_unit(None, f"{t}.g", unit(rows(a["rw_g1"][j]), 0, 8, 0))
            enter(sp, (), f"n1{l}")
            w2 = a["rw_w2"][j].rearrange("d r n -> (d r) n")
            a2 = a["rw_a2"][j].rearrange("d r n -> (d r) n")

            def load_w2(label, col):
                sp.dma_start(W2S, w2[:, bass.ds(col, P)]).then_inc(side_loaded[3], C.mark(side_loaded[3], None, 16))
                sp.dma_start(A2S, a2[:, bass.ds(col, P)]).then_inc(side_loaded[3], C.mark(side_loaded[3], label, 16))

            def load_g2(label, col):
                sp.dma_start(G2S, a["rw_g2"][j][:, bass.ds(col, P)]).then_inc(g2_loaded, C.mark(g2_loaded, label, 16))

            load_w2(f"{t}p.s2", 0)
            with C.loop(sp, b, KD - 1) as i:
                sp.wait_ge(pe_done, C.at(f"{b}.gate", i, 1))
                sp.sem_inc(loads_started, 1)
                load_g2(f"{b}.g2", i * P)
                sp.wait_ge(w2_used, C.at(f"{b}.wa", i, 1))
                sp.sem_inc(loads_started, 1)
                load_w2(f"{b}.s2", i * P + P)
            sp.wait_ge(pe_done, C.at(f"{b}.gate"))
            load_g2(f"{t}z.g2", (KD - 1) * P)
            proj_sp(f"mo{l}", a["rw_wo"][j], 1)

        def rwkv_pe(l, lo):
            t0 = f"r{l}"
            enter(pe, (pe_done, w_used), f"n1{l}")
            for n, (name, m) in enumerate(MIXES):
                pe.wait_ge(vec_done, C.at(f"{t0}.mix{m}"))
                with C.loop(pe, t0 + name, 4) as i:
                    for q in range(2):
                        pe.wait_ge(act_done, C.at(f"{t0}.{name}e{q}", i, 1))
                        use_unit(i, f"{t0}.{name}{q}", PS[:, q, :], lambda k: XM[n % 2][:, k, :], 8, True, True)
                    if l == 0:
                        ride_pe(t0 + name, i, 2)
            for n, (name, m) in enumerate(LORA):
                pe.wait_ge(vec_done, C.at(f"{t0}.mix{m}"))
                use_unit(None, f"{t0}.{name}", PS[:, 2 + n, :], lambda k: XM[(n + 1) % 2][:, k, :], 8, True, True)
            pe.wait_ge(act_done, C.at(f"{t0}.ge"))

            def gram_kk(i, t, c, banks):
                for h in range(2):
                    hs = slice(64 * h, 64 * h + 64)
                    for d in range(2):
                        ch = ORDER[d][c]
                        cs = slice(ch * P, (ch + 1) * P)
                        mm = pe.matmul(PS[:, banks[h], 256 * d:256 * d + 256], AD[hs, d, cs], AR[hs, d, :, cs],
                                       start=True, stop=True)
                mm.then_inc(pe_done, C.mark(pe_done, f"{t}.g1{c}"))

            def gram_rest(i, t, c, banks):
                for h in range(2):
                    hs = slice(64 * h, 64 * h + 64)
                    for d in range(2):
                        ch = ORDER[d][c]
                        cs = slice(ch * P, (ch + 1) * P)
                        mm = pe.matmul(PS[:, 4 + h, d * P:(d + 1) * P], AR[hs, d, 0, cs], AD[hs, d, cs], start=True,
                                       stop=True)
                mm.then_inc(pe_done, C.mark(pe_done, f"{t}.gt{c}"))
                if c == 0:
                    pe.wait_ge(primed, C.at(f"{t0}b.prod", i, 1) if i is not None else C.at(f"{t0}b.prod"))
                    pe.wait_ge(act_done, C.at(f"{t0}b.ge", i, 1) if i is not None else C.at(f"{t0}b.ge"))
                for h in range(2):
                    hs = slice(64 * h, 64 * h + 64)
                    for d in range(2):
                        ch = ORDER[d][c]
                        cs = slice(ch * P, (ch + 1) * P)
                        mm = pe.matmul(PS[:, banks[h], 256 * d:256 * d + 256], SD[hs, d, cs], AR[hs, d, :, cs],
                                       start=True, stop=True)
                mm.then_inc(pe_done, C.mark(pe_done, f"{t}.g2{c}"))

            def four(bank, lhs, rhs):
                for q in range(4):
                    qs = slice(q * P, (q + 1) * P)
                    mm = pe.matmul(PS[:, bank, qs], lhs[:, qs], rhs[:, qs], start=True, stop=True)
                return mm

            def invert(i, tile, t, pair, n):
                two = [(e, 2 * pair + e) for e in range(2)]
                if n == 0:
                    c = 2 * pair
                    if pair:
                        pe.wait_ge(vec_done, C.at(f"{t}.xf1", i))
                    gram_kk(i, t, c, (0, 1))
                    gram_rest(i, t, c, (2, 3))
                    if pair == 0:
                        pe.wait_ge(vec_done, C.at(f"{t0}b.out", i, 1) if i is not None else C.at(f"{t0}b.out"))
                    gram_kk(i, t, c + 1, (6, 7))
                    pe.wait_ge(vec_done, C.at(f"{t}.ga{c}", i))
                    gram_rest(i, t, c + 1, (0, 1))
                elif n == 1:
                    for e, c in two:
                        pe.wait_ge(vec_done, C.at(f"{t}.ga{2 * pair + 1}", i))
                        pe.wait_ge(pool_done, C.at(f"{t}.dt{c}", i))
                        four(IB[e][0], XTR[c], NB[e][0])
                        four(IB[e][1], NB[e][0], XTR[c]).then_inc(pe_done, C.mark(pe_done, f"{t}.d2{c}"))
                elif n == 2:
                    for e, c in two:
                        pe.wait_ge(vec_done, C.at(f"{t}.u2{c}", i))
                        pe.wait_ge(act_done, C.at(f"{t}.d2t{c}", i))
                        four(IB[e][0], XTR[c], NB[e][4])
                        four(IB[e][1], NB[e][2], NB[e][3]).then_inc(pe_done, C.mark(pe_done, f"{t}.x1{c}"))
                elif n == 3:
                    for e, c in two:
                        pe.wait_ge(vec_done, C.at(f"{t}.x1v{c}", i))
                        pe.wait_ge(act_done, C.at(f"{t}.d4{c}", i))
                        four(IB[e][0], NB[e][3], NB[e][0]).then_inc(pe_done, C.mark(pe_done, f"{t}.x2{c}"))
                elif n % 2 == 0:
                    m = (n - 4) // 2
                    for e, c in two:
                        pe.wait_ge(vec_done, C.at(f"{t}.xv{m}{c}", i))
                        x = NB[e][2 + m % 2]
                        for q in range(4):
                            qs = slice(q * P, (q + 1) * P)
                            mm = pe.transpose(PS[:, IB[e][1], qs], x[:, qs], const("ident"))
                        mm.then_inc(pe_done, C.mark(pe_done, f"{t}.tr{m}{c}"))
                        pe.wait_ge(pool_done, C.at(f"{t}.o{m}{c}", i))
                        four(IB[e][0], NB[e][5 - m % 2], x).then_inc(pe_done, C.mark(pe_done, f"{t}.yy{m}{c}"))
                else:
                    m = (n - 5) // 2
                    for e, c in two:
                        pe.wait_ge(vec_done, C.at(f"{t}.yv{m}{c}", i))
                        pe.wait_ge(act_done, C.at(f"{t}.xt{m}{c}", i))
                        mm = four(IB[e][0], *((XTR[c], NB[e][0]) if m < 3 else (NB[e][0], XTR[c])))
                        mm.then_inc(pe_done, C.mark(pe_done, f"{t}.xx{m}{c}"))

            def chunk(i, tile, t, c, n):
                hd = [(h, d, ORDER[d][c], slice(64 * h, 64 * h + 64)) for h in range(2) for d in range(2)]
                if n == 0:
                    pe.wait_ge(vec_done, C.at(f"{t}." + {0: "gm3", 2: "xf3"}.get(c, f"st{c - 1}"), i))
                    for h, d, ch, hs in hd:
                        o = PS[:, 1 + h, 384 + 64 * d:448 + 64 * d]
                        mm = pe.matmul(o, GM2[c][h][:, d, 0, :], VTK[:, ch, hs], start=True, stop=c == 0)
                        if c:
                            mm = pe.matmul(o, AR[hs, d, 0, ch * P:(ch + 1) * P], STR[c % 2][hs, d, :], start=False, stop=True)
                    mm.then_inc(pe_done, C.mark(pe_done, f"{t}.w{c}"))
                elif n == 1:
                    pe.wait_ge(act_done, C.at(f"{t}.ws{c}", i))
                    for h, d, ch, hs in hd:
                        q = 2 * h + d
                        mm = pe.matmul(PS[:, 2, 64 * q:64 * q + 64], XTR[c][:, q * P:(q + 1) * P], WS[:, h, d, :],
                                       start=True, stop=True)
                    mm.then_inc(pe_done, C.mark(pe_done, f"{t}.u{c}"))
                else:
                    pe.wait_ge(vec_done, C.at(f"{t}.us{c}", i))
                    if c < NCH - 1:
                        for h, d, ch, hs in hd:
                            o = PS[hs, 2, 256 + 64 * d:320 + 64 * d]
                            pe.matmul(o, KBT[:, d, ch, hs], VTK[:, ch, hs], start=True, stop=False)
                            mm = pe.matmul(o, BNT[:, d, ch, hs], US[:, h, d, :], start=False, stop=True)
                        mm.then_inc(pe_done, C.mark(pe_done, f"{t}.sp{c}"))
                    for h, d, ch, hs in hd:
                        o = PS[hs, 0, d * P:(d + 1) * P]
                        pe.matmul(o, VTK[:, ch, hs], GM2[c][h][:, d, 1, :], start=True, stop=False)
                        if c:
                            pe.matmul(o, STR[c % 2][hs, d, :], AR[hs, d, 1, ch * P:(ch + 1) * P], start=False, stop=False)
                        mm = pe.matmul(o, US[:, h, d, :], GM1[c][h][:, d, 1, :], start=False, stop=True)
                    mm.then_inc(pe_done, C.mark(pe_done, f"{t}.yp{c}"))

            def turn(i, tile, t, n):
                if n == 0:
                    pe.wait_ge(vec_done, C.at(f"{t}.gm1", i))
                    srcs = ((0, SD[:, 0]), (1, SD[:, 1]), (2, AD[:, 0]), (3, AD[:, 1]))
                else:
                    pe.wait_ge(act_done, C.at(f"{t}.t2e", i))
                    pe.matmul(PS[:, 1, :], const("blk"), BS, start=True, stop=True).then_inc(
                        pe_done, C.mark(pe_done, f"{t}.bs"))
                    srcs = ((0, YT),)
                for bank, src in srcs:
                    for c in range(NCH):
                        mm = pe.transpose(PS[:, bank, c * P:(c + 1) * P], src[:, c * P:(c + 1) * P], const("ident"))
                    mm.then_inc(pe_done, C.mark(pe_done, f"{t}.t{n}{bank}"))

            def stage(i, tile, t, n):
                def low_rank(w, x, d):
                    ds = slice(64 * d, 64 * d + 64)
                    return pe.matmul(PS[:, 3, :], w[ds, :], x[ds, :], start=True, stop=True)

                if n == 0:
                    if not t.endswith("p"):
                        pe.wait_ge(vec_done, C.at(f"{t}.gm3", i))
                    pe.wait_ge(side_loaded[3], C.at(f"{t}.s2", i))
                    low_rank(W2S, TH, 0).then_inc(pe_done, C.mark(pe_done, f"{t}.pw0"))
                elif n == 1:
                    pe.wait_ge(act_done, C.at(f"{t}.s0", i))
                    low_rank(W2S, TH, 1).then_inc(pe_done, C.mark(pe_done, f"{t}.pw1"))
                elif n == 2:
                    pe.wait_ge(act_done, C.at(f"{t}.s1", i))
                    low_rank(A2S, AL, 0).then_inc(pe_done, C.mark(pe_done, f"{t}.pa"))
                elif n == 3:
                    pe.wait_ge(act_done, C.at(f"{t}.sa0", i))
                    low_rank(A2S, AL, 1).then_inc(w2_used, C.mark(w2_used, f"{t}.wa"))
                elif n == 4:
                    pe.wait_ge(act_done, C.at(f"{t}.sa1", i))
                    pe.matmul(PS[:, 3, :], const("blk"), KK, start=True, stop=True).then_inc(
                        pe_done, C.mark(pe_done, f"{t}.kks"))

            steps = {"I": invert, "C": chunk, "T": turn, "S": stage}

            def trip(i, tile, t, staging):
                pe.wait_ge(primed, C.at(f"{t0}b.prod1", i, 1) if staging else C.at(f"{t0}b.prod1"))
                pe.wait_ge(kk_rows, C.at(f"{t0}b.ar0", i, 1) if staging else C.at(f"{t0}b.ar0"))
                play(steps, i, tile, t, staging)
                pe.wait_ge(g2_loaded, C.at(f"{t}.g2", i))
                if staging:
                    pe.wait_ge(act_done, C.at(f"{t}.kkl", i))
                pe.matmul(PS[:, 3, :], G2S, GS, start=True, stop=True).then_inc(
                    pe_done, C.mark(pe_done, f"{t}.gate"))
                pe.wait_ge(vec_done, C.at(f"{t}.y3", i))
                pe.matmul(PS[:, 6, :], const("cent"), YT, start=True, stop=True).then_inc(
                    pe_done, C.mark(pe_done, f"{t}.ce"))
                pe.wait_ge(act_done, C.at(f"{t}.ysq", i))
                pe.matmul(PS[:, 7, :], const("blkmean"), NB[0][0], start=True, stop=True).then_inc(
                    pe_done, C.mark(pe_done, f"{t}.post"))

            for n in range(5):
                stage(None, 0, f"{t0}p", n)
            with C.loop(pe, f"{t0}b", KD - 1) as i:
                trip(i, i, f"{t0}b", True)
            trip(None, KD - 1, f"{t0}z", False)
            pe.wait_ge(vec_done, C.at(f"{t0}z.out"))
            proj_pe(f"mo{l}", lambda k: RKV[:, 0, k, lo:T], 1, lo)
            leave((pe_done, w_used), f"mix{l}")

        def rwkv_act(l, lo):
            t0 = f"r{l}"
            enter(act, (act_done,), f"n1{l}")
            for n, (name, m) in enumerate(MIXES):
                with C.loop(act, t0 + name, 4) as i:
                    for q in range(2):
                        act.wait_ge(w_used, C.at(f"{t0}.{name}{q}.used", i))
                        s(act.activation(RKV[:, n, i * 2 + q, :], PS[:, q, :], ACT.Copy), f"{t0}.{name}e{q}", i)
            for n, (dst, func) in enumerate(((TH, ACT.Tanh), (AL, ACT.Copy), (GS, ACT.Sigmoid))):
                name = LORA[n][0]
                act.wait_ge(w_used, C.at(f"{t0}.{name}.used"))
                s(act.activation(dst, PS[:, 2 + n, :], func), f"{t0}.{name}e")

            def invert(i, tile, t, pair, n):
                two = [(e, 2 * pair + e) for e in range(2)]
                cp = lambda dst, e, k, label: s(act.activation(dst, PS[:, IB[e][k], :], ACT.Copy), label, i)
                for e, c in two:
                    if n == 1:
                        act.wait_ge(pe_done, C.at(f"{t}.d2{c}", i))
                        cp(NB[e][3], e, 1, f"{t}.d2t{c}")
                    elif n == 2:
                        act.wait_ge(pe_done, C.at(f"{t}.x1{c}", i))
                        cp(NB[e][3], e, 1, f"{t}.d4{c}")
                    elif n >= 4 and n % 2 == 0:
                        m = (n - 4) // 2
                        act.wait_ge(pe_done, C.at(f"{t}.tr{m}{c}", i))
                        cp(XTR[c], e, 1, f"{t}.xt{m}{c}")

            def chunk(i, tile, t, c, n):
                if n == 0:
                    act.wait_ge(pe_done, C.at(f"{t}.w{c}", i))
                    s(act.activation(WS[:, :, :, :].rearrange("p h d f -> p h (d f)"), PS[:, 1:3, 384:512], ACT.Copy),
                      f"{t}.ws{c}", i)

            def turn(i, tile, t, n):
                if n == 0:
                    for bank, dst in enumerate((KBT[:, 0], KBT[:, 1], BNT[:, 0], BNT[:, 1])):
                        act.wait_ge(pe_done, C.at(f"{t}.t0{bank}", i))
                        s(act.activation(dst.rearrange("p c f -> p (c f)"), PS[:, bank, :], ACT.Copy),
                          {1: f"{t}.t2e", 3: f"{t}.t4e"}.get(bank), i)
                else:
                    act.wait_ge(pe_done, C.at(f"{t}.t10", i))
                    s(act.activation(VTK[:, :, :].rearrange("p c f -> p (c f)"), PS[:, 0, :], ACT.Copy),
                      f"{t}.vt", i)

            def stage(i, tile, t, n):
                if n == 0:
                    act.wait_ge(vec_done, C.at(f"{t}.kf", i))
                    s(act.activation(KK, KF, ACT.Square), None, i)
                if n < 4:
                    act.wait_ge(*((w2_used, C.at(f"{t}.wa", i)) if n == 3
                                  else (pe_done, C.at(f"{t}." + ("pw0", "pw1", "pa")[n], i))))
                    s(act.activation((SD, AD)[n // 2][:, n % 2, :], PS[:, 3, :], ACT.Sigmoid, bias=PCN[:, n:n + 1]),
                      f"{t}." + ("s0", "s1", "sa0", "sa1")[n], i)
                elif n == 4:
                    act.wait_ge(pe_done, C.at(f"{t}.kks", i))
                    s(act.activation(KK, PS[:, 3, :], ACT.Ln, bias=MC[:, 4:5]), f"{t}.kkl", i)
                    s(act.activation(KK, KK, ACT.Exp, scale=-0.5), None, i)
                elif n == 5:
                    act.wait_ge(vec_done, C.at(f"{t}.sums", i))
                    s(act.activation(PN[:, :, :], ARS[:, :, 1, :], ACT.Exp, scale=LOG_W, bias=MC[:, 3:4]), None, i)
                    for d in range(2):
                        ends = ARS[:, d, 1, :].rearrange("p (c t) -> p c t", c=NCH)[:, :, END_R[d]]
                        s(act.activation(PCTS[:, d, :], ends, ACT.Exp, scale=-LOG_W), None, i)
                    act.activation(ARS[:, :, :, :], ARS[:, :, :, :], ACT.Exp, scale=-LOG_W, bias=MC[:, 2:3]).then_inc(
                        staged, C.mark(staged, f"{t}.staged"))
                    act.wait_ge(staged, C.at(f"{t}.staged", i))

            steps = {"I": invert, "C": chunk, "T": turn, "S": stage}

            def trip(i, tile, t, staging):
                act.wait_ge(vec_done, C.at(f"{t0}b.out", i, 1) if staging else C.at(f"{t0}b.out"))
                s(act.activation(YT, RKV[:, 2, tile, :], ACT.Copy), f"{t}.vc", i)
                play(steps, i, tile, t, staging)
                act.wait_ge(pe_done, C.at(f"{t}.gate", i))
                s(act.activation(NB[0][3], PS[:, 3, :], ACT.Copy), f"{t}.ge", i)
                act.wait_ge(pe_done, C.at(f"{t}.ce", i))
                s(act.activation(NB[0][0], PS[:, 6, :], ACT.Square), f"{t}.ysq", i)
                act.wait_ge(pe_done, C.at(f"{t}.post", i))
                s(act.activation(NB[0][2], PS[:, 7, :], ACT.Ln, bias=MC[:, 1:2]), None, i)
                s(act.activation(NB[0][2], NB[0][2], ACT.Exp, scale=-0.5), f"{t}.ry", i)

            for n in range(6):
                stage(None, 0, f"{t0}p", n)
            with C.loop(act, f"{t0}b", KD - 1) as i:
                trip(i, i, f"{t0}b", True)
            trip(None, KD - 1, f"{t0}z", False)
            leave((act_done,), f"mix{l}")

        def rwkv_pool(l):
            t0 = f"r{l}"
            if l == 0:
                enter(pool, (pool_done,), f"n1{l}")
                for n, (name, m) in enumerate(MIXES):
                    with C.loop(pool, t0 + name, 4) as i:
                        ride_pool(t0 + name, 0, i, 2, i * 2 + (24 + 8 * n))

            def kept(i, c, dst, mask, label):
                for h in range(2):
                    g(pool.tensor_tensor(dst[:, 256 * h:256 * h + 256].rearrange("p (q t) -> p q t", q=2),
                                         GM1[c][h][:, :, 0, :], const(mask).unsqueeze(1).broadcast_to([P, 2, P]),
                                         ALU.mult), label if h else None, i)

            def prime(i, t):
                pool.wait_ge(primed, C.at(f"{t}.kkn", i))
                pool.tensor_tensor(AR[:, :, 0, :], ARS[:, :, 0, :], KK.unsqueeze(1).broadcast_to([P, 2, T]),
                                   ALU.mult).then_inc(kk_rows, C.mark(kk_rows, f"{t}.ar0"))

            def trip(i, t):
                for pair in range(2):
                    two = [(e, 2 * pair + e) for e in range(2)]
                    for e, c in two:
                        pool.wait_ge(vec_done, C.at(f"{t}.ga{c}", i))
                        kept(i, c, XTR[c], "mask8", f"{t}.dt{c}")
                    for e, c in two:
                        kept(i, c, NB[e][5], LEVELS[0], f"{t}.o0{c}")
                    for n in range(1, 4):
                        for e, c in two:
                            pool.wait_ge(pe_done, C.at(f"{t}.x1{c}" if n == 1 else f"{t}.yy{n - 2}{c}", i))
                            if n == 1:
                                pool.wait_ge(vec_done, C.at(f"{t}.x1v{c}", i))
                            kept(i, c, NB[e][5 - n % 2], LEVELS[n], f"{t}.o{n}{c}")

            prime(None, f"{t0}p")
            with C.loop(pool, f"{t0}b", KD - 1) as i:
                trip(i, f"{t0}b")
                prime(i, f"{t0}b")
            trip(None, f"{t0}z")
            leave((pool_done,), f"mix{l}")

        def rwkv_vec(l, lo):
            j, t0 = l // 3, f"r{l}"
            B = B_RW + j
            enter(vec, (vec_done,), f"n1{l}")
            h2 = H[:, :].rearrange("p (n t) -> p n t", t=SEG)
            d2 = BIG[:, 16384:20480].rearrange("p (n t) -> p n t", t=SEG)
            v(vec.tensor_tensor(d2[:, :, 1:SEG - 1], h2[:, :, 0:SEG - 2], h2[:, :, 2:SEG], ALU.add))
            v(vec.tensor_copy(d2[:, :, 0:1], h2[:, :, 1:2]))
            v(vec.tensor_copy(d2[:, :, SEG - 1:SEG], h2[:, :, SEG - 2:SEG - 1]))
            v(vec.scalar_tensor_tensor(d2[:, :, :], d2[:, :, :], 0.5, h2[:, :, :], ALU.mult, ALU.subtract))
            used = lambda name, m: f"{t0}.{name}1.used" if (name, m) in MIXES else f"{t0}.{name}.used"
            order = MIXES + LORA

            def mix(n):
                name, m = order[n]
                if n >= 2:
                    vec.wait_ge(w_used, C.at(used(*order[n - 2])))
                for k in range(KD):
                    v(vec.scalar_tensor_tensor(XM[n % 2][:, k, :], DX[:, k, :], columns(B, 8 * m + k, 1), Hk[:, k, :],
                                               ALU.mult, ALU.add), f"{t0}.mix{m}" if k == KD - 1 else None)

            mix(0)
            for n, (name, m) in enumerate(order):
                if n + 1 < len(order):
                    mix(n + 1)
                if l == 0 and n < len(MIXES):
                    with C.loop(vec, t0 + name, 4) as i:
                        ride_sum(t0 + name, i, 2)
                        ride_vec(t0 + name, 0, i, i * 2 + (24 + 8 * n), 2)
            if l == 0:
                norm_gain(0, 1)
            vec.wait_ge(act_done, C.at(f"{t0}.ge"))
            vec.wait_ge(w_used, C.at(used(*order[-1])))
            both = lambda ap: ap.unsqueeze(1).broadcast_to([P, 2, T])

            def invert(i, tile, t, pair, n):
                two = [(e, 2 * pair + e) for e in range(2)]
                bank = lambda e, k: PS[:, IB[e][k], :]
                flat = lambda ap: ap.rearrange("p d n t -> p (d n t)")
                if n == 0:
                    for e, c in two:
                        b1, b2 = ((0, 1), (2, 3)) if e == 0 else ((6, 7), (0, 1))
                        vec.wait_ge(pe_done, C.at(f"{t}.g1{c}", i))
                        for h in range(2):
                            v(vec.tensor_tensor(flat(GM1[c][h]), PS[:, b1[h], :], const("gs0", 4), ALU.mult), None, i)
                        vec.wait_ge(pe_done, C.at(f"{t}.gt{c}", i))
                        for h in range(2):
                            v(vec.tensor_tensor(NB[e][0][:, 256 * h:256 * h + 256], PS[:, 4 + h, 0:256],
                                                const("gt0", 2), ALU.mult), f"{t}.ga{c}" if h else None, i)
                        vec.wait_ge(pe_done, C.at(f"{t}.g2{c}", i))
                        for h in range(2):
                            v(vec.tensor_tensor(flat(GM2[c][h]), PS[:, b2[h], :], const("gs0", 4), ALU.mult),
                              f"{t}.gm{c}" if h else None, i)
                for e, c in two:
                    if n == 1:
                        vec.wait_ge(pe_done, C.at(f"{t}.d2{c}", i))
                        v(vec.tensor_copy(NB[e][2], bank(e, 0)), None, i)
                        v(vec.tensor_tensor(quad(NB[e][4]), quad(NB[e][2]),
                                            const("ident").unsqueeze(1).broadcast_to([P, 4, P]), ALU.add),
                          f"{t}.u2{c}", i)
                    elif n == 2:
                        vec.wait_ge(pe_done, C.at(f"{t}.x1{c}", i))
                        v(vec.tensor_tensor(NB[e][0], bank(e, 0), NB[e][4], ALU.add), f"{t}.x1v{c}", i)
                    elif n == 3:
                        vec.wait_ge(pe_done, C.at(f"{t}.x2{c}", i))
                        v(vec.tensor_tensor(NB[e][2], bank(e, 0), NB[e][0], ALU.add), f"{t}.xv0{c}", i)
                    elif n >= 4 and n % 2 == 0:
                        m = (n - 4) // 2
                        vec.wait_ge(pe_done, C.at(f"{t}.yy{m}{c}", i))
                        v(vec.tensor_copy(NB[e][0], bank(e, 0)), f"{t}.yv{m}{c}", i)
                    elif n >= 5:
                        m = (n - 5) // 2
                        vec.wait_ge(pe_done, C.at(f"{t}.xx{m}{c}", i))
                        if m < 3:
                            v(vec.tensor_tensor(NB[e][2 + (m + 1) % 2], bank(e, 0), NB[e][2 + m % 2], ALU.add),
                              f"{t}.xv{m + 1}{c}", i)
                        else:
                            v(vec.tensor_tensor(XTR[c], bank(e, 0), XTR[c], ALU.add), f"{t}.xf{c}", i)

            def chunk(i, tile, t, c, n):
                if n == 1:
                    vec.wait_ge(pe_done, C.at(f"{t}.u{c}", i))
                    v(vec.tensor_copy(US[:, :, :, :].rearrange("p h d f -> p (h d f)"), PS[:, 2, 0:256]),
                      f"{t}.us{c}", i)
                if n < 2:
                    return
                if c < NCH - 1:
                    vec.wait_ge(pe_done, C.at(f"{t}.sp{c}", i))
                    s3 = PS[:, 2, 256:384].rearrange("p (d f) -> p d f", d=2)
                    new = STR[(c + 1) % 2]
                    if c:
                        v(vec.tensor_tensor(new, STR[c % 2], s3, ALU.add), None, i)
                    for d in range(2):
                        ch = ORDER[d][c]
                        v(vec.tensor_scalar(new[:, d, :], new[:, d, :] if c else s3[:, d, :], PCT[:, d, ch:ch + 1],
                                            None, ALU.mult), f"{t}.st{c}" if d else None, i)
                vec.wait_ge(pe_done, C.at(f"{t}.yp{c}", i))
                for d in range(2):
                    ch = ORDER[d][c]
                    y, ps = YT[:, ch * P:(ch + 1) * P], PS[:, 0, d * P:(d + 1) * P]
                    label = f"{t}.y{c}" if d else None
                    if c % 2 == 0:
                        v(vec.tensor_copy(y, ps), label, i)
                    else:
                        v(vec.tensor_tensor(y, y, ps, ALU.add), label, i)

            def turn(i, tile, t, n):
                if n == 1:
                    vec.wait_ge(pe_done, C.at(f"{t}.bs", i))
                    v(vec.tensor_tensor(BV, RKV[:, 2, tile, :], PS[:, 1, :], ALU.mult), f"{t}.bv", i)

            def stage(i, tile, t, n):
                if n == 0:
                    nxt = tile if t.endswith("p") else tile + 1
                    v(vec.tensor_copy(PCN[:, 0:9], columns(B, 48, 72).rearrange("p (n c) -> p n c", c=8)[:, :, nxt]),
                      None, i)
                    v(vec.tensor_scalar(PCN[:, 9:10], PCN[:, 5:6], -1.0, 1.0, ALU.mult, ALU.add), None, i)
                    v(vec.tensor_scalar(KF, RKV[:, 1, nxt, :], PCN[:, 4:5], None, ALU.mult), f"{t}.kf", i)
                elif n in (2, 3):
                    d = n - 2
                    vec.wait_ge(act_done, C.at(f"{t}.s{d}", i))
                    for c in range(NCH):
                        cs = slice(c * P, (c + 1) * P)
                        v(vec.tensor_tensor_scan(ARS[:, d, 1, cs], const("ones"), SD[:, d, cs], 0.0, ALU.mult,
                                                 ALU.add), None, i)
                    if d == 0:
                        v(vec.tensor_tensor(ARS[:, 0, 0, :], ARS[:, 0, 1, :], SD[:, 0, :], ALU.subtract), None, i)
                    else:
                        c4 = lambda ap: ap.rearrange("p (c t) -> p c t", c=NCH)
                        v(vec.tensor_tensor(c4(ARS[:, 1, 0, :]),
                                            c4(ARS[:, 1, 1, :])[:, :, P - 1:P].broadcast_to([P, NCH, P]),
                                            c4(ARS[:, 1, 1, :]), ALU.subtract), None, i)
                        v(vec.tensor_tensor(ARS[:, 1, 1, :], ARS[:, 1, 0, :], SD[:, 1, :], ALU.add), f"{t}.sums", i)

            steps = {"I": invert, "C": chunk, "T": turn, "S": stage}

            def prime(i, nxt, t):
                vec.wait_ge(staged, C.at(f"{t}.staged", i))
                v(vec.tensor_copy(PCT[:, :, :], PCTS[:, :, :]), None, i)
                vec.tensor_tensor(KK, KK, KF, ALU.mult).then_inc(primed, C.mark(primed, f"{t}.kkn"))
                vec.wait_ge(primed, C.at(f"{t}.kkn", i))
                v(vec.tensor_scalar(SD[:, :, :], AD[:, :, :], PCN[:, 5:6], PCN[:, 9:10], ALU.mult, ALU.add), None, i)
                v(vec.tensor_tensor(AD[:, :, :], AD[:, :, :], both(KK), ALU.mult), None, i)
                v(vec.scalar_tensor_tensor(AD[:, :, :], AD[:, :, :], -1.0, PN[:, :, :], ALU.mult, ALU.mult), None, i)
                vec.tensor_tensor(AR[:, :, 1, :], ARS[:, :, 1, :], both(RKV[:, 0, nxt, :]), ALU.mult).then_inc(
                    primed, C.mark(primed, f"{t}.prod1"))
                v(vec.tensor_tensor(SD[:, :, :], SD[:, :, :], both(RKV[:, 1, nxt, :]), ALU.mult), None, i)
                v(vec.tensor_tensor(BS, SD[:, 0, :], SD[:, 1, :], ALU.add), None, i)
                vec.tensor_tensor(SD[:, :, :], SD[:, :, :], PN[:, :, :], ALU.mult).then_inc(
                    primed, C.mark(primed, f"{t}.prod"))
                v(vec.scalar_tensor_tensor(BS, BS, PCN[:, 6:7], RKV[:, 0, nxt, :], ALU.mult, ALU.mult), None, i)

            def trip(i, tile, t, staging):
                v(vec.tensor_copy(PC, PCN), None, i)
                play(steps, i, tile, t, staging)
                if staging:
                    prime(i, tile + 1, t)
                vec.wait_ge(act_done, C.at(f"{t}.ry", i))
                v(vec.tensor_tensor(YT, NB[0][2], PS[:, 6, :], ALU.mult), None, i)
                v(vec.tensor_scalar(YT, YT, PC[:, 7:8], PC[:, 8:9], ALU.mult, ALU.add), None, i)
                v(vec.tensor_tensor(YT, YT, BV, ALU.add), None, i)
                v(vec.tensor_tensor(RKV[:, 0, tile, :], YT, NB[0][3], ALU.mult), f"{t}.out", i)

            stage(None, 0, f"{t0}p", 0)
            stage(None, 0, f"{t0}p", 2)
            stage(None, 0, f"{t0}p", 3)
            prime(None, 0, f"{t0}p")
            with C.loop(vec, f"{t0}b", KD - 1) as i:
                trip(i, i, f"{t0}b", True)
            trip(None, KD - 1, f"{t0}z", False)
            proj_vec(f"mo{l}", l, 1, lo)
            leave((vec_done,), f"mix{l}")

        MIX = {}
        MIX[2] = {'sp': attn_sp, 'pe': attn_pe, 'act': attn_act, 'vec': attn_vec, 'pool': attn_pool}
        MIX[1] = {'sp': ssd_sp, 'pe': ssd_pe, 'act': ssd_act, 'vec': ssd_vec, 'pool': ssd_pool}
        MIX[0] = MIX[3] = {'sp': rwkv_sp, 'pe': rwkv_pe, 'act': rwkv_act, 'vec': rwkv_vec, 'pool': rwkv_pool}
        MIX = {n: m for n, m in MIX.items() if n in only}


        block = ctx.enter_context(nc.Block())
        kinds = ["rwkv", "ssd", "attn", "rwkv"]

        def los(l):
            return SEG if l == DEPTH - 1 else 0

        def before(l):
            return "ada" if l == list(layers)[0] else f"ffn{l - 1}"

        @block.sync
        def _(sp):
            start_sp()
            ada_sp()
            for l in layers:
                if mixers and l in MIX:
                    MIX[l]["sp"](l)
                ffn_sp(l)
            end_sp()

        @block.gpsimd
        def _(pool):
            for l in layers:
                if mixers and l in MIX and "pool" in MIX[l]:
                    MIX[l]["pool"](l)
                ffn_pool(l, f"mix{l}" if mixers and l in MIX else before(l))

        @block.tensor
        def _(pe):
            start_pe()
            ada_pe()
            for l in layers:
                if mixers and l in MIX:
                    norm_pe(f"n1{l}", before(l), 0)
                    MIX[l]["pe"](l, los(l))
                norm_pe(f"n2{l}", f"mix{l}" if mixers and l in MIX else before(l), los(l))
                ffn_pe(l, los(l))
            norm_pe("nf", f"ffn{list(layers)[-1]}", SEG)
            end_pe("nf")

        @block.scalar
        def _(act):
            start_act()
            for l in layers:
                if mixers and l in MIX:
                    norm_act(f"n1{l}", before(l), 0, 2 * l, mod_shift(l, 0))
                    MIX[l]["act"](l, los(l))
                norm_act(f"n2{l}", f"mix{l}" if mixers and l in MIX else before(l), los(l), 2 * l + 1, mod_shift(l, 1))
                ffn_act(l, los(l))
            norm_act("nf", f"ffn{list(layers)[-1]}", SEG, 2 * DEPTH, lambda k, n: MS[:, 2 * DEPTH, k, 0:1])
            end_act("nf")

        @block.vector
        def _(vec):
            start_vec()
            ada_vec()
            for l in layers:
                if mixers and l in MIX:
                    norm_vec(f"n1{l}", before(l), 0, 2 * l, mod_shift(l, 0))
                    MIX[l]["vec"](l, los(l))
                norm_vec(f"n2{l}", f"mix{l}" if mixers and l in MIX else before(l), los(l), 2 * l + 1, mod_shift(l, 1))
                ffn_vec(l, los(l))
            norm_vec("nf", f"ffn{list(layers)[-1]}", SEG, 2 * DEPTH, lambda k, n: MS[:, 2 * DEPTH, k, 0:1])
    return C


_INS = ['x', 'c', 'ctx', 'c_ctx', 'ada_w', 'ada_b', 'norm1_g', 'norm2_g', 'ffn_w_in', 'ffn_conv', 'ffn_w_out',
        'final_g', 'rw_mu', 'rw_wr', 'rw_wk', 'rw_wv', 'rw_wo', 'rw_w0', 'rw_w1', 'rw_w2', 'rw_a0', 'rw_a1', 'rw_a2',
        'rw_g1', 'rw_g2', 'rw_kk', 'rw_ka', 'rw_rk', 'rw_ln_g', 'rw_ln_b', 'ssd_w_in', 'ssd_conv_w', 'ssd_conv_b',
        'ssd_dt_bias', 'ssd_a_log', 'ssd_d', 'ssd_norm_g', 'ssd_w_out', 'at_w_qkv', 'at_w_o', 'at_sink']


def shape_constants():
    import numpy as np
    f = np.float32
    r, c = np.arange(P)[:, None], np.arange(P)[None, :]
    same = lambda n: (r // n == c // n).astype(f)
    level = lambda n: ((r // (2 * n) == c // (2 * n)) & (r // n != c // n)).astype(f)
    m = {"ident": np.eye(P, dtype=f), "mean": np.full((P, P), 1.0 / D, f), "blk": same(64),
         "cent": np.eye(P, dtype=f) - same(64) / 64, "blkmean": same(64) / 64, "ones": np.ones((P, P), f),
         "mean256": np.full((P, P), 1.0 / 256, f),
         "mask8": same(8), "lev8": level(8), "lev16": level(16), "lev32": level(32), "lev64": level(64),
         "gs0": (r < c).astype(f), "gi0": (r <= c).astype(f), "gs1": (r > c).astype(f), "gi1": (r >= c).astype(f),
         "gt0": (r > c) * same(8), "gt1": (r < c) * same(8)}
    consts = np.concatenate([m[n] for n in CONST], 1)

    inv = (f(10000.0) ** (-np.arange(0, 32, 2, dtype=f) / f(32))).astype(f)
    tok = np.arange(SEQ)
    p = np.arange(P)
    pos = np.where((p % 64)[:, None] < 32, (tok // 64)[None, :], (tok % 64)[None, :]).astype(f)
    ang = (pos * inv[p % 16][:, None]).astype(f)
    cos, sin = np.cos(ang).astype(f), np.sin(ang).astype(f)
    rot = np.zeros((P, P), f)
    for q in range(P):
        if q % 32 < 16:
            rot[q + 16, q] = -1.0
        else:
            rot[q - 16, q] = 1.0
    dup = [np.zeros((P, P), f) for _ in range(2)]
    for h in range(2):
        for q in range(P):
            dup[h][64 * h + q % 64, q] = 1.0
    am = []
    for b in range(2):
        q = b * P + np.arange(P)[:, None]
        k = np.arange(SEQ)[None, :]
        am.append(np.where(np.abs(q - k) <= 128, f(0), f(NEG)))
    attn = np.concatenate([cos, sin, rot, dup[0], dup[1], rot @ dup[0], rot @ dup[1], am[0], am[1]], 1).astype(f)
    return consts, attn, dup, rot


def kernel(**inputs):
    import numpy as _np
    import concourse.bacc as _bacc
    from concourse import mybir as _mybir
    from concourse.bass_utils import run_bass_kernel_spmd as _run

    consts, attn, _, _ = shape_constants()
    extra = {"consts": consts, "attn_consts": attn}

    def build(draft):
        nc = _bacc.Bacc("TRN2", target_bir_lowering=False, num_devices=1)
        arrays, args = {}, {}
        for name in _INS + list(extra):
            arr = _np.ascontiguousarray(extra[name] if name in extra else inputs[name])
            arrays[f"in_{name}_dram"] = arr
            args[name] = nc.dram_tensor(f"in_{name}_dram", arr.shape, _mybir.dt.from_np(arr.dtype),
                                        kind="ExternalInput").ap()
        out = nc.dram_tensor("out_0_dram", (1, SEQ, D), F32, kind="ExternalOutput").ap()
        scratch = nc.dram_tensor("scratch_dram", (64, T), F32, kind="Internal").ap()
        counts = program(nc, args, out, draft, scratch, **OPTIONS)
        return nc, arrays, counts

    _, _, draft = build(None)
    nc, arrays, _ = build(draft)
    r = _run(nc, [arrays], core_ids=[0])
    return r.results[0]["out_0_dram"]


OPTIONS = {}
```
